# Optimizing a Trainium2 kernel written in Bass

```python
import jax, jax.numpy as jnp
from jax import lax
import numpy as np

D_MODEL = 1024
BATCH = 1
SEQ = 256
DEPTH = 2

GRID_W = 64
N_HEADS = 8
KV_HEADS = 2
HEAD_DIM = 64
Q_PER_KV = N_HEADS // KV_HEADS
AXIS_DIM = HEAD_DIM // 2
ROPE_THETA = 10000.0
Q_BLOCK = 128
Q_DIM = N_HEADS * HEAD_DIM
KV_DIM = KV_HEADS * HEAD_DIM
CONV_CH = D_MODEL // 2
CONV_WIDTH = 31
IN_PROJ_DIM = Q_DIM + 2 * KV_DIM + 2 * CONV_CH
MIX_DIM = Q_DIM + CONV_CH
POOL_WINDOWS = (2, 4, 8, 16)
POOL_GROUPS = len(POOL_WINDOWS)
POOL_GC = D_MODEL // POOL_GROUPS
FFN_DIM = 2816
N_EXPERTS = 8
TOP_K = 2
EXPERT_DIM = 3584
PLE_DIM = 256
EPS = 1e-6

kernel_name = "hybrid_attn_conv_pool_moe_encoder"

def rms_norm(x, g):
    xf = x.astype(jnp.float32)
    y = xf * lax.rsqrt(jnp.mean(xf * xf, axis=-1, keepdims=True) + EPS)
    return (y * g.astype(jnp.float32)).astype(x.dtype)

def layer_norm(x, g, b):
    xf = x.astype(jnp.float32)
    mu = jnp.mean(xf, axis=-1, keepdims=True)
    var = jnp.mean(jnp.square(xf - mu), axis=-1, keepdims=True)
    y = (xf - mu) * lax.rsqrt(var + EPS)
    return (y * g.astype(jnp.float32) + b.astype(jnp.float32)).astype(x.dtype)

def axial_rope_tables(seq):
    rows = seq // GRID_W
    r = jnp.broadcast_to(jnp.arange(rows, dtype=jnp.float32)[:, None], (rows, GRID_W)).reshape(seq)
    c = jnp.broadcast_to(jnp.arange(GRID_W, dtype=jnp.float32)[None, :], (rows, GRID_W)).reshape(seq)
    inv = ROPE_THETA ** (-jnp.arange(0, AXIS_DIM, 2, dtype=jnp.float32) / AXIS_DIM)
    ang = jnp.concatenate([r[:, None] * inv, c[:, None] * inv], axis=-1)
    return jnp.cos(ang)[None, :, None, :], jnp.sin(ang)[None, :, None, :]

def apply_rope(x, cos, sin):
    xf = x.astype(jnp.float32)
    half = HEAD_DIM // 2
    x1, x2 = xf[..., :half], xf[..., half:]
    return jnp.concatenate([x1 * cos - x2 * sin, x2 * cos + x1 * sin], axis=-1).astype(x.dtype)

def block_attention(q, k, v):
    b, s = q.shape[0], q.shape[1]
    nb = s // Q_BLOCK
    qb = q.reshape(b, nb, Q_BLOCK, KV_HEADS, Q_PER_KV, HEAD_DIM).transpose(1, 0, 2, 3, 4, 5)
    scale = HEAD_DIM ** -0.5

    def one_block(q_blk):
        sc = jnp.einsum('bqhgd,bkhd->bhgqk', q_blk, k).astype(jnp.float32) * scale
        pr = jax.nn.softmax(sc, axis=-1).astype(v.dtype)
        return jnp.einsum('bhgqk,bkhd->bqhgd', pr, v)

    out = lax.map(one_block, qb)
    return out.transpose(1, 0, 2, 3, 4, 5).reshape(b, s, Q_DIM)

def attn_conv_mixer(hn, w_in, q_g, k_g, conv_w, conv_b, cln_g, cln_b, w_out, cos, sin):
    b, s, _ = hn.shape
    proj = jnp.einsum('bsd,de->bse', hn, w_in)
    q = proj[..., :Q_DIM].reshape(b, s, N_HEADS, HEAD_DIM)
    k = proj[..., Q_DIM:Q_DIM + KV_DIM].reshape(b, s, KV_HEADS, HEAD_DIM)
    v = proj[..., Q_DIM + KV_DIM:Q_DIM + 2 * KV_DIM].reshape(b, s, KV_HEADS, HEAD_DIM)
    u = proj[..., Q_DIM + 2 * KV_DIM:]
    q = apply_rope(rms_norm(q, q_g), cos, sin)
    k = apply_rope(rms_norm(k, k_g), cos, sin)
    a_out = block_attention(q, k, v)
    u = u[..., :CONV_CH] * jax.nn.sigmoid(u[..., CONV_CH:])
    u = lax.conv_general_dilated(
        u, conv_w[:, None, :], window_strides=(1,),
        padding=[(CONV_WIDTH // 2, CONV_WIDTH // 2)],
        dimension_numbers=('NWC', 'WIO', 'NWC'),
        feature_group_count=CONV_CH) + conv_b
    c_out = jax.nn.silu(layer_norm(u, cln_g, cln_b))
    mix = jnp.concatenate([a_out, c_out], axis=-1)
    return jnp.einsum('bse,ed->bsd', mix, w_out)

def multiscale_pool_mixer(hn, pool_w, pool_scale):
    b, s, d = hn.shape
    hf = hn.astype(jnp.float32)
    cs = jnp.concatenate([jnp.zeros((b, 1, d), jnp.float32), jnp.cumsum(hf, axis=1)], axis=1)
    t = jnp.arange(s)
    outs = []
    for g, w in enumerate(POOL_WINDOWS):
        left = w // 2
        right = w - 1 - left
        lo = jnp.clip(t - left, 0, s - 1)
        hi = jnp.clip(t + right, 0, s - 1)
        seg = cs[..., g * POOL_GC:(g + 1) * POOL_GC]
        win_sum = seg[:, hi + 1] - seg[:, lo]
        cnt = (hi - lo + 1).astype(jnp.float32)[None, :, None]
        outs.append(win_sum / cnt - hf[..., g * POOL_GC:(g + 1) * POOL_GC])
    y = jnp.stack(outs, axis=2).astype(hn.dtype)
    y = jnp.einsum('bsgc,gcd->bsgd', y, pool_w).reshape(b, s, d)
    return y * pool_scale

def swiglu(h, wg, wu, wd):
    return jnp.einsum('bsf,fd->bsd', jax.nn.silu(jnp.einsum('bsd,df->bsf', h, wg)) * jnp.einsum('bsd,df->bsf', h, wu), wd)

def moe_swiglu(h, router_w, wg, wu, wd):
    logits = jnp.einsum('bsd,de->bse', h, router_w).astype(jnp.float32)
    top_v, top_i = lax.top_k(logits, TOP_K)
    top_p = jax.nn.softmax(top_v, axis=-1)
    gates = jnp.einsum('bske,bsk->bse', jax.nn.one_hot(top_i, N_EXPERTS, dtype=jnp.float32), top_p).astype(h.dtype)
    out = jnp.zeros_like(h)
    for e in range(N_EXPERTS):
        out = out + gates[..., e:e + 1] * swiglu(h, wg[e], wu[e], wd[e])
    return out

def setup_inputs(seed: int = 0) -> dict:
    key = jax.random.key(seed)
    ks = iter(jax.random.split(key, 40))
    n_even = (DEPTH + 1) // 2
    n_odd = DEPTH // 2
    f32 = jnp.float32

    def nrm(shape, scale):
        return jax.random.normal(next(ks), shape, f32) * scale

    def gain(shape):
        return 1.0 + 0.05 * jax.random.normal(next(ks), shape, f32)

    return {
        "x": nrm((BATCH, SEQ, D_MODEL), 1.0),
        "p": nrm((DEPTH, BATCH, SEQ, PLE_DIM), 1.0),
        "norm_mix": gain((DEPTH, D_MODEL)),
        "norm_ffn": gain((DEPTH, D_MODEL)),
        "w_in": nrm((n_even, D_MODEL, IN_PROJ_DIM), D_MODEL ** -0.5),
        "q_norm": gain((n_even, HEAD_DIM)),
        "k_norm": gain((n_even, HEAD_DIM)),
        "conv_w": nrm((n_even, CONV_WIDTH, CONV_CH), CONV_WIDTH ** -0.5),
        "conv_b": nrm((n_even, CONV_CH), 0.02),
        "conv_ln_g": gain((n_even, CONV_CH)),
        "conv_ln_b": nrm((n_even, CONV_CH), 0.02),
        "w_out": nrm((n_even, MIX_DIM, D_MODEL), MIX_DIM ** -0.5),
        "ffn_wg": nrm((n_even, D_MODEL, FFN_DIM), D_MODEL ** -0.5),
        "ffn_wu": nrm((n_even, D_MODEL, FFN_DIM), D_MODEL ** -0.5),
        "ffn_wd": nrm((n_even, FFN_DIM, D_MODEL), FFN_DIM ** -0.5),
        "pool_w": nrm((n_odd, POOL_GROUPS, POOL_GC, POOL_GC), POOL_GC ** -0.5),
        "pool_scale": gain((n_odd, D_MODEL)),
        "router_w": nrm((n_odd, D_MODEL, N_EXPERTS), D_MODEL ** -0.5),
        "moe_wg": nrm((n_odd, N_EXPERTS, D_MODEL, EXPERT_DIM), D_MODEL ** -0.5),
        "moe_wu": nrm((n_odd, N_EXPERTS, D_MODEL, EXPERT_DIM), D_MODEL ** -0.5),
        "moe_wd": nrm((n_odd, N_EXPERTS, EXPERT_DIM, D_MODEL), EXPERT_DIM ** -0.5),
        "ple_norm": gain((DEPTH, D_MODEL)),
        "ple_gate_w": nrm((DEPTH, D_MODEL, D_MODEL), D_MODEL ** -0.5),
        "ple_proj": nrm((DEPTH, PLE_DIM, D_MODEL), PLE_DIM ** -0.5),
    }

def reference(x, p, norm_mix, norm_ffn, w_in, q_norm, k_norm, conv_w, conv_b,
              conv_ln_g, conv_ln_b, w_out, ffn_wg, ffn_wu, ffn_wd, pool_w,
              pool_scale, router_w, moe_wg, moe_wu, moe_wd, ple_norm,
              ple_gate_w, ple_proj):
    cos, sin = axial_rope_tables(x.shape[1])
    h = x
    for i in range(DEPTH):
        j = i // 2
        hn = rms_norm(h, norm_mix[i])
        if i % 2 == 0:
            h = h + attn_conv_mixer(hn, w_in[j], q_norm[j], k_norm[j], conv_w[j], conv_b[j],
                                    conv_ln_g[j], conv_ln_b[j], w_out[j], cos, sin)
            h = h + swiglu(rms_norm(h, norm_ffn[i]), ffn_wg[j], ffn_wu[j], ffn_wd[j])
        else:
            h = h + multiscale_pool_mixer(hn, pool_w[j], pool_scale[j])
            h = h + moe_swiglu(rms_norm(h, norm_ffn[i]), router_w[j], moe_wg[j], moe_wu[j], moe_wd[j])
        gate = jax.nn.sigmoid(jnp.einsum('bsd,de->bse', rms_norm(h, ple_norm[i]), ple_gate_w[i]))
        h = h + gate * jnp.einsum('bsk,kd->bsd', p[i], ple_proj[i])
    return h


_drawn_inputs = setup_inputs


def setup_inputs(seed=0):
    import zlib

    import numpy as np

    out = dict(_drawn_inputs(seed))
    spreads = {}
    factors = {'q_norm': 5.538, 'k_norm': 8.0, 'conv_b': 2.82, 'conv_ln_b': 3.522, 'ple_norm': 2.721}
    for name, (base, spread) in spreads.items():
        noise = np.random.default_rng([zlib.crc32(name.encode()), seed]).standard_normal(out[name].shape)
        drawn = base * np.exp(spread * noise) if base else spread * noise
        out[name] = __import__('jax').numpy.asarray(drawn.astype(out[name].dtype))
    for name, factor in factors.items():
        out[name] = (out[name] * factor).astype(out[name].dtype)
    return out
```

```python
import concourse.bass as bass
import numpy as np
from concourse import mybir

F32 = mybir.dt.float32
F32R = mybir.dt.float32r
I32 = mybir.dt.int32
U32 = mybir.dt.uint32
ALU = mybir.AluOpType
ACT = mybir.ActivationFunctionType
AX = mybir.AxisListType

P = 128
D = 1024
SEQ = 256
T = SEQ // P
KT = D // P
GRID_W = 64
HEADS, KV_HEADS, HEAD_DIM = 8, 2, 64
HALF = HEAD_DIM // 2
QK = (HEADS + KV_HEADS) * HEAD_DIM
CONV_CH, CONV_W = 512, 31
CT = CONV_CH // P
PAD = CONV_W // 2
POOL_WINDOWS = (2, 4, 8, 16)
FFN = 2816
NE, EF = 8, 3584
PLE = 256
EPS = 1e-6

COLS = 512
ROWS = 4
PIECE = 1024
CHUNK = 4 * PIECE
RING = 7
AHEAD = 4
FREE_AFTER = 4
NOWHERE = -1000.0

C_IDENT, C_IOTA, C_MEAN, C_ONES, C_BEFORE, C_COS, C_SIN, C_END = 0, 128, 256, 384, 512, 640, 704, 768

V_GAINS, V_CONV_W = 0, 6 * KT
V_CONV_B = V_CONV_W + CT * CONV_W
V_LN_G, V_LN_B, V_ROUTER = V_CONV_B + CT, V_CONV_B + 2 * CT, V_CONV_B + 3 * CT
V_END = V_ROUTER + KT * NE


def dense_chunks():
    out = [("w_in", "col", 0, 4), ("w_in", "kv", 0, 2), ("w_in", "a", 0, 4), ("w_in", "b", 0, 4),
           ("w_out", "row", 0, 4), ("w_out", "row", 1, 4)]
    groups = -(-FFN // COLS)
    for j in range(groups + 1):
        n = 4 if (j + 1) * COLS <= FFN else 2
        if j < groups:
            out += [("ffn_wg", "col", j, n), ("ffn_wu", "col", j, n)]
        if j >= 1:
            n = 4 if j * COLS <= FFN else 2
            out.append(("ffn_wd", "row", j - 1, n))
    out += [("gate0", "row", 0, 4), ("gate0", "row", 1, 4), ("proj0", "row", 0, 2), ("pool_w", "pool", 0, 2)]
    return out


def expert_chunks():
    groups = EF // COLS
    out = []
    for j in range(groups + 1):
        if j < groups:
            out += [("moe_wg", j), ("moe_wu", j)]
        if j >= 1:
            out.append(("moe_wd", j - 1))
    return out


DENSE = dense_chunks()
EXPERT = expert_chunks()
TAIL = [("gate1", "row", 0, 4), ("gate1", "row", 1, 4), ("proj1", "row", 0, 2)]
ND, NX = len(DENSE), len(EXPERT)
GROUPS = EF // COLS
XP = 4 * NX
ITERS = 2 * NE
FIRST = [sum(c[3] for c in DENSE[:n]) for n in range(ND + 1)]
PB = FIRST[ND]
PT = PB + ITERS * XP
assert NX % RING == 0 and XP % AHEAD == 0


def slot_of(n):
    return n if n < FREE_AFTER else n - FREE_AFTER if n < 2 * FREE_AFTER else (n - FREE_AFTER) % RING


def fills_of(n):
    return sum(slot_of(m) == slot_of(n) for m in range(n + 1))


def last_piece_before(n):
    before = [m for m in range(n) if slot_of(m) == slot_of(n)]
    return FIRST[before[-1] + 1] if before else None


XSLOT = [slot_of(ND + i) for i in range(NX)]
XFILL = [sum(slot_of(m) == XSLOT[i] for m in range(ND)) + 1 + sum(XSLOT[q] == XSLOT[i] for q in range(i))
         for i in range(NX)]
PER = NX // RING


def kernel_program(nc, a, out):
    def sb(name, shape, dt=F32):
        return nc.alloc_sbuf_tensor(name, shape, dt)

    def sem(name):
        return nc.alloc_semaphore(name)

    ring = sb("ring", [P, RING, CHUNK])
    hi_ring = sb("hi_ring", [P, AHEAD, PIECE], F32R)
    lo_ring = sb("lo_ring", [P, AHEAD, PIECE], F32R)
    xT_hi = sb("xT_hi", [P, KT, SEQ], F32R)
    xT_lo = sb("xT_lo", [P, KT, SEQ], F32R)
    mT_hi = sb("mT_hi", [P, KT, SEQ], F32R)
    mT_lo = sb("mT_lo", [P, KT, SEQ], F32R)
    h = sb("h", [P, T, D])
    tok = sb("tok", [P, T, D])
    misc = sb("misc", [P, 2304])
    cst = sb("cst", [P, C_END])
    vec = sb("vec", [P, V_END])
    gains = vec[:, V_GAINS:V_CONV_W].rearrange("p (i k) -> p i k", k=KT)
    conv_w = vec[:, V_CONV_W:V_CONV_B].rearrange("p (c w) -> p c w", c=CT)
    conv_b, ln_g, ln_b = vec[:, V_CONV_B:V_LN_G], vec[:, V_LN_G:V_LN_B], vec[:, V_LN_B:V_ROUTER]
    rw = vec[:, V_ROUTER:V_END].rearrange("p (k e) -> p k e", k=KT)
    ss = sb("ss", [P, 6, T])
    std = sb("std", [P, 6, T])
    rstd = sb("rstd", [P, 6, T])
    eps = sb("eps", [P, 1])
    s_small = sb("s_small", [P, 64])
    rw_hi = sb("rw_hi", [P, KT, NE], F32R)
    rw_lo = sb("rw_lo", [P, KT, NE], F32R)
    rt = sb("rt", [P, 160])
    idx8 = sb("idx8", [P, T, 8], U32)
    slot_tab = sb("slot_tab", [P, T, ITERS + 1])
    gate_tab = sb("gate_tab", [P, T, ITERS + 1])
    most = sb("most", [P, 1], I32)

    ident = cst[:, C_IDENT:C_IOTA]
    iota = cst[:, C_IOTA:C_MEAN]
    mean_mat = cst[:, C_MEAN:C_ONES]
    ones_mat = cst[:, C_ONES:C_BEFORE]
    before_mat = cst[:, C_BEFORE:C_COS]
    cos = cst[:, C_COS:C_SIN].rearrange("p (t f) -> p t f", t=T)
    sin = cst[:, C_SIN:C_END].rearrange("p (t f) -> p t f", t=T)

    scratch = ring[:, FREE_AFTER:RING, :].rearrange("p s n -> p (s n)")
    taken = [0]

    def carve(n):
        taken[0] += n
        assert taken[0] <= (RING - FREE_AFTER) * CHUNK
        return scratch[:, taken[0] - n:taken[0]]

    qk = carve(T * QK).rearrange("p (t n) -> p t n", t=T)
    qk_gain = carve(QK)
    rope4 = carve(T * 4 * QK // 2)
    rot = carve(T * 768).rearrange("p (t n) -> p t n", t=T)
    v_sb = carve(T * P).rearrange("p (t n) -> p t n", t=T)
    qT = carve(4 * SEQ).rearrange("p (c n) -> p c n", c=4)
    kT = carve(2 * SEQ).rearrange("p (c n) -> p c n", c=2)
    prob = carve(2 * 512).rearrange("p (b t n) -> p b t n", b=2, t=T)
    probT = carve(2 * 512).rearrange("p (b k n) -> p b k n", b=2, k=T)
    upad = carve(CT * (SEQ + 2 * PAD)).rearrange("p (c n) -> p c n", c=CT)
    conv = carve(CT * SEQ).rearrange("p (c n) -> p c n", c=CT)
    sq = rope4[:, 0:T * QK].rearrange("p (t n) -> p t n", t=T)
    rope = rope4.rearrange("p (t q n f) -> p t q n f", t=T, q=4, f=HALF)
    sig_b = probT_all = None
    sig_b = scratch[:, taken[0] - CT * SEQ - CT * (SEQ + 2 * PAD) - 1024:
                    taken[0] - CT * SEQ - CT * (SEQ + 2 * PAD)].rearrange("p (c n) -> p c n", c=CT)
    ln_sq = rope4[:, 0:CT * SEQ].rearrange("p (c n) -> p c n", c=CT)
    ln_out = rope4[:, CT * SEQ:2 * CT * SEQ].rearrange("p (c n) -> p c n", c=CT)
    ln_std = prob[:, 0, 0, :]
    ln_rstd = prob[:, 0, 1, :]

    ffn_act = misc[:, 0:1024].rearrange("p (f n) -> p f n", f=4)
    p_tok = misc[:, 1024:1536].rearrange("p (t n) -> p t n", t=T)
    bands = misc[:, 0:2048].rearrange("p (t g n) -> p t g n", t=T, g=4)
    scale_row = misc[:, 0:D]
    x_act = misc[:, 0:512]
    y_sb = misc[:, 512:1536]
    pick = misc[:, 1536:1792].rearrange("p (t n) -> p t n", t=T)
    pick_gated = misc[:, 1792:2048].rearrange("p (t n) -> p t n", t=T)
    spread = misc[:, 2048:2304]

    Y = nc.alloc_psum_tensor("Y", [P, 4, 512], F32)
    G = nc.alloc_psum_tensor("G", [P, 4, 512], F32)
    G8 = G[:, :, :].rearrange("p b (k n) -> p (b k) n", k=2)

    xg_hi, xg_lo = xT_hi[:, :, 0:P], xT_lo[:, :, 0:P]
    aT_hi = mT_hi[:, :, 0:P].rearrange("p (b f) n -> p b f n", b=2)
    aT_lo = mT_lo[:, :, 0:P].rearrange("p (b f) n -> p b f n", b=2)

    slot_in = [sem(f"slot_in{i}") for i in range(RING)]
    hi_done, lo_done, pe_piece = sem("hi_done"), sem("lo_done"), sem("pe_piece")
    x_in, small_in, p_in, band_in, scale_in = sem("x_in"), sem("small_in"), sem("p_in"), sem("band_in"), sem("scale_in")
    eps_set = sem("eps_set")
    h_ready = sem("h_ready")
    ss_done, std_done, rstd_done, tok_done = sem("ss_done"), sem("std_done"), sem("rstd_done"), sem("tok_done")
    tr_done, nhi_done, nlo_done = sem("tr_done"), sem("nhi_done"), sem("nlo_done")
    qkv_copied, qk_ss, qk_std, qk_rot = sem("qkv_copied"), sem("qk_ss"), sem("qk_std"), sem("qk_rot")
    qk_tr, qk_tr_copied = sem("qk_tr"), sem("qk_tr_copied")
    sig_done, glu_done, pads_set = sem("sig_done"), sem("glu_done"), sem("pads_set")
    conv_v, conv_p = sem("conv_v"), sem("conv_p")
    sc_done, neg_done, exp_done, nrm_done = sem("sc_done"), sem("neg_done"), sem("exp_done"), sem("nrm_done")
    pt_done, pt_copied, o_done, o_hi, o_lo = sem("pt_done"), sem("pt_copied"), sem("o_done"), sem("o_hi"), sem("o_lo")
    mean_mm, cent_done, sq_done, var_mm = sem("mean_mm"), sem("cent_done"), sem("sq_done"), sem("var_mm")
    lnstd_done, lnn_done, silu_c, c_hi, c_lo = sem("lnstd_done"), sem("lnn_done"), sem("silu_c"), sem("c_hi"), sem("c_lo")
    fsilu, fmul, fhi, flo = sem("fsilu"), sem("fmul"), sem("fhi"), sem("flo")
    ptok_tr, p_hi, p_lo, sig_gate, gated = sem("ptok_tr"), sem("p_hi"), sem("p_lo"), sem("sig_gate"), sem("gated")
    scaled = sem("scaled")
    rw_hi_done, rw_lo_done, logit_mm, route_v, gap_exp = sem("rw_hi_done"), sem("rw_lo_done"), sem("logit_mm"), sem("route_v"), sem("gap_exp")
    mask_done, rank_mm, tabs_done = sem("mask_done"), sem("rank_mm"), sem("tabs_done")
    pick_done = sem("pick_done")
    gath_mm, xhi_done, xlo_done = sem("gath_mm"), sem("xhi_done"), sem("xlo_done")
    xsilu, xmul = sem("xsilu"), sem("xmul")
    at_mm, at_hi, at_lo = sem("at_mm"), sem("at_hi"), sem("at_lo")
    y_out, sp_mm, sp_out, scat_mm, scat_add = sem("y_out"), sem("sp_mm"), sem("sp_out"), sem("scat_mm"), sem("scat_add")
    last_mm = sem("last_mm")
    chain_v, chain_a, chain_p = sem("chain_v"), sem("chain_a"), sem("chain_p")
    stored = sem("stored")

    w_in = a["w_in"][0].rearrange("(k p) n -> p k n", p=P)

    def dense_source(name, kind, j, pieces):
        if name == "w_in":
            c0, n = {"col": (0, 512), "kv": (512, 256), "a": (768, 512), "b": (1280, 512)}[kind]
            return w_in[:, :, c0:c0 + n], KT, n
        if kind == "col":
            n = COLS * pieces // 4
            return a[name][0].rearrange("(k p) n -> p k n", p=P)[:, :, j * COLS:j * COLS + n], KT, n
        if kind == "pool":
            return a["pool_w"][0].rearrange("g (k p) n -> p (g k) n", p=P), 8, 256
        m = {"w_out": lambda: a["w_out"][0], "ffn_wd": lambda: a["ffn_wd"][0],
             "gate0": lambda: a["ple_gate_w"][0], "proj0": lambda: a["ple_proj"][0],
             "gate1": lambda: a["ple_gate_w"][1], "proj1": lambda: a["ple_proj"][1]}[name]()
        rows = m[j * ROWS * P:(j * ROWS + pieces) * P, :]
        return rows.rearrange("(r p) n -> p r n", p=P), pieces, D

    def moe_source(name, j, e):
        w = a[name][0]
        if name == "moe_wd":
            return w[bass.ds(e, 1), j * COLS:(j + 1) * COLS, :].rearrange("o (r p) n -> p (o r) n", p=P), ROWS, D
        return w[bass.ds(e, 1), :, j * COLS:(j + 1) * COLS].rearrange("o (k p) n -> p (o k) n", p=P), KT, COLS

    def piece_at(buf, n, width):
        return buf[:, n % AHEAD, :].rearrange("p (r n) -> p r n", n=width)

    block = nc.Block()
    block.__enter__()

    @block.sync
    def _(sp):
        def load(n_slot, src, rows, width):
            dst = ring[:, n_slot, 0:rows * width].rearrange("p (r n) -> p r n", r=rows)
            sp.dma_start(dst, src).then_inc(slot_in[n_slot], 16)

        sp.dma_start(h[:, :, :], a["x"][0].rearrange("(t p) d -> p t d", p=P)).then_inc(x_in, 16)
        for n, chunk in enumerate(DENSE):
            if last_piece_before(n) is not None:
                sp.wait_ge(lo_done, last_piece_before(n))
            if n == 2 * FREE_AFTER:
                sp.wait_ge(c_lo, 1)
                sp.wait_ge(o_lo, 4)
            load(slot_of(n), *dense_source(*chunk))

        def expert_loads(first, last, base):
            with sp.Fori(first, last) as it:
                for i, (name, j) in enumerate(EXPERT):
                    before = PB + 4 * (i - RING + 1) if i >= RING else FIRST[ND - RING + i + 1]
                    sp.wait_ge(lo_done, it * XP + before)
                    load(XSLOT[i], *moe_source(name, j, it - base))

        def tail_load(m):
            sp.wait_ge(lo_done, PT + 4 * (m - RING + 1))
            load(XSLOT[m], *dense_source(*TAIL[m]))

        expert_loads(0, NE, 0)
        sp.wait_ge(tabs_done, 1)
        n_most = sp.value_load(most[0:1, 0:1])
        with sp.If(n_most > P):
            expert_loads(NE, ITERS, NE)
            tail_load(0)
        with sp.Else():
            sp.wait_ge(lo_done, PB + NE * XP + 4 * (1 - RING))
            load(XSLOT[0], *dense_source(*TAIL[0]))
            for s in range(RING):
                i0 = XSLOT.index(s)
                sp.wait_ge(slot_in[s], 16 * (XFILL[i0] - 1 + PER * NE + (s == XSLOT[0])))
                sp.sem_inc(slot_in[s], 16 * PER * NE)
            sp.nop()
        tail_load(1)
        tail_load(2)
        for t in range(T):
            sp.wait_ge(gated, 3 + t)
            sp.dma_start(out[0].rearrange("(t p) d -> p t d", p=P)[:, t, :], h[:, t, :]).then_inc(stored, 16)
        sp.wait_ge(stored, 16 * T)

    @block.scalar
    def _(act):
        small = [(cst[:, :], a["consts"]), (vec[:, :], a["vectors"]),
                 (qk_gain, a["qk_gain"].broadcast_to([P, QK]))]
        for dst, src in small:
            act.dma_start(dst, src).then_inc(small_in, 16)
        n_small = 16 * 3

        def hi(n, chunk_sem=None, value=None, where=None):
            if chunk_sem is not None:
                act.wait_ge(chunk_sem, value)
            act.activation(hi_ring[:, n % AHEAD, :], where, ACT.Copy).then_inc(hi_done, 1)

        did = [0]

        def hi_upto(last):
            while did[0] <= min(last, PB - 1):
                n = did[0]
                c = max(m for m in range(ND) if FIRST[m] <= n)
                s = slot_of(c)
                if n >= AHEAD:
                    act.wait_ge(pe_piece, n - AHEAD + 1)
                off = (n - FIRST[c]) * PIECE
                hi(n, slot_in[s], 16 * fills_of(c), ring[:, s, off:off + PIECE])
                did[0] += 1
            for q in range(max(did[0] - PB, 0), last - PB + 1):
                act.wait_ge(pe_piece, PB + q - AHEAD + 1)
                hi(PB + q, slot_in[XSLOT[0]], 16 * XFILL[0], ring[:, XSLOT[0], q * PIECE:(q + 1) * PIECE])
                did[0] += 1

        def norm(i):
            act.wait_ge(h_ready, i + 1) if i else act.wait_ge(x_in, 16)
            for t in range(T):
                act.activation(tok[:, t, :], h[:, t, :], ACT.Square, accum_out=ss[:, i, t:t + 1]).then_inc(ss_done, 1)
            act.wait_ge(ss_done, T * (i + 1))
            act.activation(std[:, i, :], ss[:, i, :], ACT.Sqrt, bias=eps[:, 0:1], scale=1.0 / D).then_inc(std_done, 1)

        def norm_hi(i):
            for k in range(KT):
                act.wait_ge(tr_done, KT * i + (k | 1) + 1)
                act.activation(xT_hi[:, k, :], G8[:, k, :], ACT.Copy, scale=gains[:, i, k:k + 1]).then_inc(nhi_done, 1)

        act.wait_ge(eps_set, 1)
        norm(0)
        hi_upto(AHEAD - 1)
        act.wait_ge(small_in, n_small)
        norm_hi(0)
        hi_upto(5 + AHEAD)
        act.wait_ge(pe_piece, 4)
        act.activation(qk[:, :, 0:512], Y[:, 0:2, :], ACT.Copy).then_inc(qkv_copied, 1)
        act.wait_ge(pe_piece, 6)
        act.activation(qk[:, :, 512:QK], Y[:, 2:4, 0:128], ACT.Copy).then_inc(qkv_copied, 1)
        act.activation(v_sb[:, :, :], Y[:, 2:4, 128:256], ACT.Copy).then_inc(qkv_copied, 1)
        hi_upto(6 + AHEAD)
        act.wait_ge(qk_ss, 1)
        act.activation(s_small[:, 20:40], s_small[:, 0:20], ACT.Sqrt, bias=eps[:, 0:1], scale=1.0 / HEAD_DIM).then_inc(qk_std, 1)
        hi_upto(13 + AHEAD)
        act.wait_ge(pe_piece, 14)
        act.activation(sig_b, G8[:, 4:8, :], ACT.Sigmoid).then_inc(sig_done, 1)
        act.wait_ge(qk_tr, 1)
        act.activation(qT[:, :, :], Y[:, 0:2, :].rearrange("p b (k n) -> p (b k) n", k=2), ACT.Copy).then_inc(qk_tr_copied, 1)
        act.activation(kT[:, :, :], Y[:, 2, :].rearrange("p (k n) -> p k n", k=2), ACT.Copy).then_inc(qk_tr_copied, 1)
        for i in range(HEADS + 2):
            if i < HEADS:
                act.wait_ge(neg_done, i + 1)
                for t in range(T):
                    act.activation(prob[:, i % 2, t, :], Y[:, i % 2, t * SEQ:(t + 1) * SEQ], ACT.Exp,
                                   bias=s_small[:, 44 + 2 * (i % 2) + t:45 + 2 * (i % 2) + t], scale=HEAD_DIM ** -0.5,
                                   accum_out=s_small[:, 48 + 2 * (i % 2) + t:49 + 2 * (i % 2) + t]).then_inc(exp_done, 1)
            if 1 <= i <= HEADS:
                act.wait_ge(pt_done, i)
                act.activation(probT[:, (i - 1) % 2, :, :],
                               Y[:, 2 + (i - 1) % 2, :].rearrange("p (k n) -> p k n", k=2), ACT.Copy).then_inc(pt_copied, 1)
            if i >= 3 and i % 2 == 1:
                c = (i - 3) // 2
                act.wait_ge(o_done, c + 1)
                act.activation(mT_hi[:, c, :], G[:, c, 0:SEQ], ACT.Copy).then_inc(o_hi, 1)
        hi_upto(17 + AHEAD)
        act.wait_ge(cent_done, 1)
        act.activation(ln_sq, conv, ACT.Square).then_inc(sq_done, 1)
        act.wait_ge(var_mm, 1)
        act.activation(ln_std, G[:, 1, 0:SEQ], ACT.Sqrt, bias=eps[:, 0:1]).then_inc(lnstd_done, 1)
        act.wait_ge(lnn_done, 1)
        for c in range(CT):
            act.activation(ln_out[:, c, :], conv[:, c, :], ACT.Silu, bias=ln_b[:, c:c + 1], scale=ln_g[:, c:c + 1]).then_inc(silu_c, 1)
        act.wait_ge(silu_c, CT)
        act.activation(mT_hi[:, 4:8, :], ln_out, ACT.Copy).then_inc(c_hi, 1)
        hi_upto(21 + AHEAD)
        norm(1)
        norm_hi(1)

        for n in range(6, ND):
            name, _, j, pieces = DENSE[n]
            if not name.startswith("ffn"):
                continue
            hi_upto(FIRST[n + 1] - 1 + AHEAD)
            f = pieces if name != "ffn_wd" else 0
            if name == "ffn_wg":
                act.wait_ge(pe_piece, FIRST[n + 1])
                if j >= 1:
                    act.wait_ge(flo, j)
                act.activation(ffn_act[:, 0:f, :], G8[:, 0:f, :], ACT.Silu).then_inc(fsilu, 1)
            if name == "ffn_wu":
                act.wait_ge(fmul, j + 1)
                b = 4 * (j % 2)
                act.activation(mT_hi[:, b:b + f, :], ffn_act[:, 0:f, :], ACT.Copy).then_inc(fhi, 1)

        def ple(i, gate_end, proj_end, split_last, split):
            split(split_last[0])
            act.wait_ge(ptok_tr, i + 1)
            act.activation(mT_hi[:, 0:2, :], G8[:, 0:2, :], ACT.Copy).then_inc(p_hi, 1)
            act.wait_ge(pe_piece, gate_end)
            for t in range(T):
                act.activation(tok[:, t, :], Y[:, 2 * t:2 * t + 2, :].rearrange("p b n -> p (b n)"), ACT.Sigmoid).then_inc(sig_gate, 1)
            split(split_last[1])

        act.dma_start(p_tok, a["p"][0, 0].rearrange("(t p) n -> p t n", p=P)).then_inc(p_in, 16)
        norm(2)
        norm_hi(2)
        g0 = [n for n in range(ND) if DENSE[n][0] == "proj0"][0]
        ple(0, FIRST[g0], FIRST[g0 + 1], (FIRST[g0] - 1 + AHEAD, FIRST[g0 + 1] - 1 + AHEAD), hi_upto)
        act.wait_ge(p_lo, 1)
        act.dma_start(bands, a["bands"].rearrange("p (t g n) -> p t g n", t=T, g=4)).then_inc(band_in, 16)
        norm(3)
        norm_hi(3)
        act.wait_ge(tr_done, 4 * KT)
        act.dma_start(scale_row, a["pool_scale"][0:1, :].broadcast_to([P, D])).then_inc(scale_in, 16)
        hi_upto(PB - 1 + AHEAD)
        act.activation(rw_hi[:, :, :], rw, ACT.Copy).then_inc(rw_hi_done, 1)
        norm(4)
        norm_hi(4)
        act.wait_ge(route_v, 1)
        act.activation(rt[:, 48:50], rt[:, 46:48], ACT.Exp).then_inc(gap_exp, 1)

        def gathered_hi(value):
            act.wait_ge(gath_mm, value)
            for k in range(KT):
                src = (G[:, 3, :], Y[:, 2, :])[k // 4][:, (k % 4) * P:(k % 4 + 1) * P]
                act.activation(xg_hi[:, k, :], src, ACT.Copy, scale=gains[:, 4, k:k + 1]).then_inc(xhi_done, 1)

        gathered_hi(1)

        def experts(first, last):
            with act.Fori(first, last) as it:
                for q in range(XP):
                    n = q + AHEAD
                    c, nxt = (n // 4) % NX, n // XP
                    act.wait_ge(pe_piece, it * XP + (PB + q + 1))
                    if n % 4 == 0:
                        act.wait_ge(slot_in[XSLOT[c]], it * (16 * PER) + 16 * (XFILL[c] + PER * nxt))
                    hi(PB + n, None, None, ring[:, XSLOT[c], (n % 4) * PIECE:(n % 4 + 1) * PIECE])
                    name, j = EXPERT[q // 4]
                    s = q % 4
                    if name == "moe_wg" and s == 3:
                        if j >= 1:
                            act.wait_ge(at_mm, it * GROUPS + j)
                            act.activation(aT_hi[:, (j - 1) % 2, :, :], G[:, 2, :].rearrange("p (f n) -> p f n", f=4),
                                           ACT.Copy).then_inc(at_hi, 1)
                        act.wait_ge(pe_piece, it * XP + (PB + q + 1))
                        act.activation(x_act, G[:, 0, :], ACT.Silu).then_inc(xsilu, 1)
                    if name == "moe_wu" and s == 3 and j == 3:
                        act.wait_ge(sp_mm, it + 1)
                        act.activation(spread, Y[:, 3, 0:SEQ], ACT.Copy).then_inc(sp_out, 1)
                    if name == "moe_wu" and s == 3 and j == GROUPS - 1:
                        gathered_hi(it + 2)
                    if name == "moe_wd" and s == 2 and j == GROUPS - 2:
                        act.wait_ge(at_mm, it * GROUPS + GROUPS)
                        act.activation(aT_hi[:, (GROUPS - 1) % 2, :, :], G[:, 2, :].rearrange("p (f n) -> p f n", f=4),
                                       ACT.Copy).then_inc(at_hi, 1)
                    if name == "moe_wd" and s == 3 and j == GROUPS - 1:
                        act.wait_ge(pe_piece, it * XP + (PB + q + 1))
                        act.activation(y_sb, Y[:, 0:2, :].rearrange("p b n -> p (b n)"), ACT.Copy).then_inc(y_out, 1)

        experts(0, NE)
        act.wait_ge(tabs_done, 1)
        n_most = act.value_load(most[0:1, 0:1])
        with act.If(n_most > P):
            experts(NE, ITERS)
        with act.Else():
            for s, base, per in ((hi_done, PB + AHEAD, XP), (y_out, 1, 1), (sp_out, 1, 1)):
                act.wait_ge(s, base + NE * per)
                act.sem_inc(s, NE * per)
            act.nop()

        tdid = [AHEAD]

        def tail_upto(last):
            while tdid[0] <= last:
                q = tdid[0]
                c = q // 4
                act.wait_ge(pe_piece, PT + q - AHEAD + 1)
                if q % 4 == 0:
                    act.wait_ge(slot_in[XSLOT[c]], 16 * (XFILL[c] + PER * ITERS))
                hi(PT + q, None, None, ring[:, XSLOT[c], (q % 4) * PIECE:(q % 4 + 1) * PIECE])
                tdid[0] += 1

        act.wait_ge(last_mm, 1)
        act.dma_start(p_tok, a["p"][1, 0].rearrange("(t p) n -> p t n", p=P)).then_inc(p_in, 16)
        norm(5)
        norm_hi(5)
        ple(1, PT + 8, PT + 10, (9, 9), tail_upto)

    @block.vector
    def _(dve):
        chain = [0]

        def link(ins):
            chain[0] += 1
            ins.then_inc(chain_v, 1)
            dve.wait_ge(chain_v, chain[0])

        def lo(n, where):
            dve.tensor_tensor(lo_ring[:, n % AHEAD, :], where, hi_ring[:, n % AHEAD, :].bitcast(F32),
                              ALU.subtract).then_inc(lo_done, 1)

        did = [0]

        def lo_upto(last):
            while did[0] <= last:
                n = did[0]
                dve.wait_ge(hi_done, n + 1)
                if n < PB:
                    c = max(m for m in range(ND) if FIRST[m] <= n)
                    off = (n - FIRST[c]) * PIECE
                    lo(n, ring[:, slot_of(c), off:off + PIECE])
                else:
                    lo(n, ring[:, XSLOT[0], (n - PB) * PIECE:(n - PB + 1) * PIECE])
                did[0] += 1

        def norm(i):
            dve.wait_ge(std_done, i + 1)
            link(dve.reciprocal(rstd[:, i, :], std[:, i, :]))
            for t in range(T):
                dve.tensor_scalar(tok[:, t, :], h[:, t, :], rstd[:, i, t:t + 1], None, ALU.mult).then_inc(tok_done, 1)

        def norm_lo(i):
            for k in range(KT):
                dve.wait_ge(nhi_done, KT * i + (k | 1) + 1)
                dve.scalar_tensor_tensor(out=xT_lo[:, k, :], in0=G8[:, k, :], scalar=gains[:, i, k:k + 1],
                                         in1=xT_hi[:, k, :].bitcast(F32), op0=ALU.mult, op1=ALU.subtract).then_inc(nlo_done, 1)

        def add_rows(end, count):
            dve.wait_ge(pe_piece, end)
            for t in range(T):
                ins = dve.tensor_tensor(h[:, t, :], h[:, t, :], Y[:, 2 * t:2 * t + 2, :].rearrange("p b n -> p (b n)"), ALU.add)
                ins.then_inc(h_half, 1)
            dve.wait_ge(h_half, T * count)
            dve.sem_inc(h_ready, 1)

        h_half = sem("h_half")

        dve.memset(eps[:, :], EPS).then_inc(eps_set, 1)
        dve.wait_ge(x_in, 16)
        dve.sem_inc(h_ready, 1)
        norm(0)
        lo_upto(AHEAD - 1)
        norm_lo(0)
        lo_upto(5 + AHEAD)
        dve.wait_ge(qkv_copied, 2)
        qkh = qk.rearrange("p t (n f) -> p (t n) f", f=HEAD_DIM)
        link(dve.tensor_tensor(sq, qk, qk, ALU.mult))
        dve.tensor_reduce(s_small[:, 0:20], sq.rearrange("p t (n f) -> p (t n) f", f=HEAD_DIM), AX.X, ALU.add).then_inc(qk_ss, 1)
        lo_upto(6 + AHEAD)
        dve.wait_ge(qk_std, 1)
        link(dve.reciprocal(s_small[:, 0:20], s_small[:, 20:40]))
        link(dve.tensor_tensor(qkh, qkh, s_small[:, 0:20].unsqueeze(2).broadcast_to([P, 20, HEAD_DIM]), ALU.mult))
        for t in range(T):
            ins = dve.tensor_tensor(qk[:, t, :], qk[:, t, :], qk_gain, ALU.mult)
        link(ins)
        for t in range(T):
            x = qk[:, t, :].rearrange("p (n c f) -> p n c f", c=2, f=HALF)
            cb = cos[:, t, :].unsqueeze(1).broadcast_to([P, 10, HALF])
            sn = sin[:, t, :].unsqueeze(1).broadcast_to([P, 10, HALF])
            r = rope[:, t]
            dve.tensor_tensor(r[:, 0], x[:, :, 0, :], cb, ALU.mult)
            dve.tensor_tensor(r[:, 1], x[:, :, 1, :], sn, ALU.mult)
            dve.tensor_tensor(r[:, 2], x[:, :, 1, :], cb, ALU.mult)
            ins = dve.tensor_tensor(r[:, 3], x[:, :, 0, :], sn, ALU.mult)
        link(ins)
        for t in range(T):
            r = rope[:, t]
            q_out = rot[:, t, 0:512].rearrange("p (n c f) -> p n c f", c=2, f=HALF)
            k_out = rot[:, t, 512:768].rearrange("p (n u c f) -> p n u c f", u=2, c=2, f=HALF)
            for c, (m, op) in enumerate(((0, ALU.subtract), (2, ALU.add))):
                ins = dve.tensor_tensor(q_out[:, :, c, :], r[:, m, 0:8, :], r[:, m + 1, 0:8, :], op)
                for u in range(2):
                    ins = dve.tensor_tensor(k_out[:, :, u, c, :], r[:, m, 8:10, :], r[:, m + 1, 8:10, :], op)
        ins.then_inc(qk_rot, 1)
        lo_upto(13 + AHEAD)
        dve.wait_ge(pads_set, 1)
        dve.wait_ge(sig_done, 1)
        dve.tensor_tensor(upad[:, :, PAD:PAD + SEQ], G8[:, 0:4, :], sig_b, ALU.mult).then_inc(glu_done, 1)
        dve.wait_ge(glu_done, 1)

        taps = [(k, c) for k in range(CONV_W) for c in range(CT - 1)]

        def tap(n):
            k, c = taps[n]
            if k == 0:
                dve.tensor_scalar(conv[:, c, :], upad[:, c, 0:SEQ], conv_w[:, c, 0:1], conv_b[:, c:c + 1],
                                  ALU.mult, ALU.add).then_inc(conv_v, 1)
            else:
                dve.wait_ge(conv_v, n - (CT - 1) + 1)
                dve.scalar_tensor_tensor(out=conv[:, c, :], in0=upad[:, c, k:k + SEQ], scalar=conv_w[:, c, k:k + 1],
                                         in1=conv[:, c, :], op0=ALU.mult, op1=ALU.add).then_inc(conv_v, 1)

        nt = 0
        for i in range(HEADS + 2):
            if i < HEADS:
                b = i % 2
                dve.wait_ge(sc_done, i + 1)
                link(dve.tensor_reduce(s_small[:, 40 + 2 * b:42 + 2 * b], Y[:, b, :].rearrange("p (t n) -> p t n", t=T), AX.X, ALU.max))
                dve.tensor_scalar(s_small[:, 44 + 2 * b:46 + 2 * b], s_small[:, 40 + 2 * b:42 + 2 * b], -HEAD_DIM ** -0.5,
                                  None, ALU.mult).then_inc(neg_done, 1)
            for _ in range(5):
                if nt < len(taps):
                    tap(nt)
                    nt += 1
            if i < HEADS:
                dve.wait_ge(exp_done, T * (i + 1))
                link(dve.reciprocal(s_small[:, 52 + 2 * b:54 + 2 * b], s_small[:, 48 + 2 * b:50 + 2 * b]))
                for t in range(T):
                    ins = dve.tensor_scalar(prob[:, b, t, :], prob[:, b, t, :], s_small[:, 52 + 2 * b + t:53 + 2 * b + t], None, ALU.mult)
                ins.then_inc(nrm_done, 1)
            if i >= 3 and i % 2 == 1:
                c = (i - 3) // 2
                dve.wait_ge(o_hi, c + 1)
                dve.tensor_tensor(mT_lo[:, c, :], G[:, c, 0:SEQ], mT_hi[:, c, :].bitcast(F32), ALU.subtract).then_inc(o_lo, 1)
        while nt < len(taps):
            if nt % 12 == 0 and did[0] <= 17 + AHEAD:
                lo_upto(did[0])
            tap(nt)
            nt += 1
        lo_upto(17 + AHEAD)
        dve.wait_ge(mean_mm, 1)
        dve.wait_ge(conv_p, 1)
        dve.tensor_tensor(conv, conv, G[:, 0, 0:SEQ].unsqueeze(1).broadcast_to([P, CT, SEQ]), ALU.subtract).then_inc(cent_done, 1)
        dve.wait_ge(lnstd_done, 1)
        link(dve.reciprocal(ln_rstd, ln_std))
        dve.tensor_tensor(conv, conv, ln_rstd.unsqueeze(1).broadcast_to([P, CT, SEQ]), ALU.mult).then_inc(lnn_done, 1)
        dve.wait_ge(c_hi, 1)
        dve.tensor_tensor(mT_lo[:, 4:8, :], ln_out, mT_hi[:, 4:8, :].bitcast(F32), ALU.subtract).then_inc(c_lo, 1)
        lo_upto(21 + AHEAD)
        add_rows(22, 1)
        norm(1)
        norm_lo(1)

        for n in range(6, ND):
            name, _, j, pieces = DENSE[n]
            if not name.startswith("ffn"):
                continue
            lo_upto(FIRST[n + 1] - 1 + AHEAD)
            if name == "ffn_wu":
                b = 4 * (j % 2)
                dve.wait_ge(pe_piece, FIRST[n + 1])
                dve.wait_ge(fsilu, j + 1)
                dve.tensor_tensor(ffn_act[:, 0:pieces, :], ffn_act[:, 0:pieces, :], G8[:, 4:4 + pieces, :], ALU.mult).then_inc(fmul, 1)
                dve.wait_ge(fhi, j + 1)
                dve.tensor_tensor(mT_lo[:, b:b + pieces, :], ffn_act[:, 0:pieces, :], mT_hi[:, b:b + pieces, :].bitcast(F32),
                                  ALU.subtract).then_inc(flo, 1)
        add_rows(FIRST[ND - 4], 2)

        def ple(i, proj_end, split_last, split):
            split(split_last[0])
            dve.wait_ge(p_hi, i + 1)
            dve.tensor_tensor(mT_lo[:, 0:2, :], G8[:, 0:2, :], mT_hi[:, 0:2, :].bitcast(F32), ALU.subtract).then_inc(p_lo, 1)
            split(split_last[1])
            dve.wait_ge(pe_piece, proj_end)
            for t in range(T):
                dve.wait_ge(sig_gate, T * i + t + 1)
                link(dve.tensor_tensor(tok[:, t, :], tok[:, t, :], G[:, 2 * t:2 * t + 2, :].rearrange("p b n -> p (b n)"), ALU.mult))
                dve.tensor_tensor(h[:, t, :], h[:, t, :], tok[:, t, :], ALU.add).then_inc(gated, 1)

        norm(2)
        norm_lo(2)
        g0 = [n for n in range(ND) if DENSE[n][0] == "proj0"][0]
        ple(0, FIRST[g0 + 1], (FIRST[g0] - 1 + AHEAD, FIRST[g0 + 1] - 1 + AHEAD), lo_upto)
        dve.wait_ge(gated, T)
        dve.sem_inc(h_ready, 1)
        norm(3)
        norm_lo(3)
        lo_upto(PB - 1 + AHEAD)
        dve.wait_ge(rw_hi_done, 1)
        dve.tensor_tensor(rw_lo[:, :, :], rw, rw_hi[:, :, :].bitcast(F32), ALU.subtract).then_inc(rw_lo_done, 1)
        dve.wait_ge(pe_piece, PB)
        dve.wait_ge(scale_in, 16)
        for t in range(T):
            dve.tensor_tensor(tok[:, t, :], Y[:, 2 * t:2 * t + 2, :].rearrange("p b n -> p (b n)"), scale_row, ALU.mult).then_inc(scaled, 1)
        dve.wait_ge(scaled, T)
        for t in range(T):
            ins = dve.tensor_tensor(h[:, t, :], h[:, t, :], tok[:, t, :], ALU.add)
        link(ins)
        dve.sem_inc(h_ready, 1)
        norm(4)
        norm_lo(4)

        logit = rt[:, 0:16].rearrange("p (t e) -> p t e", t=T)
        best = rt[:, 16:32].rearrange("p (t e) -> p t e", t=T)
        idxf = rt[:, 32:36].rearrange("p (t e) -> p t e", t=T)
        gap, ex = rt[:, 46:48], rt[:, 48:50]
        p1, p2, one_more = rt[:, 50:52], rt[:, 52:54], rt[:, 54:56]
        hot1 = rt[:, 56:72].rearrange("p (t e) -> p t e", t=T)
        hot2 = rt[:, 72:88].rearrange("p (t e) -> p t e", t=T)
        mask = rt[:, 88:104].rearrange("p (t e) -> p t e", t=T)
        gate_a = rt[:, 104:120].rearrange("p (t e) -> p t e", t=T)
        rank1 = rt[:, 120:136].rearrange("p (t e) -> p t e", t=T)
        top_count = rt[:, 136:137]
        dve.wait_ge(logit_mm, 1)
        link(dve.tensor_copy(logit, Y[:, 0, 0:16].rearrange("p (t e) -> p t e", t=T)))
        for t in range(T):
            link(dve.max(best[:, t, :], logit[:, t, :]))
            link(dve.max_index(idx8[:, t, :], best[:, t, :], logit[:, t, :]))
        link(dve.tensor_copy(idxf, idx8[:, :, 0:2]))
        dve.tensor_tensor(gap, best[:, :, 1], best[:, :, 0], ALU.subtract).then_inc(route_v, 1)
        for t in range(T):
            dve.tensor_scalar(hot1[:, t, :], iota[:, 0:NE], idxf[:, t, 0:1], None, ALU.is_equal)
            ins = dve.tensor_scalar(hot2[:, t, :], iota[:, 0:NE], idxf[:, t, 1:2], None, ALU.is_equal)
        link(ins)
        dve.tensor_tensor(mask, hot1, hot2, ALU.add).then_inc(mask_done, 1)
        dve.wait_ge(gap_exp, 1)
        link(dve.tensor_scalar(one_more, ex, 1.0, None, ALU.add))
        link(dve.reciprocal(p1, one_more))
        link(dve.tensor_tensor(p2, p1, ex, ALU.mult))
        for t in range(T):
            link(dve.tensor_scalar(gate_a[:, t, :], hot1[:, t, :], p1[:, t:t + 1], None, ALU.mult))
            link(dve.scalar_tensor_tensor(out=gate_a[:, t, :], in0=hot2[:, t, :], scalar=p2[:, t:t + 1], in1=gate_a[:, t, :],
                                          op0=ALU.mult, op1=ALU.add))
        for s in range(2):
            dve.tensor_copy(gate_tab[:, :, s * NE:(s + 1) * NE], gate_a)
        dve.memset(gate_tab[:, :, ITERS:], 0.0)
        dve.memset(slot_tab[:, :, ITERS:], NOWHERE)
        dve.wait_ge(mask_done, 1)
        dve.wait_ge(rank_mm, 1)
        ranks = Y[:, 1, 0:16].rearrange("p (t e) -> p t e", t=T)
        link(dve.scalar_tensor_tensor(out=rank1, in0=ranks, scalar=-NOWHERE, in1=mask, op0=ALU.add, op1=ALU.mult))
        for s in range(2):
            dve.tensor_scalar(slot_tab[:, :, s * NE:(s + 1) * NE], rank1, NOWHERE - s * P, None, ALU.add)
        link(dve.tensor_reduce(top_count, Y[:, 2, 0:8], AX.X, ALU.max))
        link(dve.tensor_copy(most[:, :], top_count))
        dve.sem_inc(tabs_done, 1)

        def gathered_lo(value):
            for k in range(KT):
                dve.wait_ge(xhi_done, value + (k | 3) + 1)
                src = (G[:, 3, :], Y[:, 2, :])[k // 4][:, (k % 4) * P:(k % 4 + 1) * P]
                dve.scalar_tensor_tensor(out=xg_lo[:, k, :], in0=src, scalar=gains[:, 4, k:k + 1],
                                         in1=xg_hi[:, k, :].bitcast(F32), op0=ALU.mult, op1=ALU.subtract).then_inc(xlo_done, 1)

        def picks(it):
            for t in range(T):
                slot = slot_tab[:, t, bass.ds(it, 1)]
                dve.tensor_scalar(pick[:, t, :], iota, slot, rstd[:, 4, t:t + 1], ALU.is_equal, ALU.mult).then_inc(pick_done, 1)
                dve.tensor_scalar(pick_gated[:, t, :], iota, slot, gate_tab[:, t, bass.ds(it, 1)], ALU.is_equal, ALU.mult).then_inc(pick_done, 1)

        picks(0)
        gathered_lo(0)

        def experts(first, last):
            with dve.Fori(first, last) as it:
                for q in range(XP):
                    n = q + AHEAD
                    c = (n // 4) % NX
                    dve.wait_ge(hi_done, it * XP + (PB + n + 1))
                    lo(PB + n, ring[:, XSLOT[c], (n % 4) * PIECE:(n % 4 + 1) * PIECE])
                    name, j = EXPERT[q // 4]
                    s = q % 4

                    def at_low(j):
                        dve.wait_ge(at_hi, it * GROUPS + (j + 1))
                        dve.tensor_tensor(aT_lo[:, j % 2, :, :], G[:, 2, :].rearrange("p (f n) -> p f n", f=4),
                                          aT_hi[:, j % 2, :, :].bitcast(F32), ALU.subtract).then_inc(at_lo, 1)

                    if name == "moe_wg" and s == 3:
                        if j >= 1:
                            at_low(j - 1)
                        else:
                            dve.wait_ge(scat_mm, it + 1)
                            dve.wait_ge(scat_add, it * 4 + 1)
                            for u, src in enumerate((G[:, 3, :], Y[:, 2, :], Y[:, 3, :], G[:, 2, :])):
                                acc = tok[:, u // 2, (u % 2) * 512:(u % 2 + 1) * 512]
                                dve.tensor_tensor(acc, acc, src, ALU.add).then_inc(scat_add, 1)
                    if name == "moe_wu" and s == 0 and j == 5:
                        dve.wait_ge(sp_mm, it + 1)
                        picks(it + 1)
                    if name == "moe_wu" and s == 3:
                        dve.wait_ge(pe_piece, it * XP + (PB + q + 1))
                        dve.wait_ge(xsilu, it * GROUPS + (j + 1))
                        dve.tensor_tensor(x_act, x_act, G[:, 1, :], ALU.mult).then_inc(xmul, 1)
                        if j == GROUPS - 1:
                            gathered_lo(it * KT + KT)
                    if name == "moe_wd" and s == 2 and j == GROUPS - 2:
                        at_low(GROUPS - 1)

        experts(0, NE)
        dve.wait_ge(tabs_done, 1)
        n_most = dve.value_load(most[0:1, 0:1])
        with dve.If(n_most > P):
            experts(NE, ITERS)
        with dve.Else():
            for s, base, per in ((lo_done, PB + AHEAD, XP), (xlo_done, KT, KT), (scat_add, 1, 4)):
                dve.wait_ge(s, base + NE * per)
                dve.sem_inc(s, NE * per)
            dve.nop()
        dve.wait_ge(last_mm, 1)
        dve.wait_ge(scat_add, 4 * ITERS + 1)
        for u, src in enumerate((G[:, 3, :], Y[:, 2, :], Y[:, 3, :], G[:, 2, :])):
            acc = tok[:, u // 2, (u % 2) * 512:(u % 2 + 1) * 512]
            dve.tensor_tensor(acc, acc, src, ALU.add).then_inc(scat_add, 1)
        dve.wait_ge(scat_add, 4 * ITERS + 5)
        for t in range(T):
            ins = dve.tensor_tensor(h[:, t, :], h[:, t, :], tok[:, t, :], ALU.add)
        link(ins)
        dve.sem_inc(h_ready, 1)

        tdid = [AHEAD]

        def tail_upto(last):
            while tdid[0] <= last:
                q = tdid[0]
                dve.wait_ge(hi_done, PT + q + 1)
                lo(PT + q, ring[:, XSLOT[q // 4], (q % 4) * PIECE:(q % 4 + 1) * PIECE])
                tdid[0] += 1

        norm(5)
        norm_lo(5)
        ple(1, PT + 10, (9, 9), tail_upto)

    @block.gpsimd
    def _(pool):
        pool.memset(upad[:, :, 0:PAD], 0.0)
        pool.memset(upad[:, :, PAD + SEQ:], 0.0).then_inc(pads_set, 1)
        c = CT - 1
        pool.wait_ge(small_in, 16 * 3)
        pool.wait_ge(glu_done, 1)
        pool.wait_ge(qk_tr, 1)
        pool.tensor_scalar(conv[:, c, :], upad[:, c, 0:SEQ], conv_w[:, c, 0:1], conv_b[:, c:c + 1], ALU.mult, ALU.add).then_inc(chain_p, 1)
        n = 1
        for k in range(1, CONV_W):
            tmp = rot[:, 0, (k % 2) * SEQ:(k % 2 + 1) * SEQ]
            pool.tensor_scalar(tmp, upad[:, c, k:k + SEQ], conv_w[:, c, k:k + 1], None, ALU.mult).then_inc(chain_p, 1)
            n += 1
            pool.wait_ge(chain_p, n)
            ins = pool.tensor_tensor(conv[:, c, :], conv[:, c, :], tmp, ALU.add)
            ins.then_inc(chain_p, 1)
            n += 1
        pool.wait_ge(chain_p, n)
        pool.sem_inc(conv_p, 1)

        pool.wait_ge(tabs_done, 1)
        pool.memset(y_sb, 0.0).then_inc(y_out, 1)
        pool.memset(spread, 0.0).then_inc(sp_out, 1)
        pool.memset(tok[:, :, :], 0.0).then_inc(scat_add, 1)

    @block.tensor
    def _(pe):
        def piece(n, last):
            last.then_inc(pe_piece, 1)

        def three(dst, s_hi, s_lo, m_hi, m_lo, start, stop):
            pe.matmul(dst, s_hi, m_hi, start=start, stop=False, skip_group_check=True)
            pe.matmul(dst, s_lo, m_hi, start=False, stop=False, skip_group_check=True)
            return pe.matmul(dst, s_hi, m_lo, start=False, stop=stop, skip_group_check=True)

        def norm(i):
            pe.wait_ge(tok_done, T * (i + 1))
            for k in range(KT):
                for t in range(T):
                    ins = pe.transpose(G8[:, k, t * P:(t + 1) * P], tok[:, t, k * P:(k + 1) * P], ident)
                ins.then_inc(tr_done, 1)

        def cols_tokens(n0, pieces, dst, width, i, wait_k):
            per = PIECE // width
            for s in range(pieces):
                pe.wait_ge(lo_done, n0 + s + 1)
                w_hi, w_lo = piece_at(hi_ring, n0 + s, width), piece_at(lo_ring, n0 + s, width)
                for r in range(per):
                    k = s * per + r
                    if wait_k:
                        pe.wait_ge(nlo_done, KT * i + k + 1)
                    for t in range(T):
                        ins = three(dst(t), xT_hi[:, k, t * P:(t + 1) * P], xT_lo[:, k, t * P:(t + 1) * P],
                                    w_hi[:, r, :], w_lo[:, r, :], k == 0, k == KT - 1)
                piece(n0 + s, ins)
            return ins

        def cols_channels(n0, pieces, bank0, width, i):
            per = PIECE // width
            tiles = width // P
            pe.wait_ge(nlo_done, KT * (i + 1))
            for s in range(pieces):
                pe.wait_ge(lo_done, n0 + s + 1)
                w_hi, w_lo = piece_at(hi_ring, n0 + s, width), piece_at(lo_ring, n0 + s, width)
                for r in range(per):
                    k = s * per + r
                    for f in range(tiles):
                        ins = three(G8[:, 2 * bank0 + f, :], w_hi[:, r, f * P:(f + 1) * P], w_lo[:, r, f * P:(f + 1) * P],
                                    xT_hi[:, k, :], xT_lo[:, k, :], k == 0 and f % 2 == 0, k == KT - 1)
                piece(n0 + s, ins)
            return ins

        def rows(n, s_hi, s_lo, bank, first, last):
            pe.wait_ge(lo_done, n + 1)
            w_hi, w_lo = hi_ring[:, n % AHEAD, :], lo_ring[:, n % AHEAD, :]
            for t in range(T):
                for c in range(2):
                    ins = three(bank[:, 2 * t + c, :], s_hi[:, t * P:(t + 1) * P], s_lo[:, t * P:(t + 1) * P],
                                w_hi[:, c * 512:(c + 1) * 512], w_lo[:, c * 512:(c + 1) * 512], first, last)
            piece(n, ins)
            return ins

        pe.wait_ge(small_in, 16 * 3)
        norm(0)
        cols_tokens(0, 4, lambda t: Y[:, t, :], 512, 0, True)
        cols_tokens(4, 2, lambda t: Y[:, 2 + t, 0:256], 256, 0, False)
        cols_channels(6, 4, 0, 512, 0)
        cols_channels(10, 4, 2, 512, 0)
        pe.wait_ge(qk_rot, 1)
        pe.wait_ge(qkv_copied, 3)
        for c in range(6):
            for t in range(T):
                ins = pe.transpose(Y[:, c // 2, (c % 2) * SEQ + t * P:(c % 2) * SEQ + (t + 1) * P],
                                   rot[:, t, c * P:(c + 1) * P], ident)
        ins.then_inc(qk_tr, 1)
        pe.wait_ge(qk_tr_copied, 2)
        for i in range(HEADS + 2):
            if i < HEADS:
                if i >= 2:
                    pe.wait_ge(exp_done, T * (i - 1))
                lo_p = (i % 2) * HEAD_DIM
                for t in range(T):
                    ins = pe.matmul(Y[:, i % 2, t * SEQ:(t + 1) * SEQ], qT[lo_p:lo_p + HEAD_DIM, i // 2, t * P:(t + 1) * P],
                                    kT[lo_p:lo_p + HEAD_DIM, i // 4, :], start=True, stop=True)
                ins.then_inc(sc_done, 1)
            if 1 <= i <= HEADS:
                hd = i - 1
                pe.wait_ge(nrm_done, hd + 1)
                if hd >= 2:
                    pe.wait_ge(pt_copied, hd - 1)
                for k in range(T):
                    for t in range(T):
                        ins = pe.transpose(Y[:, 2 + hd % 2, k * SEQ + t * P:k * SEQ + (t + 1) * P],
                                           prob[:, hd % 2, t, k * P:(k + 1) * P], ident)
                ins.then_inc(pt_done, 1)
            if i >= 2:
                hd = i - 2
                pe.wait_ge(pt_copied, hd + 1)
                pe.wait_ge(glu_done, 1)
                lo_p = (hd % 2) * HEAD_DIM
                for k in range(T):
                    ins = pe.matmul(G[lo_p:lo_p + HEAD_DIM, hd // 2, 0:SEQ],
                                    v_sb[:, k, (hd // 4) * HEAD_DIM:(hd // 4 + 1) * HEAD_DIM],
                                    probT[:, hd % 2, k, :], start=(k == 0), stop=(k == T - 1))
                if hd % 2:
                    ins.then_inc(o_done, 1)
        pe.wait_ge(o_lo, 4)
        for e in range(4):
            rows(14 + e, mT_hi[:, e, :], mT_lo[:, e, :], Y, e == 0, False)
        pe.wait_ge(conv_v, CONV_W * (CT - 1))
        pe.wait_ge(conv_p, 1)
        for c in range(CT):
            ins = pe.matmul(G[:, 0, 0:SEQ], mean_mat, conv[:, c, :], start=(c == 0), stop=(c == CT - 1))
        ins.then_inc(mean_mm, 1)
        pe.wait_ge(sq_done, 1)
        for c in range(CT):
            ins = pe.matmul(G[:, 1, 0:SEQ], mean_mat, ln_sq[:, c, :], start=(c == 0), stop=(c == CT - 1))
        ins.then_inc(var_mm, 1)
        pe.wait_ge(c_lo, 1)
        for e in range(4, 8):
            rows(14 + e, mT_hi[:, e, :], mT_lo[:, e, :], Y, False, e == 7)

        norm(1)
        for n in range(6, ND):
            name, _, j, pieces = DENSE[n]
            if name == "ffn_wg":
                if j >= 1:
                    pe.wait_ge(fsilu, j)
                cols_channels(FIRST[n], pieces, 0, COLS * pieces // 4, 1)
            if name == "ffn_wu":
                if j >= 1:
                    pe.wait_ge(fmul, j)
                cols_channels(FIRST[n], pieces, 2, COLS * pieces // 4, 1)
            if name == "ffn_wd":
                pe.wait_ge(flo, j + 1)
                for f in range(pieces):
                    b = 4 * (j % 2) + f
                    rows(FIRST[n] + f, mT_hi[:, b, :], mT_lo[:, b, :], Y, j == 0 and f == 0, j * COLS + (f + 1) * P == FFN)

        def ple(i, norm_i, gate_n, proj_n):
            pe.wait_ge(p_in, 16 * (i + 1))
            pe.wait_ge(nlo_done, KT * (norm_i + 1))
            for k in range(2):
                for t in range(T):
                    ins = pe.transpose(G8[:, k, t * P:(t + 1) * P], p_tok[:, t, k * P:(k + 1) * P], ident)
            ins.then_inc(ptok_tr, 1)
            for k in range(KT):
                rows(gate_n + k, xT_hi[:, k, :], xT_lo[:, k, :], Y, k == 0, k == KT - 1)
            pe.wait_ge(p_lo, i + 1)
            for k in range(2):
                rows(proj_n + k, mT_hi[:, k, :], mT_lo[:, k, :], G, k == 0, k == 1)

        norm(2)
        g0 = [n for n in range(ND) if DENSE[n][0] == "proj0"][0]
        ple(0, 2, FIRST[g0 - 2], FIRST[g0])

        pe.wait_ge(tok_done, T * 4)
        pe.wait_ge(band_in, 16)
        for k in range(KT):
            for t in range(T):
                ins = pe.matmul(G8[:, k, :], tok[:, t, k * P:(k + 1) * P], bands[:, t, k // 2, :], start=(t == 0), stop=(t == T - 1))
            ins.then_inc(tr_done, 1)
        for s in range(2):
            n = FIRST[ND - 1] + s
            pe.wait_ge(lo_done, n + 1)
            w_hi, w_lo = piece_at(hi_ring, n, 256), piece_at(lo_ring, n, 256)
            for r in range(4):
                g, k = 2 * s + r // 2, 4 * s + r
                pe.wait_ge(nlo_done, KT * 3 + k + 1)
                for t in range(T):
                    ins = three(Y[:, 2 * t + g // 2, (g % 2) * 256:(g % 2 + 1) * 256], xT_hi[:, k, t * P:(t + 1) * P],
                                xT_lo[:, k, t * P:(t + 1) * P], w_hi[:, r, :], w_lo[:, r, :], k % 4 == 0, k % 2 == 1)
            piece(n, ins)

        norm(4)
        pe.wait_ge(nlo_done, KT * 5)
        pe.wait_ge(rw_lo_done, 1)
        for t in range(T):
            for k in range(KT):
                ins = three(Y[:, 0, t * NE:(t + 1) * NE], xT_hi[:, k, t * P:(t + 1) * P], xT_lo[:, k, t * P:(t + 1) * P],
                            rw_hi[:, k, :], rw_lo[:, k, :], t == 0 and k == 0, k == KT - 1)
        ins.then_inc(logit_mm, 1)
        pe.wait_ge(mask_done, 1)
        mask = rt[:, 88:104].rearrange("p (t e) -> p t e", t=T)
        pe.matmul(Y[:, 1, 0:NE], before_mat, mask[:, 0, :], start=True, stop=True)
        pe.matmul(Y[:, 1, NE:2 * NE], before_mat, mask[:, 1, :], start=True, stop=False)
        pe.matmul(Y[:, 1, NE:2 * NE], ones_mat, mask[:, 0, :], start=False, stop=True)
        pe.matmul(Y[:, 2, 0:NE], ones_mat, mask[:, 0, :], start=True, stop=False)
        pe.matmul(Y[:, 2, 0:NE], ones_mat, mask[:, 1, :], start=False, stop=True).then_inc(rank_mm, 1)

        def gather():
            for k in range(KT):
                dst = (G[:, 3, :], Y[:, 2, :])[k // 4][:, (k % 4) * P:(k % 4 + 1) * P]
                for t in range(T):
                    ins = pe.matmul(dst, h[:, t, k * P:(k + 1) * P], pick[:, t, :], start=(t == 0), stop=(t == T - 1))
            ins.then_inc(gath_mm, 1)

        def scatter():
            for u, dst in enumerate((G[:, 3, :], Y[:, 2, :], Y[:, 3, :], G[:, 2, :])):
                ins = pe.matmul(dst, spread[:, (u // 2) * P:(u // 2 + 1) * P], y_sb[:, (u % 2) * 512:(u % 2 + 1) * 512],
                                start=True, stop=True)
            return ins

        pe.wait_ge(pick_done, 4)
        pe.wait_ge(tabs_done, 1)
        gather()

        def experts(first, last):
            with pe.Fori(first, last) as it:
                def transposes(j):
                    pe.wait_ge(xmul, it * GROUPS + (j + 1))
                    if j:
                        pe.wait_ge(at_lo, it * GROUPS + j)
                    else:
                        pe.wait_ge(scat_add, it * 4 + 5)
                    for f in range(4):
                        ins = pe.transpose(G[:, 2, f * P:(f + 1) * P], x_act[:, f * P:(f + 1) * P], ident)
                    ins.then_inc(at_mm, 1)

                for i, (name, j) in enumerate(EXPERT):
                    if name == "moe_wd":
                        for f in range(4):
                            if f == 0:
                                pe.wait_ge(at_lo, it * GROUPS + (j + 1))
                            n = PB + 4 * i + f
                            pe.wait_ge(lo_done, it * XP + (n + 1))
                            for c in range(2):
                                ins = three(Y[:, c, :], aT_hi[:, j % 2, f, :], aT_lo[:, j % 2, f, :],
                                            hi_ring[:, n % AHEAD, c * 512:(c + 1) * 512], lo_ring[:, n % AHEAD, c * 512:(c + 1) * 512],
                                            j == 0 and f == 0, j == GROUPS - 1 and f == 3)
                            piece(n, ins)
                            if j == GROUPS - 2 and f == 2:
                                transposes(GROUPS - 1)
                        continue
                    bank, free = (0, xsilu) if name == "moe_wg" else (1, xmul)
                    if j:
                        pe.wait_ge(free, it * GROUPS + j)
                    if name == "moe_wg" and j == 0:
                        pe.wait_ge(xlo_done, it * KT + KT)
                    for s in range(4):
                        n = PB + 4 * i + s
                        pe.wait_ge(lo_done, it * XP + (n + 1))
                        w_hi, w_lo = piece_at(hi_ring, n, 512), piece_at(lo_ring, n, 512)
                        for r in range(2):
                            k = 2 * s + r
                            ins = three(G[:, bank, :], xg_hi[:, k, :], xg_lo[:, k, :], w_hi[:, r, :], w_lo[:, r, :],
                                        k == 0, k == KT - 1)
                        piece(n, ins)
                    if name == "moe_wg":
                        if j == 0:
                            pe.wait_ge(y_out, it + 1)
                            pe.wait_ge(sp_out, it + 1)
                            scatter().then_inc(scat_mm, 1)
                        else:
                            transposes(j - 1)
                    elif j == 3:
                        pe.wait_ge(pick_done, it * 4 + 4)
                        pe.wait_ge(scat_add, it * 4 + 5)
                        for t in range(T):
                            ins = pe.transpose(Y[:, 3, t * P:(t + 1) * P], pick_gated[:, t, :], ident)
                        ins.then_inc(sp_mm, 1)
                    elif j == GROUPS - 1:
                        pe.wait_ge(pick_done, it * 4 + 8)
                        gather()

        experts(0, NE)
        n_most = pe.value_load(most[0:1, 0:1])
        with pe.If(n_most > P):
            experts(NE, ITERS)
        with pe.Else():
            pe.wait_ge(pe_piece, PB + NE * XP)
            pe.sem_inc(pe_piece, NE * XP)
            pe.nop()
        pe.wait_ge(xlo_done, ITERS * KT + KT)
        pe.wait_ge(y_out, ITERS + 1)
        pe.wait_ge(sp_out, ITERS + 1)
        scatter().then_inc(last_mm, 1)
        norm(5)
        ple(1, 5, PT, PT + 8)

    block.__exit__(None, None, None)


def host_constants():
    c = np.zeros((P, C_END), np.float32)
    c[:, C_IDENT:C_IOTA] = np.eye(P)
    c[:, C_IOTA:C_MEAN] = np.arange(P)[None, :]
    c[:, C_MEAN:C_ONES] = 1.0 / CONV_CH
    c[:, C_ONES:C_BEFORE] = 1.0
    c[:, C_BEFORE:C_COS] = np.arange(P)[:, None] < np.arange(P)[None, :]
    pos = np.arange(SEQ)
    inv = (np.float32(10000.0) ** (-np.arange(0, HALF, 2, dtype=np.float32) / np.float32(HALF))).astype(np.float32)
    row, col = (pos // GRID_W).astype(np.float32), (pos % GRID_W).astype(np.float32)
    ang = np.concatenate([row[:, None] * inv, col[:, None] * inv], axis=-1).astype(np.float32)
    c[:, C_COS:C_SIN] = np.cos(ang).reshape(T, P, HALF).transpose(1, 0, 2).reshape(P, -1)
    c[:, C_SIN:C_END] = np.sin(ang).reshape(T, P, HALF).transpose(1, 0, 2).reshape(P, -1)
    bands = np.zeros((4, SEQ, SEQ), np.float32)
    for g, w in enumerate(POOL_WINDOWS):
        lo = np.clip(pos - w // 2, 0, SEQ - 1)
        hi = np.clip(pos + w - 1 - w // 2, 0, SEQ - 1)
        for t in range(SEQ):
            bands[g, lo[t]:hi[t] + 1, t] = 1.0 / (hi[t] - lo[t] + 1)
            bands[g, t, t] -= 1.0
    bands = bands.reshape(4, T, P, SEQ).transpose(2, 1, 0, 3).reshape(P, -1)
    return c, np.ascontiguousarray(bands)


def vectors(v):
    def along(x):
        return x.reshape(-1, P).T

    parts = [along(v[n][i]) for i in range(2) for n in ("norm_mix", "norm_ffn", "ple_norm")]
    parts.append(v["conv_w"][0].reshape(CONV_W, CT, P).transpose(2, 1, 0).reshape(P, -1))
    parts += [along(v[n][0]) for n in ("conv_b", "conv_ln_g", "conv_ln_b")]
    parts.append(v["router_w"][0].reshape(KT, P, NE).transpose(1, 0, 2).reshape(P, -1))
    return np.ascontiguousarray(np.concatenate(parts, axis=1))


_INS = ["x", "p", "w_in", "w_out", "ffn_wg", "ffn_wu", "ffn_wd", "pool_w", "pool_scale", "moe_wg", "moe_wu", "moe_wd",
        "ple_gate_w", "ple_proj"]


def kernel(**inputs):
    import concourse.bacc as _bacc
    from concourse.bass_utils import run_bass_kernel_spmd as _run

    nc = _bacc.Bacc("TRN2", target_bir_lowering=False, num_devices=1)
    consts, bands = host_constants()
    arrays = {f"in_{n}": np.ascontiguousarray(inputs[n]) for n in _INS}
    arrays["in_consts"], arrays["in_bands"] = consts, bands
    v = {n: np.asarray(inputs[n]) for n in inputs}
    arrays["in_vectors"] = vectors(v)
    arrays["in_qk_gain"] = np.concatenate([v["q_norm"][0]] * HEADS + [v["k_norm"][0]] * KV_HEADS)[None, :]
    a = {n[3:]: nc.dram_tensor(n, x.shape, mybir.dt.from_np(x.dtype), kind="ExternalInput").ap() for n, x in arrays.items()}
    out = nc.dram_tensor("out_0", (1, SEQ, D), F32, kind="ExternalOutput").ap()
    kernel_program(nc, a, out)
    r = _run(nc, [arrays], core_ids=[0])
    return r.results[0]["out_0"]
```

```python
import concourse.bass as bass
import numpy as np
from concourse import mybir

F32 = mybir.dt.float32
F32R = mybir.dt.float32r
I32 = mybir.dt.int32
U32 = mybir.dt.uint32
ALU = mybir.AluOpType
ACT = mybir.ActivationFunctionType
AX = mybir.AxisListType

P = 128
D = 1024
SEQ = 256
T = SEQ // P
KT = D // P
GRID_W = 64
HEADS, KV_HEADS, HEAD_DIM = 8, 2, 64
HALF = HEAD_DIM // 2
QK = (HEADS + KV_HEADS) * HEAD_DIM
CONV_CH, CONV_W = 512, 31
CT = CONV_CH // P
PAD = CONV_W // 2
POOL_WINDOWS = (2, 4, 8, 16)
FFN = 2816
NE, EF = 8, 3584
PLE = 256
EPS = 1e-6

COLS = 512
ROWS = 4
PIECE = 1024
CHUNK = 4 * PIECE
RING = 7
AHEAD = 4
FREE_AFTER = 4
NOWHERE = -1000.0

C_IDENT, C_IOTA, C_MEAN, C_ONES, C_BEFORE, C_COS, C_SIN, C_END = 0, 128, 256, 384, 512, 640, 704, 768

V_GAINS, V_CONV_W = 0, 6 * KT
V_CONV_B = V_CONV_W + CT * CONV_W
V_LN_G, V_LN_B, V_ROUTER = V_CONV_B + CT, V_CONV_B + 2 * CT, V_CONV_B + 3 * CT
V_END = V_ROUTER + KT * NE


def dense_chunks():
    out = [("w_in", "a", 0, 4), ("w_in", "b", 0, 4), ("w_in", "col", 0, 4), ("w_in", "kv", 0, 2),
           ("w_out", "row", 0, 4), ("w_out", "row", 1, 4)]
    groups = -(-FFN // COLS)
    for j in range(groups + 1):
        n = 4 if (j + 1) * COLS <= FFN else 2
        if j < groups:
            out += [("ffn_wg", "col", j, n), ("ffn_wu", "col", j, n)]
        if j >= 1:
            n = 4 if j * COLS <= FFN else 2
            out.append(("ffn_wd", "row", j - 1, n))
    out += [("proj0", "row", 0, 2), ("gate0", "row", 0, 4), ("gate0", "row", 1, 4), ("pool_w", "pool", 0, 2)]
    return out


def expert_chunks():
    groups = EF // COLS
    out = []
    for j in range(groups + 1):
        if j < groups:
            out += [("moe_wg", j), ("moe_wu", j)]
        if j >= 1:
            out.append(("moe_wd", j - 1))
    return out


DENSE = dense_chunks()
EXPERT = expert_chunks()
TAIL_GATE = (2, 4, 2)
RAW = (1, 2, 4, 5)
SCALED = (0, 3)
EARLY = 16
DIAGS = 6
ND, NX = len(DENSE), len(EXPERT)
GROUPS = EF // COLS
XP = 4 * NX
ITERS = 2 * NE
FIRST = [sum(c[3] for c in DENSE[:n]) for n in range(ND + 1)]
PB = FIRST[ND]
PT = PB + ITERS * XP
assert NX % RING == 0 and XP % AHEAD == 0


def slot_of(n):
    return n if n < FREE_AFTER else n - FREE_AFTER if n < 2 * FREE_AFTER else (n - FREE_AFTER) % RING


def fills_of(n):
    return sum(slot_of(m) == slot_of(n) for m in range(n + 1))


def last_piece_before(n):
    before = [m for m in range(n) if slot_of(m) == slot_of(n)]
    return FIRST[before[-1] + 1] if before else None


XSLOT = [slot_of(ND + i) for i in range(NX)]
XFILL = [sum(slot_of(m) == XSLOT[i] for m in range(ND)) + 1 + sum(XSLOT[q] == XSLOT[i] for q in range(i))
         for i in range(NX)]
PER = NX // RING


def kernel_program(nc, a, out):
    def sb(name, shape, dt=F32):
        return nc.alloc_sbuf_tensor(name, shape, dt)

    def sem(name):
        return nc.alloc_semaphore(name)

    ring = sb("ring", [P, RING, CHUNK])
    hi_ring = sb("hi_ring", [P, AHEAD, PIECE], F32R)
    lo_ring = sb("lo_ring", [P, AHEAD, PIECE], F32R)
    xT_hi = sb("xT_hi", [P, KT, SEQ], F32R)
    xT_lo = sb("xT_lo", [P, KT, SEQ], F32R)
    mT_hi = sb("mT_hi", [P, KT, SEQ], F32R)
    mT_lo = sb("mT_lo", [P, KT, SEQ], F32R)
    h = sb("h", [P, T, D])
    tok = sb("tok", [P, T, D])
    misc = sb("misc", [P, 2304])
    cst = sb("cst", [P, C_END])
    vec = sb("vec", [P, V_END])
    gains = vec[:, V_GAINS:V_CONV_W].rearrange("p (i k) -> p i k", k=KT)
    conv_w = vec[:, V_CONV_W:V_CONV_B].rearrange("p (c w) -> p c w", c=CT)
    conv_b, ln_g, ln_b = vec[:, V_CONV_B:V_LN_G], vec[:, V_LN_G:V_LN_B], vec[:, V_LN_B:V_ROUTER]
    rw = vec[:, V_ROUTER:V_END].rearrange("p (k e) -> p k e", k=KT)
    ss = sb("ss", [P, 6, T])
    std = sb("std", [P, 6, T])
    rstd = sb("rstd", [P, 6, T])
    eps = sb("eps", [P, 1])
    s_small = sb("s_small", [P, 64])
    rw_hi = sb("rw_hi", [P, KT, NE], F32R)
    rw_lo = sb("rw_lo", [P, KT, NE], F32R)
    rt = sb("rt", [P, 160])
    idx8 = sb("idx8", [P, T, 8], U32)
    slot_tab = sb("slot_tab", [P, T, ITERS + 1])
    gate_tab = sb("gate_tab", [P, T, ITERS + 1])
    most = sb("most", [P, 1], I32)

    ident = cst[:, C_IDENT:C_IOTA]
    iota = cst[:, C_IOTA:C_MEAN]
    mean_mat = cst[:, C_MEAN:C_ONES]
    ones_mat = cst[:, C_ONES:C_BEFORE]
    before_mat = cst[:, C_BEFORE:C_COS]
    cos = cst[:, C_COS:C_SIN].rearrange("p (t f) -> p t f", t=T)
    sin = cst[:, C_SIN:C_END].rearrange("p (t f) -> p t f", t=T)

    scratch = ring[:, FREE_AFTER:RING, :].rearrange("p s n -> p (s n)")
    taken = [0]

    def carve(n):
        taken[0] += n
        assert taken[0] <= (RING - FREE_AFTER) * CHUNK
        return scratch[:, taken[0] - n:taken[0]]

    qk = carve(T * QK).rearrange("p (t n) -> p t n", t=T)
    qk_gain = carve(QK)
    rope4 = carve(T * 4 * QK // 2)
    rot = carve(T * 768).rearrange("p (t n) -> p t n", t=T)
    v_sb = carve(T * P).rearrange("p (t n) -> p t n", t=T)
    diag_early = scratch[:, taken[0]:taken[0] + 12 * P].rearrange("p (n c) -> p n c", c=P)
    qT = carve(4 * SEQ).rearrange("p (c n) -> p c n", c=4)
    kT = carve(2 * SEQ).rearrange("p (c n) -> p c n", c=2)
    prob = carve(2 * 512).rearrange("p (b t n) -> p b t n", b=2, t=T)
    probT = carve(2 * 512).rearrange("p (b k n) -> p b k n", b=2, k=T)
    upad = carve(CT * (SEQ + 2 * PAD)).rearrange("p (c n) -> p c n", c=CT)
    conv = carve(CT * SEQ).rearrange("p (c n) -> p c n", c=CT)
    sq = rope4[:, 0:T * QK].rearrange("p (t n) -> p t n", t=T)
    rope = rope4.rearrange("p (t q n f) -> p t q n f", t=T, q=4, f=HALF)
    sig_b = scratch[:, taken[0] - CT * SEQ - CT * (SEQ + 2 * PAD) - 1024:
                    taken[0] - CT * SEQ - CT * (SEQ + 2 * PAD)].rearrange("p (c n) -> p c n", c=CT)
    ln_sq = rope4[:, 0:CT * SEQ].rearrange("p (c n) -> p c n", c=CT)
    ln_out = rope4[:, CT * SEQ:2 * CT * SEQ].rearrange("p (c n) -> p c n", c=CT)
    diag_late = rot.rearrange("p t (n c) -> p (t n) c", c=P)

    def diag_of(c, k):
        return (diag_early if k < EARLY else diag_late)[:, (c - 2) * DIAGS + k % DIAGS, :]

    def diag_used(k):
        return k - DIAGS + 1 if k < EARLY or k >= EARLY + DIAGS else 0

    ln_std = prob[:, 0, 0, :]
    ln_rstd = prob[:, 0, 1, :]

    ffn_act = misc[:, 0:1024].rearrange("p (f n) -> p f n", f=4)
    factor_diag = misc[:, 1536:1792].rearrange("p (t n) -> p t n", t=T)
    factor_row = misc[:, 1792:2048]
    p_tok = [misc[:, at:at + 512].rearrange("p (t n) -> p t n", t=T) for at in (1024, 0)]
    pT_hi, pT_lo = [mT_hi[:, 0:2, :], mT_hi[:, 4:6, :]], [mT_lo[:, 0:2, :], mT_lo[:, 4:6, :]]
    bands = misc[:, 0:2048].rearrange("p (t g n) -> p t g n", t=T, g=4)
    scale_row = misc[:, 0:D]
    x_act = misc[:, 0:512]
    y_sb = misc[:, 512:1536]
    pick = misc[:, 1536:1792].rearrange("p (t n) -> p t n", t=T)
    pick_gated = misc[:, 1792:2048].rearrange("p (t n) -> p t n", t=T)
    spread = misc[:, 2048:2304]

    Y = nc.alloc_psum_tensor("Y", [P, 4, 512], F32)
    G = nc.alloc_psum_tensor("G", [P, 4, 512], F32)
    G8 = G[:, :, :].rearrange("p b (k n) -> p (b k) n", k=2)
    Y8 = Y[:, :, :].rearrange("p b (k n) -> p (b k) n", k=2)

    xg_hi, xg_lo = xT_hi[:, :, 0:P], xT_lo[:, :, 0:P]
    aT_hi = mT_hi[:, :, 0:P].rearrange("p (b f) n -> p b f n", b=2)
    aT_lo = mT_lo[:, :, 0:P].rearrange("p (b f) n -> p b f n", b=2)

    slot_in = [sem(f"slot_in{i}") for i in range(RING)]
    hi_done, lo_done, pe_piece = sem("hi_done"), sem("lo_done"), sem("pe_piece")
    small_in, p_in, band_in, scale_in = sem("small_in"), sem("p_in"), sem("band_in"), sem("scale_in")
    x_in = [sem(f"x_in{t}") for t in range(T)]
    eps_set = sem("eps_set")
    h_ready = sem("h_ready")
    warm = sem("warm")
    ss_done, std_done, rstd_done, tok_done = sem("ss_done"), sem("std_done"), sem("rstd_done"), sem("tok_done")
    tr_done, nhi_done, nlo_done = sem("tr_done"), sem("nhi_done"), sem("nlo_done")
    qkv_copied, qk_ss, qk_std, qk_rot = sem("qkv_copied"), sem("qk_ss"), sem("qk_std"), sem("qk_rot")
    qk_tr, qk_tr_copied = sem("qk_tr"), sem("qk_tr_copied")
    sig_done, glu_done, pads_set = sem("sig_done"), sem("glu_done"), sem("pads_set")
    conv_v, diag_a, diag_p, conv_mm_a, conv_mm_p, conv_out = sem("conv_v"), sem("diag_a"), sem("diag_p"), sem("conv_mm_a"), sem("conv_mm_p"), sem("conv_out")
    sc_done, neg_done, exp_done, nrm_done = sem("sc_done"), sem("neg_done"), sem("exp_done"), sem("nrm_done")
    pt_done, pt_copied, o_done, o_hi, o_lo = sem("pt_done"), sem("pt_copied"), sem("o_done"), sem("o_hi"), sem("o_lo")
    mean_mm, cent_done, sq_done, var_mm = sem("mean_mm"), sem("cent_done"), sem("sq_done"), sem("var_mm")
    lnstd_done, lnn_done, silu_c, c_hi, c_lo = sem("lnstd_done"), sem("lnn_done"), sem("silu_c"), sem("c_hi"), sem("c_lo")
    factor_d, factor_mm, factor_out, fscaled = sem("factor_d"), sem("factor_mm"), sem("factor_out"), sem("fscaled")
    fsilu, fmul, fhi, flo = sem("fsilu"), sem("fmul"), sem("fhi"), sem("flo")
    ptok_tr, p_hi, p_lo, sig_gate, gated = sem("ptok_tr"), sem("p_hi"), sem("p_lo"), sem("sig_gate"), sem("gated")
    scaled = sem("scaled")
    rw_hi_done, rw_lo_done, logit_mm, route_v, gap_exp = sem("rw_hi_done"), sem("rw_lo_done"), sem("logit_mm"), sem("route_v"), sem("gap_exp")
    mask_done, rank_mm, tabs_done = sem("mask_done"), sem("rank_mm"), sem("tabs_done")
    pick_done = sem("pick_done")
    gath_mm, xhi_done, xlo_done = sem("gath_mm"), sem("xhi_done"), sem("xlo_done")
    xsilu, xmul = sem("xsilu"), sem("xmul")
    at_mm, at_hi, at_lo = sem("at_mm"), sem("at_hi"), sem("at_lo")
    y_out, sp_mm, sp_out, scat_mm, scat_add = sem("y_out"), sem("sp_mm"), sem("sp_out"), sem("scat_mm"), sem("scat_add")
    last_mm, tail_in = sem("last_mm"), sem("tail_in")
    chain_v, chain_a, chain_p = sem("chain_v"), sem("chain_a"), sem("chain_p")
    stored = sem("stored")

    w_in = a["w_in"][0].rearrange("(k p) n -> p k n", p=P)

    def dense_source(name, kind, j, pieces):
        if name == "w_in":
            c0, n = {"col": (0, 512), "kv": (512, 256), "a": (768, 512), "b": (1280, 512)}[kind]
            return w_in[:, :, c0:c0 + n], KT, n
        if kind == "col":
            n = COLS * pieces // 4
            return a[name][0].rearrange("(k p) n -> p k n", p=P)[:, :, j * COLS:j * COLS + n], KT, n
        if kind == "pool":
            return a["pool_w"][0].rearrange("g (k p) n -> p (g k) n", p=P), 8, 256
        m = {"w_out": lambda: a["w_out"][0], "ffn_wd": lambda: a["ffn_wd"][0],
             "gate0": lambda: a["ple_gate_w"][0], "proj0": lambda: a["ple_proj"][0]}[name]()
        rows = m[j * ROWS * P:(j * ROWS + pieces) * P, :]
        return rows.rearrange("(r p) n -> p r n", p=P), pieces, D

    def moe_source(name, j, e):
        w = a[name][0]
        if name == "moe_wd":
            return w[bass.ds(e, 1), j * COLS:(j + 1) * COLS, :].rearrange("o (r p) n -> p (o r) n", p=P), ROWS, D
        return w[bass.ds(e, 1), :, j * COLS:(j + 1) * COLS].rearrange("o (k p) n -> p (o k) n", p=P), KT, COLS

    def piece_at(buf, n, width):
        return buf[:, n % AHEAD, :].rearrange("p (r n) -> p r n", n=width)

    block = nc.Block()
    block.__enter__()

    @block.sync
    def _(sp):
        def load(n_slot, src, rows, width):
            dst = ring[:, n_slot, 0:rows * width].rearrange("p (r n) -> p r n", r=rows)
            sp.dma_start(dst, src).then_inc(slot_in[n_slot], 16)

        for t in range(T):
            sp.dma_start(h[:, t, :], a["x"][0, t * P:(t + 1) * P, :]).then_inc(x_in[t], 16)
        for n, chunk in enumerate(DENSE):
            if last_piece_before(n) is not None:
                sp.wait_ge(lo_done, last_piece_before(n))
            if n == 2 * FREE_AFTER:
                sp.wait_ge(c_lo, 4)
                sp.wait_ge(o_lo, 4)
            load(slot_of(n), *dense_source(*chunk))

        def expert_loads(first, last, base):
            with sp.Fori(first, last) as it:
                for i, (name, j) in enumerate(EXPERT):
                    before = PB + 4 * (i - RING + 1) if i >= RING else FIRST[ND - RING + i + 1]
                    sp.wait_ge(lo_done, it * XP + before)
                    load(XSLOT[i], *moe_source(name, j, it - base))

        def tail_load(m):
            k0 = sum(TAIL_GATE[:m])
            off = 2 * PIECE if m == 0 else 0
            dst = ring[:, XSLOT[m], off:off + TAIL_GATE[m] * PIECE].rearrange("p (r n) -> p r n", n=D)
            ins = sp.dma_start(dst, a["ple_gate_w"][1, k0 * P:(k0 + TAIL_GATE[m]) * P, :].rearrange("(r p) n -> p r n", p=P))
            if m:
                ins.then_inc(slot_in[XSLOT[m]], 16)
                return
            ins.then_inc(tail_in, 16)
            sp.wait_ge(tail_in, 16)
            load(XSLOT[0], a["ple_proj"][1].rearrange("(r p) n -> p r n", p=P), 2, D)

        expert_loads(0, NE, 0)
        sp.wait_ge(tabs_done, 1)
        n_most = sp.value_load(most[0:1, 0:1])
        with sp.If(n_most > P):
            expert_loads(NE, ITERS, NE)
            sp.wait_ge(lo_done, PT + 4 * (1 - RING))
            tail_load(0)
        with sp.Else():
            sp.wait_ge(lo_done, PB + NE * XP + 4 * (1 - RING))
            tail_load(0)
            for s in range(RING):
                i0 = XSLOT.index(s)
                sp.wait_ge(slot_in[s], 16 * (XFILL[i0] - 1 + PER * NE + (s == XSLOT[0])))
                sp.sem_inc(slot_in[s], 16 * PER * NE)
            sp.nop()
        for m in (1, 2):
            sp.wait_ge(lo_done, PT + 4 * (m - RING + 1))
            tail_load(m)
        for t in range(T):
            sp.wait_ge(gated, 1 + t)
            sp.dma_start(out[0].rearrange("(t p) d -> p t d", p=P)[:, t, :], h[:, t, :]).then_inc(stored, 16)
        sp.wait_ge(stored, 16 * T)

    @block.scalar
    def _(act):
        small = [(cst[:, :], a["consts"]), (vec[:, :], a["vectors"]),
                 (qk_gain, a["qk_gain"].broadcast_to([P, QK]))]
        for dst, src in small:
            act.dma_start(dst, src).then_inc(small_in, 16)
        n_small = 16 * 3

        def hi(n, chunk_sem=None, value=None, where=None):
            if chunk_sem is not None:
                act.wait_ge(chunk_sem, value)
            act.activation(hi_ring[:, n % AHEAD, :], where, ACT.Copy).then_inc(hi_done, 1)

        did = [0]

        def hi_upto(last):
            while did[0] <= min(last, PB - 1):
                n = did[0]
                c = max(m for m in range(ND) if FIRST[m] <= n)
                s = slot_of(c)
                if n >= AHEAD:
                    act.wait_ge(pe_piece, n - AHEAD + 1)
                off = (n - FIRST[c]) * PIECE
                hi(n, slot_in[s], 16 * fills_of(c), ring[:, s, off:off + PIECE])
                did[0] += 1
            for q in range(max(did[0] - PB, 0), last - PB + 1):
                act.wait_ge(pe_piece, PB + q - AHEAD + 1)
                hi(PB + q, slot_in[XSLOT[0]], 16 * XFILL[0], ring[:, XSLOT[0], q * PIECE:(q + 1) * PIECE])
                did[0] += 1

        def norm(i):
            act.activation(std[:, i, 0:1], eps[:, 0:1], ACT.Sqrt).then_inc(warm, 1)
            act.wait_ge(warm, i + 1)
            for t in range(T):
                act.wait_ge(h_ready, T * i + t + 1) if i else act.wait_ge(x_in[t], 16)
                act.activation(tok[:, t, :], h[:, t, :], ACT.Square, accum_out=ss[:, i, t:t + 1]).then_inc(ss_done, 1)
            act.wait_ge(ss_done, T * (i + 1))
            act.activation(std[:, i, :], ss[:, i, :], ACT.Sqrt, bias=eps[:, 0:1], scale=1.0 / D).then_inc(std_done, 1)

        def norm_hi(i, bank=G8):
            for k in range(KT):
                act.wait_ge(tr_done, KT * i + (k | 1) + 1)
                act.activation(xT_hi[:, k, :], bank[:, k, :], ACT.Copy, scale=gains[:, i, k:k + 1]).then_inc(nhi_done, 1)

        act.wait_ge(eps_set, 1)
        norm(0)
        hi_upto(AHEAD - 1)
        act.wait_ge(small_in, n_small)
        norm_hi(0)
        hi_upto(7 + AHEAD)
        act.wait_ge(pe_piece, 8)
        act.activation(sig_b, G8[:, 4:8, :], ACT.Sigmoid).then_inc(sig_done, 1)

        def diagonals(first, last):
            for k in range(first, min(last, CONV_W)):
                if diag_used(k) > 0:
                    act.wait_ge(conv_mm_a, diag_used(k))
                act.activation(diag_of(3, k), ident, ACT.Copy, scale=conv_w[:, 3, k:k + 1]).then_inc(diag_a, 1)

        diagonals(0, DIAGS)
        hi_upto(11 + AHEAD)
        act.wait_ge(pe_piece, 12)
        act.activation(qk[:, :, 0:512], Y[:, 0:2, :], ACT.Copy).then_inc(qkv_copied, 1)
        hi_upto(13 + AHEAD)
        act.wait_ge(pe_piece, 14)
        act.activation(qk[:, :, 512:QK], Y[:, 2:4, 0:128], ACT.Copy).then_inc(qkv_copied, 1)
        act.activation(v_sb[:, :, :], Y[:, 2:4, 128:256], ACT.Copy).then_inc(qkv_copied, 1)
        diagonals(DIAGS, DIAGS + 4)
        act.wait_ge(qk_ss, 1)
        act.activation(s_small[:, 20:40], s_small[:, 0:20], ACT.Sqrt, bias=eps[:, 0:1], scale=1.0 / HEAD_DIM).then_inc(qk_std, 1)
        diagonals(DIAGS + 4, EARLY)
        act.wait_ge(qk_tr, 1)
        act.activation(qT[:, :, :], Y[:, 0:2, :].rearrange("p b (k n) -> p (b k) n", k=2), ACT.Copy).then_inc(qk_tr_copied, 1)
        act.activation(kT[:, :, :], Y[:, 2, :].rearrange("p (k n) -> p k n", k=2), ACT.Copy).then_inc(qk_tr_copied, 1)

        for i in range(HEADS + 2):
            diagonals(EARLY + 2 * i, EARLY + 2 * i + 2)
            if i < HEADS:
                act.wait_ge(neg_done, i + 1)
                for t in range(T):
                    act.activation(prob[:, i % 2, t, :], Y[:, i % 2, t * SEQ:(t + 1) * SEQ], ACT.Exp,
                                   bias=s_small[:, 44 + 2 * (i % 2) + t:45 + 2 * (i % 2) + t], scale=HEAD_DIM ** -0.5,
                                   accum_out=s_small[:, 48 + 2 * (i % 2) + t:49 + 2 * (i % 2) + t]).then_inc(exp_done, 1)
            if 1 <= i <= HEADS:
                act.wait_ge(pt_done, i)
                act.activation(probT[:, (i - 1) % 2, :, :],
                               Y[:, 2 + (i - 1) % 2, :].rearrange("p (k n) -> p k n", k=2), ACT.Copy).then_inc(pt_copied, 1)
            if i >= 3 and i % 2 == 1:
                c = (i - 3) // 2
                act.wait_ge(o_done, c + 1)
                act.activation(mT_hi[:, c, :], G[:, c % 2, 0:SEQ], ACT.Copy).then_inc(o_hi, 1)
        for c, done in ((2, conv_mm_p), (3, conv_mm_a)):
            act.wait_ge(done, CONV_W)
            act.activation(conv[:, c, :], G[:, c, 0:SEQ], ACT.Identity, bias=conv_b[:, c:c + 1]).then_inc(conv_out, 1)
        act.wait_ge(cent_done, 1)
        act.activation(ln_sq, conv, ACT.Square).then_inc(sq_done, 1)
        hi_upto(14 + AHEAD)
        act.wait_ge(var_mm, 1)
        act.activation(ln_std, G[:, 1, 0:SEQ], ACT.Sqrt, bias=eps[:, 0:1]).then_inc(lnstd_done, 1)
        act.wait_ge(lnn_done, 1)
        for c in range(CT + 1):
            if c < CT:
                act.activation(ln_out[:, c, :], conv[:, c, :], ACT.Silu, bias=ln_b[:, c:c + 1], scale=ln_g[:, c:c + 1]).then_inc(silu_c, 1)
            if c:
                act.wait_ge(silu_c, c)
                act.activation(mT_hi[:, 3 + c, :], ln_out[:, c - 1, :], ACT.Copy).then_inc(c_hi, 1)
                hi_upto(13 + c + AHEAD)
        hi_upto(21 + AHEAD)
        norm_hi(1)
        norm(1)
        hi_upto(FIRST[7] - 1 + AHEAD)
        act.wait_ge(factor_mm, 1)
        act.activation(factor_row, Y[:, 0, 0:SEQ], ACT.Copy).then_inc(factor_out, 1)

        def p_high(i):
            act.wait_ge(ptok_tr, i + 1)
            act.activation(pT_hi[i], G8[:, 2:4, :], ACT.Copy).then_inc(p_hi, 1)

        last_group = max(c[2] for c in DENSE if c[0] == "ffn_wg")
        act.dma_start(p_tok[0], a["p"][0, 0].rearrange("(t p) n -> p t n", p=P)).then_inc(p_in, 16)
        for n in range(6, ND):
            name, _, j, pieces = DENSE[n]
            if not name.startswith("ffn"):
                continue
            if (name, j) == ("ffn_wd", last_group):
                p_high(0)
            hi_upto(FIRST[n + 1] - 1 + AHEAD)
            f = pieces if name != "ffn_wd" else 0
            if name == "ffn_wg":
                act.wait_ge(fscaled, j + 1)
                act.activation(ffn_act[:, 0:f, :], ffn_act[:, 0:f, :], ACT.Silu).then_inc(fsilu, 1)
            if name == "ffn_wu":
                act.wait_ge(fmul, j + 1)
                b = 4 * (j % 2)
                act.activation(mT_hi[:, b:b + f, :], ffn_act[:, 0:f, :], ACT.Copy).then_inc(fhi, 1)

        def gate(i, norm_i, gate_end):
            act.wait_ge(pe_piece, gate_end)
            act.wait_ge(rstd_done, norm_i + 1)
            for t in range(T):
                act.activation(tok[:, t, :], Y[:, 2 * t:2 * t + 2, :].rearrange("p b n -> p (b n)"), ACT.Sigmoid,
                               scale=rstd[:, norm_i, t:t + 1]).then_inc(sig_gate, 1)

        g0 = [n for n in range(ND) if DENSE[n][0] == "proj0"][0]
        norm_hi(2, Y8)
        hi_upto(FIRST[g0 + 1] - 1 + AHEAD)
        norm(2)
        hi_upto(FIRST[g0 + 3] - 1 + AHEAD)
        gate(0, 2, FIRST[g0 + 3])
        act.dma_start(bands, a["bands"].rearrange("p (t g n) -> p t g n", t=T, g=4)).then_inc(band_in, 16)
        norm(3)
        norm_hi(3)
        act.wait_ge(tr_done, 4 * KT)
        act.dma_start(scale_row, a["pool_scale"][0:1, :].broadcast_to([P, D])).then_inc(scale_in, 16)
        hi_upto(PB - 1 + AHEAD)
        act.activation(rw_hi[:, :, :], rw, ACT.Copy).then_inc(rw_hi_done, 1)
        norm_hi(4)
        norm(4)
        act.wait_ge(route_v, 1)
        act.activation(rt[:, 48:50], rt[:, 46:48], ACT.Exp).then_inc(gap_exp, 1)

        def gathered_hi(value):
            act.wait_ge(gath_mm, value)
            for k in range(KT):
                src = (G[:, 3, :], Y[:, 2, :])[k // 4][:, (k % 4) * P:(k % 4 + 1) * P]
                act.activation(xg_hi[:, k, :], src, ACT.Copy, scale=gains[:, 4, k:k + 1]).then_inc(xhi_done, 1)

        gathered_hi(1)

        def experts(first, last):
            with act.Fori(first, last) as it:
                for q in range(XP):
                    n = q + AHEAD
                    c, nxt = (n // 4) % NX, n // XP
                    act.wait_ge(pe_piece, it * XP + (PB + q + 1))
                    if n % 4 == 0:
                        act.wait_ge(slot_in[XSLOT[c]], it * (16 * PER) + 16 * (XFILL[c] + PER * nxt))
                    hi(PB + n, None, None, ring[:, XSLOT[c], (n % 4) * PIECE:(n % 4 + 1) * PIECE])
                    name, j = EXPERT[q // 4]
                    s = q % 4
                    if name == "moe_wg" and s == 3:
                        if j >= 1:
                            act.wait_ge(at_mm, it * GROUPS + j)
                            act.activation(aT_hi[:, (j - 1) % 2, :, :], G[:, 2, :].rearrange("p (f n) -> p f n", f=4),
                                           ACT.Copy).then_inc(at_hi, 1)
                        act.wait_ge(pe_piece, it * XP + (PB + q + 1))
                        act.activation(x_act, G[:, 0, :], ACT.Silu).then_inc(xsilu, 1)
                    if name == "moe_wu" and s == 3 and j == 3:
                        act.wait_ge(sp_mm, it + 1)
                        act.activation(spread, Y[:, 3, 0:SEQ], ACT.Copy).then_inc(sp_out, 1)
                    if name == "moe_wu" and s == 3 and j == GROUPS - 1:
                        gathered_hi(it + 2)
                    if name == "moe_wd" and s == 2 and j == GROUPS - 2:
                        act.wait_ge(at_mm, it * GROUPS + GROUPS)
                        act.activation(aT_hi[:, (GROUPS - 1) % 2, :, :], G[:, 2, :].rearrange("p (f n) -> p f n", f=4),
                                       ACT.Copy).then_inc(at_hi, 1)
                    if name == "moe_wd" and s == 3 and j == GROUPS - 1:
                        act.wait_ge(pe_piece, it * XP + (PB + q + 1))
                        act.activation(y_sb, Y[:, 0:2, :].rearrange("p b n -> p (b n)"), ACT.Copy).then_inc(y_out, 1)

        experts(0, NE)
        act.wait_ge(tabs_done, 1)
        n_most = act.value_load(most[0:1, 0:1])
        with act.If(n_most > P):
            experts(NE, ITERS)
        with act.Else():
            for s, base, per in ((hi_done, PB + AHEAD, XP), (y_out, 1, 1), (sp_out, 1, 1)):
                act.wait_ge(s, base + NE * per)
                act.sem_inc(s, NE * per)
            act.nop()

        tdid = [AHEAD]

        def tail_upto(last):
            while tdid[0] <= last:
                q = tdid[0]
                c = q // 4
                act.wait_ge(pe_piece, PT + q - AHEAD + 1)
                if q % 4 == 0:
                    act.wait_ge(slot_in[XSLOT[c]], 16 * (XFILL[c] + PER * ITERS))
                hi(PT + q, None, None, ring[:, XSLOT[c], (q % 4) * PIECE:(q % 4 + 1) * PIECE])
                tdid[0] += 1

        act.dma_start(p_tok[1], a["p"][1, 0].rearrange("(t p) n -> p t n", p=P)).then_inc(p_in, 16)
        p_high(1)
        tail_upto(5)
        norm_hi(5, Y8)
        norm(5)
        tail_upto(9)
        gate(1, 5, PT + 10)

    @block.vector
    def _(dve):
        chain = [0]

        def link(ins):
            chain[0] += 1
            ins.then_inc(chain_v, 1)
            dve.wait_ge(chain_v, chain[0])

        def lo(n, where):
            dve.tensor_tensor(lo_ring[:, n % AHEAD, :], where, hi_ring[:, n % AHEAD, :].bitcast(F32),
                              ALU.subtract).then_inc(lo_done, 1)

        did = [0]

        def lo_upto(last):
            while did[0] <= last:
                n = did[0]
                dve.wait_ge(hi_done, n + 1)
                if n < PB:
                    c = max(m for m in range(ND) if FIRST[m] <= n)
                    off = (n - FIRST[c]) * PIECE
                    lo(n, ring[:, slot_of(c), off:off + PIECE])
                else:
                    lo(n, ring[:, XSLOT[0], (n - PB) * PIECE:(n - PB + 1) * PIECE])
                did[0] += 1

        def factor(i):
            dve.wait_ge(std_done, i + 1)
            dve.reciprocal(rstd[:, i, :], std[:, i, :]).then_inc(rstd_done, 1)

        def norm(i):
            factor(i)
            dve.wait_ge(rstd_done, i + 1)
            for t in range(T):
                dve.tensor_scalar(tok[:, t, :], h[:, t, :], rstd[:, i, t:t + 1], None, ALU.mult).then_inc(tok_done, 1)

        def norm_lo(i, bank=G8):
            for k in range(KT):
                dve.wait_ge(nhi_done, KT * i + (k | 1) + 1)
                dve.scalar_tensor_tensor(out=xT_lo[:, k, :], in0=bank[:, k, :], scalar=gains[:, i, k:k + 1],
                                         in1=xT_hi[:, k, :].bitcast(F32), op0=ALU.mult, op1=ALU.subtract).then_inc(nlo_done, 1)

        def add_rows(i):
            for t in range(T):
                dve.tensor_tensor(h[:, t, :], h[:, t, :], Y[:, 2 * t:2 * t + 2, :].rearrange("p b n -> p (b n)"),
                                  ALU.add).then_inc(h_ready, 1)
            dve.wait_ge(h_ready, T * (i + 1))

        dve.memset(eps[:, :], EPS).then_inc(eps_set, 1)
        for t in range(T):
            dve.wait_ge(x_in[t], 16)
        dve.sem_inc(h_ready, T)
        norm(0)
        lo_upto(AHEAD - 1)
        norm_lo(0)
        lo_upto(7 + AHEAD)
        dve.wait_ge(pads_set, 1)
        dve.wait_ge(sig_done, 1)
        dve.tensor_tensor(upad[:, :, PAD:PAD + SEQ], G8[:, 0:4, :], sig_b, ALU.mult).then_inc(glu_done, 1)
        dve.wait_ge(glu_done, 1)

        taps = [(k, c) for k in range(CONV_W) for c in range(2)]

        def tap(n):
            k, c = taps[n]
            if k == 0:
                dve.tensor_scalar(conv[:, c, :], upad[:, c, 0:SEQ], conv_w[:, c, 0:1], conv_b[:, c:c + 1],
                                  ALU.mult, ALU.add).then_inc(conv_v, 1)
            else:
                dve.wait_ge(conv_v, n - 1)
                dve.scalar_tensor_tensor(out=conv[:, c, :], in0=upad[:, c, k:k + SEQ], scalar=conv_w[:, c, k:k + 1],
                                         in1=conv[:, c, :], op0=ALU.mult, op1=ALU.add).then_inc(conv_v, 1)

        nt = 0
        for n in range(8, 14):
            for _ in range(5):
                tap(nt)
                nt += 1
            lo_upto(n + AHEAD)
        dve.wait_ge(qkv_copied, 2)
        qkh = qk.rearrange("p t (n f) -> p (t n) f", f=HEAD_DIM)
        link(dve.tensor_tensor(sq, qk, qk, ALU.mult))
        dve.tensor_reduce(s_small[:, 0:20], sq.rearrange("p t (n f) -> p (t n) f", f=HEAD_DIM), AX.X, ALU.add).then_inc(qk_ss, 1)
        dve.wait_ge(qk_std, 1)
        link(dve.reciprocal(s_small[:, 0:20], s_small[:, 20:40]))
        link(dve.tensor_tensor(qkh, qkh, s_small[:, 0:20].unsqueeze(2).broadcast_to([P, 20, HEAD_DIM]), ALU.mult))
        for t in range(T):
            ins = dve.tensor_tensor(qk[:, t, :], qk[:, t, :], qk_gain, ALU.mult)
        link(ins)
        for t in range(T):
            x = qk[:, t, :].rearrange("p (n c f) -> p n c f", c=2, f=HALF)
            cb = cos[:, t, :].unsqueeze(1).broadcast_to([P, 10, HALF])
            sn = sin[:, t, :].unsqueeze(1).broadcast_to([P, 10, HALF])
            r = rope[:, t]
            dve.tensor_tensor(r[:, 0], x[:, :, 0, :], cb, ALU.mult)
            dve.tensor_tensor(r[:, 1], x[:, :, 1, :], sn, ALU.mult)
            dve.tensor_tensor(r[:, 2], x[:, :, 1, :], cb, ALU.mult)
            ins = dve.tensor_tensor(r[:, 3], x[:, :, 0, :], sn, ALU.mult)
        link(ins)
        for t in range(T):
            r = rope[:, t]
            q_out = rot[:, t, 0:512].rearrange("p (n c f) -> p n c f", c=2, f=HALF)
            k_out = rot[:, t, 512:768].rearrange("p (n u c f) -> p n u c f", u=2, c=2, f=HALF)
            for c, (m, op) in enumerate(((0, ALU.subtract), (2, ALU.add))):
                ins = dve.tensor_tensor(q_out[:, :, c, :], r[:, m, 0:8, :], r[:, m + 1, 0:8, :], op)
                for u in range(2):
                    ins = dve.tensor_tensor(k_out[:, :, u, c, :], r[:, m, 8:10, :], r[:, m + 1, 8:10, :], op)
        ins.then_inc(qk_rot, 1)
        for i in range(HEADS + 2):
            if i < HEADS:
                b = i % 2
                dve.wait_ge(sc_done, i + 1)
                link(dve.tensor_reduce(s_small[:, 40 + 2 * b:42 + 2 * b], Y[:, b, :].rearrange("p (t n) -> p t n", t=T), AX.X, ALU.max))
                dve.tensor_scalar(s_small[:, 44 + 2 * b:46 + 2 * b], s_small[:, 40 + 2 * b:42 + 2 * b], -HEAD_DIM ** -0.5,
                                  None, ALU.mult).then_inc(neg_done, 1)
            for _ in range(4):
                if nt < len(taps):
                    tap(nt)
                    nt += 1
            if i < HEADS:
                dve.wait_ge(exp_done, T * (i + 1))
                link(dve.reciprocal(s_small[:, 52 + 2 * b:54 + 2 * b], s_small[:, 48 + 2 * b:50 + 2 * b]))
                for t in range(T):
                    ins = dve.tensor_scalar(prob[:, b, t, :], prob[:, b, t, :], s_small[:, 52 + 2 * b + t:53 + 2 * b + t], None, ALU.mult)
                ins.then_inc(nrm_done, 1)
            if i >= 3 and i % 2 == 1:
                c = (i - 3) // 2
                dve.wait_ge(o_hi, c + 1)
                dve.tensor_tensor(mT_lo[:, c, :], G[:, c % 2, 0:SEQ], mT_hi[:, c, :].bitcast(F32), ALU.subtract).then_inc(o_lo, 1)
        while nt < len(taps):
            tap(nt)
            nt += 1
        dve.wait_ge(mean_mm, 1)
        dve.tensor_tensor(conv, conv, G[:, 0, 0:SEQ].unsqueeze(1).broadcast_to([P, CT, SEQ]), ALU.subtract).then_inc(cent_done, 1)
        lo_upto(14 + AHEAD)
        dve.wait_ge(lnstd_done, 1)
        link(dve.reciprocal(ln_rstd, ln_std))
        dve.tensor_tensor(conv, conv, ln_rstd.unsqueeze(1).broadcast_to([P, CT, SEQ]), ALU.mult).then_inc(lnn_done, 1)
        for c in range(CT):
            dve.wait_ge(c_hi, c + 1)
            dve.tensor_tensor(mT_lo[:, 4 + c, :], ln_out[:, c, :], mT_hi[:, 4 + c, :].bitcast(F32), ALU.subtract).then_inc(c_lo, 1)
            lo_upto(14 + c + AHEAD)
        lo_upto(21 + AHEAD)
        dve.wait_ge(pe_piece, 22)
        add_rows(1)
        norm_lo(1)
        factor(1)
        dve.wait_ge(rstd_done, 2)
        for t in range(T):
            dve.tensor_scalar(factor_diag[:, t, :], ident, rstd[:, 1, t:t + 1], None, ALU.mult).then_inc(factor_d, 1)

        def p_low(i):
            dve.wait_ge(p_hi, i + 1)
            dve.tensor_tensor(pT_lo[i], G8[:, 2:4, :], pT_hi[i].bitcast(F32), ALU.subtract).then_inc(p_lo, 1)

        last_group = max(c[2] for c in DENSE if c[0] == "ffn_wg")
        for n in range(6, ND):
            name, _, j, pieces = DENSE[n]
            if not name.startswith("ffn"):
                continue
            if (name, j) == ("ffn_wd", last_group):
                p_low(0)
            lo_upto(FIRST[n + 1] - 1 + AHEAD)
            if name == "ffn_wg":
                if j:
                    dve.wait_ge(flo, j)
                dve.wait_ge(factor_out, 1)
                dve.wait_ge(pe_piece, FIRST[n + 1])
                dve.tensor_tensor(ffn_act[:, 0:pieces, :], G8[:, 0:pieces, :],
                                  factor_row.unsqueeze(1).broadcast_to([P, pieces, SEQ]), ALU.mult).then_inc(fscaled, 1)
            if name == "ffn_wu":
                b = 4 * (j % 2)
                dve.wait_ge(pe_piece, FIRST[n + 1])
                dve.wait_ge(fsilu, j + 1)
                dve.tensor_tensor(ffn_act[:, 0:pieces, :], ffn_act[:, 0:pieces, :], G8[:, 4:4 + pieces, :], ALU.mult).then_inc(fmul, 1)
                dve.wait_ge(fhi, j + 1)
                dve.tensor_tensor(mT_lo[:, b:b + pieces, :], ffn_act[:, 0:pieces, :], mT_hi[:, b:b + pieces, :].bitcast(F32),
                                  ALU.subtract).then_inc(flo, 1)
        g0 = [n for n in range(ND) if DENSE[n][0] == "proj0"][0]
        dve.wait_ge(pe_piece, FIRST[g0])
        for t in range(T):
            dve.scalar_tensor_tensor(out=h[:, t, :], in0=Y[:, 2 * t:2 * t + 2, :].rearrange("p b n -> p (b n)"),
                                     scalar=rstd[:, 1, t:t + 1], in1=h[:, t, :], op0=ALU.mult, op1=ALU.add).then_inc(h_ready, 1)
        dve.wait_ge(h_ready, T * 3)

        def gate(i):
            for t in range(T):
                dve.wait_ge(sig_gate, T * i + t + 1)
                link(dve.tensor_tensor(tok[:, t, :], tok[:, t, :], G[:, 2 * t:2 * t + 2, :].rearrange("p b n -> p (b n)"), ALU.mult))
                ins = dve.tensor_tensor(h[:, t, :], h[:, t, :], tok[:, t, :], ALU.add)
                ins.then_inc(gated if i else h_ready, 1)

        norm_lo(2, Y8)
        lo_upto(FIRST[g0 + 1] - 1 + AHEAD)
        factor(2)
        lo_upto(FIRST[g0 + 3] - 1 + AHEAD)
        gate(0)
        dve.wait_ge(h_ready, T * 4)
        norm(3)
        norm_lo(3)
        lo_upto(PB - 1 + AHEAD)
        dve.wait_ge(rw_hi_done, 1)
        dve.tensor_tensor(rw_lo[:, :, :], rw, rw_hi[:, :, :].bitcast(F32), ALU.subtract).then_inc(rw_lo_done, 1)
        dve.wait_ge(pe_piece, PB)
        dve.wait_ge(scale_in, 16)
        for t in range(T):
            dve.tensor_tensor(tok[:, t, :], Y[:, 2 * t:2 * t + 2, :].rearrange("p b n -> p (b n)"), scale_row, ALU.mult).then_inc(scaled, 1)
        dve.wait_ge(scaled, T)
        for t in range(T):
            dve.tensor_tensor(h[:, t, :], h[:, t, :], tok[:, t, :], ALU.add).then_inc(h_ready, 1)
        norm_lo(4)
        factor(4)
        dve.wait_ge(rstd_done, 5)

        logit = rt[:, 0:16].rearrange("p (t e) -> p t e", t=T)
        best = rt[:, 16:32].rearrange("p (t e) -> p t e", t=T)
        idxf = rt[:, 32:36].rearrange("p (t e) -> p t e", t=T)
        gap, ex = rt[:, 46:48], rt[:, 48:50]
        p1, p2, one_more = rt[:, 50:52], rt[:, 52:54], rt[:, 54:56]
        hot1 = rt[:, 56:72].rearrange("p (t e) -> p t e", t=T)
        hot2 = rt[:, 72:88].rearrange("p (t e) -> p t e", t=T)
        mask = rt[:, 88:104].rearrange("p (t e) -> p t e", t=T)
        gate_a = rt[:, 104:120].rearrange("p (t e) -> p t e", t=T)
        rank1 = rt[:, 120:136].rearrange("p (t e) -> p t e", t=T)
        top_count = rt[:, 136:137]
        dve.wait_ge(logit_mm, 1)
        for t in range(T):
            ins = dve.tensor_scalar(logit[:, t, :], Y[:, 0, t * NE:(t + 1) * NE], rstd[:, 4, t:t + 1], None, ALU.mult)
        link(ins)
        for t in range(T):
            ins = dve.max(best[:, t, :], logit[:, t, :])
        link(ins)
        for t in range(T):
            ins = dve.max_index(idx8[:, t, :], best[:, t, :], logit[:, t, :])
        link(ins)
        link(dve.tensor_copy(idxf, idx8[:, :, 0:2]))
        dve.tensor_tensor(gap, best[:, :, 1], best[:, :, 0], ALU.subtract).then_inc(route_v, 1)
        for t in range(T):
            dve.tensor_scalar(hot1[:, t, :], iota[:, 0:NE], idxf[:, t, 0:1], None, ALU.is_equal)
            ins = dve.tensor_scalar(hot2[:, t, :], iota[:, 0:NE], idxf[:, t, 1:2], None, ALU.is_equal)
        link(ins)
        dve.tensor_tensor(mask, hot1, hot2, ALU.add).then_inc(mask_done, 1)
        dve.wait_ge(gap_exp, 1)
        link(dve.tensor_scalar(one_more, ex, 1.0, None, ALU.add))
        link(dve.reciprocal(p1, one_more))
        link(dve.tensor_tensor(p2, p1, ex, ALU.mult))
        for t in range(T):
            ins = dve.tensor_scalar(gate_a[:, t, :], hot1[:, t, :], p1[:, t:t + 1], None, ALU.mult)
        link(ins)
        for t in range(T):
            ins = dve.scalar_tensor_tensor(out=gate_a[:, t, :], in0=hot2[:, t, :], scalar=p2[:, t:t + 1], in1=gate_a[:, t, :],
                                           op0=ALU.mult, op1=ALU.add)
        link(ins)
        for s in range(2):
            dve.tensor_copy(gate_tab[:, :, s * NE:(s + 1) * NE], gate_a)
        dve.memset(gate_tab[:, :, ITERS:], 0.0)
        dve.memset(slot_tab[:, :, ITERS:], NOWHERE)
        dve.wait_ge(mask_done, 1)
        dve.wait_ge(rank_mm, 1)
        ranks = Y[:, 1, 0:16].rearrange("p (t e) -> p t e", t=T)
        link(dve.scalar_tensor_tensor(out=rank1, in0=ranks, scalar=-NOWHERE, in1=mask, op0=ALU.add, op1=ALU.mult))
        for s in range(2):
            dve.tensor_scalar(slot_tab[:, :, s * NE:(s + 1) * NE], rank1, NOWHERE - s * P, None, ALU.add)
        link(dve.tensor_reduce(top_count, Y[:, 2, 0:8], AX.X, ALU.max))
        link(dve.tensor_copy(most[:, :], top_count))
        dve.sem_inc(tabs_done, 1)

        def gathered_lo(value):
            for k in range(KT):
                dve.wait_ge(xhi_done, value + (k | 3) + 1)
                src = (G[:, 3, :], Y[:, 2, :])[k // 4][:, (k % 4) * P:(k % 4 + 1) * P]
                dve.scalar_tensor_tensor(out=xg_lo[:, k, :], in0=src, scalar=gains[:, 4, k:k + 1],
                                         in1=xg_hi[:, k, :].bitcast(F32), op0=ALU.mult, op1=ALU.subtract).then_inc(xlo_done, 1)

        def picks(it):
            for t in range(T):
                slot = slot_tab[:, t, bass.ds(it, 1)]
                dve.tensor_scalar(pick[:, t, :], iota, slot, rstd[:, 4, t:t + 1], ALU.is_equal, ALU.mult).then_inc(pick_done, 1)
                dve.tensor_scalar(pick_gated[:, t, :], iota, slot, gate_tab[:, t, bass.ds(it, 1)], ALU.is_equal, ALU.mult).then_inc(pick_done, 1)

        picks(0)
        gathered_lo(0)

        def experts(first, last):
            with dve.Fori(first, last) as it:
                for q in range(XP):
                    n = q + AHEAD
                    c = (n // 4) % NX
                    dve.wait_ge(hi_done, it * XP + (PB + n + 1))
                    lo(PB + n, ring[:, XSLOT[c], (n % 4) * PIECE:(n % 4 + 1) * PIECE])
                    name, j = EXPERT[q // 4]
                    s = q % 4

                    def at_low(j):
                        dve.wait_ge(at_hi, it * GROUPS + (j + 1))
                        dve.tensor_tensor(aT_lo[:, j % 2, :, :], G[:, 2, :].rearrange("p (f n) -> p f n", f=4),
                                          aT_hi[:, j % 2, :, :].bitcast(F32), ALU.subtract).then_inc(at_lo, 1)

                    if name == "moe_wg" and s == 3:
                        if j >= 1:
                            at_low(j - 1)
                        else:
                            dve.wait_ge(scat_mm, it + 1)
                            dve.wait_ge(scat_add, it * 4 + 1)
                            for u, src in enumerate((G[:, 3, :], Y[:, 2, :], Y[:, 3, :], G[:, 2, :])):
                                acc = tok[:, u // 2, (u % 2) * 512:(u % 2 + 1) * 512]
                                dve.tensor_tensor(acc, acc, src, ALU.add).then_inc(scat_add, 1)
                    if name == "moe_wu" and s == 0 and j == 5:
                        dve.wait_ge(sp_mm, it + 1)
                        picks(it + 1)
                    if name == "moe_wu" and s == 3:
                        dve.wait_ge(pe_piece, it * XP + (PB + q + 1))
                        dve.wait_ge(xsilu, it * GROUPS + (j + 1))
                        dve.tensor_tensor(x_act, x_act, G[:, 1, :], ALU.mult).then_inc(xmul, 1)
                        if j == GROUPS - 1:
                            gathered_lo(it * KT + KT)
                    if name == "moe_wd" and s == 2 and j == GROUPS - 2:
                        at_low(GROUPS - 1)

        experts(0, NE)
        dve.wait_ge(tabs_done, 1)
        n_most = dve.value_load(most[0:1, 0:1])
        with dve.If(n_most > P):
            experts(NE, ITERS)
        with dve.Else():
            for s, base, per in ((lo_done, PB + AHEAD, XP), (xlo_done, KT, KT), (scat_add, 1, 4)):
                dve.wait_ge(s, base + NE * per)
                dve.sem_inc(s, NE * per)
            dve.nop()
        dve.wait_ge(scat_add, 4 * ITERS + 1)
        for t in range(T):
            ins = dve.tensor_tensor(h[:, t, :], h[:, t, :], tok[:, t, :], ALU.add)
        link(ins)
        dve.wait_ge(last_mm, 1)
        add_rows(5)
        p_low(1)

        tdid = [AHEAD]

        def tail_upto(last):
            while tdid[0] <= last:
                q = tdid[0]
                dve.wait_ge(hi_done, PT + q + 1)
                lo(PT + q, ring[:, XSLOT[q // 4], (q % 4) * PIECE:(q % 4 + 1) * PIECE])
                tdid[0] += 1

        tail_upto(5)
        norm_lo(5, Y8)
        factor(5)
        tail_upto(9)
        gate(1)

    @block.gpsimd
    def _(pool):
        pool.memset(upad[:, :, 0:PAD], 0.0)
        pool.memset(upad[:, :, PAD + SEQ:], 0.0).then_inc(pads_set, 1)
        pool.wait_ge(small_in, 16 * 3)
        for k in range(CONV_W):
            if k == EARLY:
                pool.wait_ge(qk_tr, 1)
            if diag_used(k) > 0:
                pool.wait_ge(conv_mm_p, diag_used(k))
            pool.tensor_scalar(diag_of(2, k), ident, conv_w[:, 2, k:k + 1], None, ALU.mult).then_inc(diag_p, 1)

        pool.wait_ge(tabs_done, 1)
        pool.memset(y_sb, 0.0).then_inc(y_out, 1)
        pool.memset(spread, 0.0).then_inc(sp_out, 1)
        pool.memset(tok[:, :, :], 0.0).then_inc(scat_add, 1)

    @block.tensor
    def _(pe):
        def piece(n, last):
            last.then_inc(pe_piece, 1)

        def three(dst, s_hi, s_lo, m_hi, m_lo, start, stop):
            pe.matmul(dst, s_hi, m_hi, start=start, stop=False, skip_group_check=True)
            pe.matmul(dst, s_lo, m_hi, start=False, stop=False, skip_group_check=True)
            return pe.matmul(dst, s_hi, m_lo, start=False, stop=stop, skip_group_check=True)

        def norm(i, bank=G8):
            src = h if i in RAW else tok
            if bank is Y8:
                pe.wait_ge(h_ready, T * (i + 1))
            for t in range(T):
                if i in RAW:
                    pe.wait_ge(h_ready, T * i + t + 1)
                else:
                    pe.wait_ge(tok_done, T * SCALED.index(i) + t + 1)
                for k in range(KT):
                    ins = pe.transpose(bank[:, k, t * P:(t + 1) * P], src[:, t, k * P:(k + 1) * P], ident)
                    if t == T - 1:
                        ins.then_inc(tr_done, 1)

        def cols_tokens(n0, pieces, dst, width):
            per = PIECE // width
            for s in range(pieces):
                pe.wait_ge(lo_done, n0 + s + 1)
                w_hi, w_lo = piece_at(hi_ring, n0 + s, width), piece_at(lo_ring, n0 + s, width)
                for r in range(per):
                    k = s * per + r
                    for t in range(T):
                        ins = three(dst(t), xT_hi[:, k, t * P:(t + 1) * P], xT_lo[:, k, t * P:(t + 1) * P],
                                    w_hi[:, r, :], w_lo[:, r, :], k == 0, k == KT - 1)
                piece(n0 + s, ins)
            return ins

        def cols_channels(n0, pieces, bank0, width, i):
            per = PIECE // width
            tiles = width // P
            pe.wait_ge(nlo_done, KT * (i + 1))
            for s in range(pieces):
                pe.wait_ge(lo_done, n0 + s + 1)
                w_hi, w_lo = piece_at(hi_ring, n0 + s, width), piece_at(lo_ring, n0 + s, width)
                for r in range(per):
                    k = s * per + r
                    for f in range(tiles):
                        ins = three(G8[:, 2 * bank0 + f, :], w_hi[:, r, f * P:(f + 1) * P], w_lo[:, r, f * P:(f + 1) * P],
                                    xT_hi[:, k, :], xT_lo[:, k, :], k == 0 and f % 2 == 0, k == KT - 1)
                piece(n0 + s, ins)
            return ins

        def rows(n, s_hi, s_lo, bank, first, last):
            pe.wait_ge(lo_done, n + 1)
            w_hi, w_lo = hi_ring[:, n % AHEAD, :], lo_ring[:, n % AHEAD, :]
            for t in range(T):
                for c in range(2):
                    ins = three(bank[:, 2 * t + c, :], s_hi[:, t * P:(t + 1) * P], s_lo[:, t * P:(t + 1) * P],
                                w_hi[:, c * 512:(c + 1) * 512], w_lo[:, c * 512:(c + 1) * 512], first, last)
            piece(n, ins)
            return ins

        pe.wait_ge(small_in, 16 * 3)
        norm(0)
        cols_channels(0, 4, 0, 512, 0)
        cols_channels(4, 4, 2, 512, 0)
        cols_tokens(8, 4, lambda t: Y[:, t, :], 512)
        cols_tokens(12, 2, lambda t: Y[:, 2 + t, 0:256], 256)

        def conv_taps(first, last):
            for k in range(first, min(last, CONV_W)):
                for c, made, done in ((2, diag_p, conv_mm_p), (3, diag_a, conv_mm_a)):
                    pe.wait_ge(made, k + 1)
                    pe.matmul(G[:, c, 0:SEQ], diag_of(c, k), upad[:, c, k:k + SEQ],
                              start=(k == 0), stop=(k == CONV_W - 1)).then_inc(done, 1)

        pe.wait_ge(glu_done, 1)
        conv_taps(0, EARLY)
        pe.wait_ge(qk_rot, 1)
        pe.wait_ge(qkv_copied, 3)
        for c in range(6):
            for t in range(T):
                ins = pe.transpose(Y[:, c // 2, (c % 2) * SEQ + t * P:(c % 2) * SEQ + (t + 1) * P],
                                   rot[:, t, c * P:(c + 1) * P], ident)
        ins.then_inc(qk_tr, 1)
        pe.wait_ge(qk_tr_copied, 2)
        for i in range(HEADS + 2):
            if i < HEADS:
                if i >= 2:
                    pe.wait_ge(exp_done, T * (i - 1))
                lo_p = (i % 2) * HEAD_DIM
                for t in range(T):
                    ins = pe.matmul(Y[:, i % 2, t * SEQ:(t + 1) * SEQ], qT[lo_p:lo_p + HEAD_DIM, i // 2, t * P:(t + 1) * P],
                                    kT[lo_p:lo_p + HEAD_DIM, i // 4, :], start=True, stop=True)
                ins.then_inc(sc_done, 1)
            conv_taps(EARLY + 2 * i, EARLY + 2 * i + 2)
            if 1 <= i <= HEADS:
                hd = i - 1
                pe.wait_ge(nrm_done, hd + 1)
                if hd >= 2:
                    pe.wait_ge(pt_copied, hd - 1)
                for k in range(T):
                    for t in range(T):
                        ins = pe.transpose(Y[:, 2 + hd % 2, k * SEQ + t * P:k * SEQ + (t + 1) * P],
                                           prob[:, hd % 2, t, k * P:(k + 1) * P], ident)
                ins.then_inc(pt_done, 1)
            if i >= 2:
                hd = i - 2
                pe.wait_ge(pt_copied, hd + 1)
                if hd >= 4 and hd % 2 == 0:
                    pe.wait_ge(o_lo, hd // 2 - 1)
                lo_p = (hd % 2) * HEAD_DIM
                for k in range(T):
                    ins = pe.matmul(G[lo_p:lo_p + HEAD_DIM, (hd // 2) % 2, 0:SEQ],
                                    v_sb[:, k, (hd // 4) * HEAD_DIM:(hd // 4 + 1) * HEAD_DIM],
                                    probT[:, hd % 2, k, :], start=(k == 0), stop=(k == T - 1))
                if hd % 2:
                    ins.then_inc(o_done, 1)
        pe.wait_ge(o_lo, 4)
        pe.wait_ge(conv_v, CONV_W * 2)
        pe.wait_ge(conv_out, 2)
        for c in range(CT):
            ins = pe.matmul(G[:, 0, 0:SEQ], mean_mat, conv[:, c, :], start=(c == 0), stop=(c == CT - 1))
        ins.then_inc(mean_mm, 1)
        rows(14, mT_hi[:, 0, :], mT_lo[:, 0, :], Y, True, False)
        pe.wait_ge(sq_done, 1)
        for c in range(CT):
            ins = pe.matmul(G[:, 1, 0:SEQ], mean_mat, ln_sq[:, c, :], start=(c == 0), stop=(c == CT - 1))
        ins.then_inc(var_mm, 1)
        for e in range(1, 4):
            rows(14 + e, mT_hi[:, e, :], mT_lo[:, e, :], Y, False, False)
        for e in range(4, 8):
            pe.wait_ge(c_lo, e - 3)
            rows(14 + e, mT_hi[:, e, :], mT_lo[:, e, :], Y, False, e == 7)

        def p_transposes(i):
            pe.wait_ge(p_in, 16 * (i + 1))
            for k in range(2):
                for t in range(T):
                    ins = pe.transpose(G8[:, 2 + k, t * P:(t + 1) * P], p_tok[i][:, t, k * P:(k + 1) * P], ident)
            ins.then_inc(ptok_tr, 1)

        last_group = max(c[2] for c in DENSE if c[0] == "ffn_wg")
        norm(1)
        for n in range(6, ND):
            name, _, j, pieces = DENSE[n]
            if name == "ffn_wg":
                if j >= 1:
                    pe.wait_ge(fscaled, j)
                cols_channels(FIRST[n], pieces, 0, COLS * pieces // 4, 1)
                if j == 0:
                    pe.wait_ge(factor_d, T)
                    for t in range(T):
                        ins = pe.matmul(Y[:, 0, t * P:(t + 1) * P], ones_mat, factor_diag[:, t, :], start=True, stop=True)
                    ins.then_inc(factor_mm, 1)
            if name == "ffn_wu":
                if j >= 1:
                    pe.wait_ge(fmul, j)
                cols_channels(FIRST[n], pieces, 2, COLS * pieces // 4, 1)
            if name == "ffn_wd":
                if j == last_group:
                    p_transposes(0)
                pe.wait_ge(factor_out, 1)
                pe.wait_ge(flo, j + 1)
                for f in range(pieces):
                    b = 4 * (j % 2) + f
                    rows(FIRST[n] + f, mT_hi[:, b, :], mT_lo[:, b, :], Y, j == 0 and f == 0, j * COLS + (f + 1) * P == FFN)

        def ple(i, norm_i, first):
            pe.wait_ge(p_lo, i + 1)
            for k in range(2):
                rows(first + k, pT_hi[i][:, k, :], pT_lo[i][:, k, :], G, k == 0, k == 1)
            norm(norm_i, Y8)
            pe.wait_ge(nlo_done, KT * (norm_i + 1))
            for k in range(KT):
                rows(first + 2 + k, xT_hi[:, k, :], xT_lo[:, k, :], Y, k == 0, k == KT - 1)

        ple(0, 2, FIRST[[n for n in range(ND) if DENSE[n][0] == "proj0"][0]])

        pe.wait_ge(tok_done, T * 2)
        pe.wait_ge(band_in, 16)
        for k in range(KT):
            for t in range(T):
                ins = pe.matmul(G8[:, k, :], tok[:, t, k * P:(k + 1) * P], bands[:, t, k // 2, :], start=(t == 0), stop=(t == T - 1))
            ins.then_inc(tr_done, 1)
        for s in range(2):
            n = FIRST[ND - 1] + s
            pe.wait_ge(lo_done, n + 1)
            w_hi, w_lo = piece_at(hi_ring, n, 256), piece_at(lo_ring, n, 256)
            for r in range(4):
                g, k = 2 * s + r // 2, 4 * s + r
                pe.wait_ge(nlo_done, KT * 3 + k + 1)
                for t in range(T):
                    ins = three(Y[:, 2 * t + g // 2, (g % 2) * 256:(g % 2 + 1) * 256], xT_hi[:, k, t * P:(t + 1) * P],
                                xT_lo[:, k, t * P:(t + 1) * P], w_hi[:, r, :], w_lo[:, r, :], k % 4 == 0, k % 2 == 1)
            piece(n, ins)

        norm(4)
        pe.wait_ge(nlo_done, KT * 5)
        pe.wait_ge(rw_lo_done, 1)
        for t in range(T):
            for k in range(KT):
                ins = three(Y[:, 0, t * NE:(t + 1) * NE], xT_hi[:, k, t * P:(t + 1) * P], xT_lo[:, k, t * P:(t + 1) * P],
                            rw_hi[:, k, :], rw_lo[:, k, :], t == 0 and k == 0, k == KT - 1)
        ins.then_inc(logit_mm, 1)
        pe.wait_ge(mask_done, 1)
        mask = rt[:, 88:104].rearrange("p (t e) -> p t e", t=T)
        pe.matmul(Y[:, 1, 0:NE], before_mat, mask[:, 0, :], start=True, stop=True)
        pe.matmul(Y[:, 1, NE:2 * NE], before_mat, mask[:, 1, :], start=True, stop=False)
        pe.matmul(Y[:, 1, NE:2 * NE], ones_mat, mask[:, 0, :], start=False, stop=True)
        pe.matmul(Y[:, 2, 0:NE], ones_mat, mask[:, 0, :], start=True, stop=False)
        pe.matmul(Y[:, 2, 0:NE], ones_mat, mask[:, 1, :], start=False, stop=True).then_inc(rank_mm, 1)

        def gather():
            for k in range(KT):
                dst = (G[:, 3, :], Y[:, 2, :])[k // 4][:, (k % 4) * P:(k % 4 + 1) * P]
                for t in range(T):
                    ins = pe.matmul(dst, h[:, t, k * P:(k + 1) * P], pick[:, t, :], start=(t == 0), stop=(t == T - 1))
            ins.then_inc(gath_mm, 1)

        def scatter(banks):
            for u, dst in enumerate(banks):
                ins = pe.matmul(dst, spread[:, (u // 2) * P:(u // 2 + 1) * P], y_sb[:, (u % 2) * 512:(u % 2 + 1) * 512],
                                start=True, stop=True)
            return ins

        pe.wait_ge(pick_done, 4)
        pe.wait_ge(tabs_done, 1)
        gather()

        def experts(first, last):
            with pe.Fori(first, last) as it:
                def transposes(j):
                    pe.wait_ge(xmul, it * GROUPS + (j + 1))
                    if j:
                        pe.wait_ge(at_lo, it * GROUPS + j)
                    else:
                        pe.wait_ge(scat_add, it * 4 + 5)
                    for f in range(4):
                        ins = pe.transpose(G[:, 2, f * P:(f + 1) * P], x_act[:, f * P:(f + 1) * P], ident)
                    ins.then_inc(at_mm, 1)

                for i, (name, j) in enumerate(EXPERT):
                    if name == "moe_wd":
                        for f in range(4):
                            if f == 0:
                                pe.wait_ge(at_lo, it * GROUPS + (j + 1))
                            n = PB + 4 * i + f
                            pe.wait_ge(lo_done, it * XP + (n + 1))
                            for c in range(2):
                                ins = three(Y[:, c, :], aT_hi[:, j % 2, f, :], aT_lo[:, j % 2, f, :],
                                            hi_ring[:, n % AHEAD, c * 512:(c + 1) * 512], lo_ring[:, n % AHEAD, c * 512:(c + 1) * 512],
                                            j == 0 and f == 0, j == GROUPS - 1 and f == 3)
                            piece(n, ins)
                            if j == GROUPS - 2 and f == 2:
                                transposes(GROUPS - 1)
                        continue
                    bank, free = (0, xsilu) if name == "moe_wg" else (1, xmul)
                    if j:
                        pe.wait_ge(free, it * GROUPS + j)
                    if name == "moe_wg" and j == 0:
                        pe.wait_ge(xlo_done, it * KT + KT)
                    for s in range(4):
                        n = PB + 4 * i + s
                        pe.wait_ge(lo_done, it * XP + (n + 1))
                        w_hi, w_lo = piece_at(hi_ring, n, 512), piece_at(lo_ring, n, 512)
                        for r in range(2):
                            k = 2 * s + r
                            ins = three(G[:, bank, :], xg_hi[:, k, :], xg_lo[:, k, :], w_hi[:, r, :], w_lo[:, r, :],
                                        k == 0, k == KT - 1)
                        piece(n, ins)
                    if name == "moe_wg":
                        if j == 0:
                            pe.wait_ge(y_out, it + 1)
                            pe.wait_ge(sp_out, it + 1)
                            scatter((G[:, 3, :], Y[:, 2, :], Y[:, 3, :], G[:, 2, :])).then_inc(scat_mm, 1)
                        else:
                            transposes(j - 1)
                    elif j == 3:
                        pe.wait_ge(pick_done, it * 4 + 4)
                        pe.wait_ge(scat_add, it * 4 + 5)
                        for t in range(T):
                            ins = pe.transpose(Y[:, 3, t * P:(t + 1) * P], pick_gated[:, t, :], ident)
                        ins.then_inc(sp_mm, 1)
                    elif j == GROUPS - 1:
                        pe.wait_ge(pick_done, it * 4 + 8)
                        gather()

        experts(0, NE)
        n_most = pe.value_load(most[0:1, 0:1])
        with pe.If(n_most > P):
            experts(NE, ITERS)
        with pe.Else():
            pe.wait_ge(pe_piece, PB + NE * XP)
            pe.sem_inc(pe_piece, NE * XP)
            pe.nop()
        pe.wait_ge(xlo_done, ITERS * KT + KT)
        pe.wait_ge(y_out, ITERS + 1)
        pe.wait_ge(sp_out, ITERS + 1)
        pe.wait_ge(scat_add, 4 * ITERS + 1)
        scatter([Y[:, b, :] for b in range(4)]).then_inc(last_mm, 1)
        p_transposes(1)
        ple(1, 5, PT)

    block.__exit__(None, None, None)


def host_constants():
    c = np.zeros((P, C_END), np.float32)
    c[:, C_IDENT:C_IOTA] = np.eye(P)
    c[:, C_IOTA:C_MEAN] = np.arange(P)[None, :]
    c[:, C_MEAN:C_ONES] = 1.0 / CONV_CH
    c[:, C_ONES:C_BEFORE] = 1.0
    c[:, C_BEFORE:C_COS] = np.arange(P)[:, None] < np.arange(P)[None, :]
    pos = np.arange(SEQ)
    inv = (np.float32(10000.0) ** (-np.arange(0, HALF, 2, dtype=np.float32) / np.float32(HALF))).astype(np.float32)
    row, col = (pos // GRID_W).astype(np.float32), (pos % GRID_W).astype(np.float32)
    ang = np.concatenate([row[:, None] * inv, col[:, None] * inv], axis=-1).astype(np.float32)
    c[:, C_COS:C_SIN] = np.cos(ang).reshape(T, P, HALF).transpose(1, 0, 2).reshape(P, -1)
    c[:, C_SIN:C_END] = np.sin(ang).reshape(T, P, HALF).transpose(1, 0, 2).reshape(P, -1)
    bands = np.zeros((4, SEQ, SEQ), np.float32)
    for g, w in enumerate(POOL_WINDOWS):
        lo = np.clip(pos - w // 2, 0, SEQ - 1)
        hi = np.clip(pos + w - 1 - w // 2, 0, SEQ - 1)
        for t in range(SEQ):
            bands[g, lo[t]:hi[t] + 1, t] = 1.0 / (hi[t] - lo[t] + 1)
            bands[g, t, t] -= 1.0
    bands = bands.reshape(4, T, P, SEQ).transpose(2, 1, 0, 3).reshape(P, -1)
    return c, np.ascontiguousarray(bands)


def vectors(v):
    def along(x):
        return x.reshape(-1, P).T

    parts = [along(v[n][i]) for i in range(2) for n in ("norm_mix", "norm_ffn", "ple_norm")]
    parts.append(v["conv_w"][0].reshape(CONV_W, CT, P).transpose(2, 1, 0).reshape(P, -1))
    parts += [along(v[n][0]) for n in ("conv_b", "conv_ln_g", "conv_ln_b")]
    parts.append(v["router_w"][0].reshape(KT, P, NE).transpose(1, 0, 2).reshape(P, -1))
    return np.ascontiguousarray(np.concatenate(parts, axis=1))


_INS = ["x", "p", "w_in", "w_out", "ffn_wg", "ffn_wu", "ffn_wd", "pool_w", "pool_scale", "moe_wg", "moe_wu", "moe_wd",
        "ple_gate_w", "ple_proj"]


def kernel(**inputs):
    import concourse.bacc as _bacc
    from concourse.bass_utils import run_bass_kernel_spmd as _run

    nc = _bacc.Bacc("TRN2", target_bir_lowering=False, num_devices=1)
    consts, bands = host_constants()
    arrays = {f"in_{n}": np.ascontiguousarray(inputs[n]) for n in _INS}
    arrays["in_consts"], arrays["in_bands"] = consts, bands
    v = {n: np.asarray(inputs[n]) for n in inputs}
    arrays["in_vectors"] = vectors(v)
    arrays["in_qk_gain"] = np.concatenate([v["q_norm"][0]] * HEADS + [v["k_norm"][0]] * KV_HEADS)[None, :]
    a = {n[3:]: nc.dram_tensor(n, x.shape, mybir.dt.from_np(x.dtype), kind="ExternalInput").ap() for n, x in arrays.items()}
    out = nc.dram_tensor("out_0", (1, SEQ, D), F32, kind="ExternalOutput").ap()
    kernel_program(nc, a, out)
    r = _run(nc, [arrays], core_ids=[0])
    return r.results[0]["out_0"]
```

```python
import concourse.bass as bass
import numpy as np
from concourse import mybir

F32 = mybir.dt.float32
F32R = mybir.dt.float32r
I32 = mybir.dt.int32
U32 = mybir.dt.uint32
ALU = mybir.AluOpType
ACT = mybir.ActivationFunctionType
AX = mybir.AxisListType

P = 128
D = 1024
SEQ = 256
T = SEQ // P
KT = D // P
GRID_W = 64
HEADS, KV_HEADS, HEAD_DIM = 8, 2, 64
HALF = HEAD_DIM // 2
QK = (HEADS + KV_HEADS) * HEAD_DIM
CONV_CH, CONV_W = 512, 31
CT = CONV_CH // P
PAD = CONV_W // 2
POOL_WINDOWS = (2, 4, 8, 16)
FFN = 2816
NE, EF = 8, 3584
PLE = 256
EPS = 1e-6

COLS = 512
ROWS = 4
PIECE = 1024
CHUNK = 4 * PIECE
RING = 7
AHEAD = 4
FREE_AFTER = 4
NOWHERE = -1000.0

C_IDENT, C_IOTA, C_MEAN, C_ONES, C_BEFORE, C_COS, C_SIN, C_END = 0, 128, 256, 384, 512, 640, 704, 768

V_GAINS, V_CONV_W = 0, 6 * KT
V_CONV_B = V_CONV_W + CT * CONV_W
V_LN_G, V_LN_B, V_ROUTER = V_CONV_B + CT, V_CONV_B + 2 * CT, V_CONV_B + 3 * CT
V_END = V_ROUTER + KT * NE


def dense_chunks():
    out = [("w_in", "a", 0, 4), ("w_in", "b", 0, 4), ("w_in", "col", 0, 4), ("w_in", "kv", 0, 2),
           ("w_out", "row", 0, 4), ("w_out", "row", 1, 4)]
    groups = -(-FFN // COLS)
    for j in range(groups + 1):
        n = 4 if (j + 1) * COLS <= FFN else 2
        if j < groups:
            out += [("ffn_wg", "col", j, n), ("ffn_wu", "col", j, n)]
        if j >= 1:
            n = 4 if j * COLS <= FFN else 2
            out.append(("ffn_wd", "row", j - 1, n))
    out += [("proj0", "row", 0, 2), ("gate0", "row", 0, 4), ("gate0", "row", 1, 4), ("pool_w", "pool", 0, 2)]
    return out


def expert_chunks():
    groups = EF // COLS
    out = []
    for j in range(groups + 1):
        if j < groups:
            out += [("moe_wg", j), ("moe_wu", j)]
        if j >= 1:
            out.append(("moe_wd", j - 1))
    return out


DENSE = dense_chunks()
EXPERT = expert_chunks()
TAIL_GATE = (2, 4, 2)
RAW = (1, 2, 4, 5)
SCALED = (0, 3)
EARLY = 20
DIAGS = 6
ND, NX = len(DENSE), len(EXPERT)
GROUPS = EF // COLS
XP = 4 * NX
ITERS = 2 * NE
FIRST = [sum(c[3] for c in DENSE[:n]) for n in range(ND + 1)]
PB = FIRST[ND]
PT = PB + ITERS * XP
assert NX % RING == 0 and XP % AHEAD == 0


def slot_of(n):
    return n if n < FREE_AFTER else n - FREE_AFTER if n < 2 * FREE_AFTER else (n - FREE_AFTER) % RING


def fills_of(n):
    return sum(slot_of(m) == slot_of(n) for m in range(n + 1))


def last_piece_before(n):
    before = [m for m in range(n) if slot_of(m) == slot_of(n)]
    return FIRST[before[-1] + 1] if before else None


XSLOT = [slot_of(ND + i) for i in range(NX)]
XFILL = [sum(slot_of(m) == XSLOT[i] for m in range(ND)) + 1 + sum(XSLOT[q] == XSLOT[i] for q in range(i))
         for i in range(NX)]
PER = NX // RING


def kernel_program(nc, a, out):
    def sb(name, shape, dt=F32):
        return nc.alloc_sbuf_tensor(name, shape, dt)

    def sem(name):
        return nc.alloc_semaphore(name)

    ring = sb("ring", [P, RING, CHUNK])
    hi_ring = sb("hi_ring", [P, AHEAD, PIECE], F32R)
    lo_ring = sb("lo_ring", [P, AHEAD, PIECE], F32R)
    xT_hi = sb("xT_hi", [P, KT, SEQ], F32R)
    xT_lo = sb("xT_lo", [P, KT, SEQ], F32R)
    mT_hi = sb("mT_hi", [P, KT, SEQ], F32R)
    mT_lo = sb("mT_lo", [P, KT, SEQ], F32R)
    h = sb("h", [P, T, D])
    tok = sb("tok", [P, T, D])
    misc = sb("misc", [P, 2304])
    cst = sb("cst", [P, C_END])
    vec = sb("vec", [P, V_END])
    gains = vec[:, V_GAINS:V_CONV_W].rearrange("p (i k) -> p i k", k=KT)
    conv_w = vec[:, V_CONV_W:V_CONV_B].rearrange("p (c w) -> p c w", c=CT)
    conv_b, ln_g, ln_b = vec[:, V_CONV_B:V_LN_G], vec[:, V_LN_G:V_LN_B], vec[:, V_LN_B:V_ROUTER]
    rw = vec[:, V_ROUTER:V_END].rearrange("p (k e) -> p k e", k=KT)
    ss = sb("ss", [P, 6, T])
    std = sb("std", [P, 6, T])
    rstd = sb("rstd", [P, 6, T])
    eps = sb("eps", [P, 1])
    unused = sb("unused", [P, 2])
    s_small = sb("s_small", [P, 64])
    rw_hi = sb("rw_hi", [P, KT, NE], F32R)
    rw_lo = sb("rw_lo", [P, KT, NE], F32R)
    rt = sb("rt", [P, 160])
    idx8 = sb("idx8", [P, T, 8], U32)
    slot_tab = sb("slot_tab", [P, T, ITERS + 1])
    gate_tab = sb("gate_tab", [P, T, ITERS + 1])
    most = sb("most", [P, 1], I32)

    ident = cst[:, C_IDENT:C_IOTA]
    iota = cst[:, C_IOTA:C_MEAN]
    mean_mat = cst[:, C_MEAN:C_ONES]
    ones_mat = cst[:, C_ONES:C_BEFORE]
    before_mat = cst[:, C_BEFORE:C_COS]
    cos = cst[:, C_COS:C_SIN].rearrange("p (t f) -> p t f", t=T)
    sin = cst[:, C_SIN:C_END].rearrange("p (t f) -> p t f", t=T)

    scratch = ring[:, FREE_AFTER:RING, :].rearrange("p s n -> p (s n)")
    taken = [0]

    def carve(n):
        taken[0] += n
        assert taken[0] <= (RING - FREE_AFTER) * CHUNK
        return scratch[:, taken[0] - n:taken[0]]

    qk = carve(T * QK).rearrange("p (t n) -> p t n", t=T)
    qk_gain = carve(QK)
    rope4 = carve(T * 4 * QK // 2)
    rot = carve(T * 768).rearrange("p (t n) -> p t n", t=T)
    v_sb = carve(T * P).rearrange("p (t n) -> p t n", t=T)
    diag_early = scratch[:, taken[0]:taken[0] + 12 * P].rearrange("p (n c) -> p n c", c=P)
    qT = carve(4 * SEQ).rearrange("p (c n) -> p c n", c=4)
    kT = carve(2 * SEQ).rearrange("p (c n) -> p c n", c=2)
    prob = carve(2 * 512).rearrange("p (b t n) -> p b t n", b=2, t=T)
    probT = carve(2 * 512).rearrange("p (b k n) -> p b k n", b=2, k=T)
    upad = carve(CT * (SEQ + 2 * PAD)).rearrange("p (c n) -> p c n", c=CT)
    conv = carve(CT * SEQ).rearrange("p (c n) -> p c n", c=CT)
    sq = rope4[:, 0:T * QK].rearrange("p (t n) -> p t n", t=T)
    rope = rope4.rearrange("p (t q n f) -> p t q n f", t=T, q=4, f=HALF)
    sig_b = scratch[:, taken[0] - CT * SEQ - CT * (SEQ + 2 * PAD) - 1024:
                    taken[0] - CT * SEQ - CT * (SEQ + 2 * PAD)].rearrange("p (c n) -> p c n", c=CT)
    ln_sq = rope4[:, 0:CT * SEQ].rearrange("p (c n) -> p c n", c=CT)
    ln_out = rope4[:, CT * SEQ:2 * CT * SEQ].rearrange("p (c n) -> p c n", c=CT)
    diag_late = rot.rearrange("p t (n c) -> p (t n) c", c=P)

    def diag_of(c, k):
        return (diag_early if k < EARLY else diag_late)[:, (c - 2) * DIAGS + k % DIAGS, :]

    def diag_used(k):
        return k - DIAGS + 1 if k < EARLY or k >= EARLY + DIAGS else 0

    ln_std = prob[:, 0, 0, :]
    ln_rstd = prob[:, 0, 1, :]

    ffn_act = misc[:, 0:1024].rearrange("p (f n) -> p f n", f=4)
    factor_diag = misc[:, 1536:1792].rearrange("p (t n) -> p t n", t=T)
    factor_row = misc[:, 1792:2048]
    p_tok = [[misc[:, at:at + PLE] for at in ats] for ats in ((1024, 1280), (1536, 2048))]

    def p_views(mT):
        return [mT[:, 0:2, :].rearrange("p k (t n) -> p k t n", t=T),
                mT[:, :, P:SEQ].rearrange("p (k b) n -> p k b n", k=2)[:, :, 2:4, :]]

    pT_hi, pT_lo = p_views(mT_hi), p_views(mT_lo)
    bands = misc[:, 0:2048].rearrange("p (t g n) -> p t g n", t=T, g=4)
    scale_row = misc[:, 0:D]
    logit_row = misc[:, D:D + SEQ]
    x_act = misc[:, 0:512]
    y_sb = misc[:, 512:1536]
    pick = misc[:, 1536:1792].rearrange("p (t n) -> p t n", t=T)
    pick_gated = misc[:, 1792:2048].rearrange("p (t n) -> p t n", t=T)
    spread = misc[:, 2048:2304]

    Y = nc.alloc_psum_tensor("Y", [P, 4, 512], F32)
    G = nc.alloc_psum_tensor("G", [P, 4, 512], F32)
    G8 = G[:, :, :].rearrange("p b (k n) -> p (b k) n", k=2)
    Y8 = Y[:, :, :].rearrange("p b (k n) -> p (b k) n", k=2)
    p_bank = [G8[:, 2:4, :], G8[:, 6:8, :]]

    xg_hi, xg_lo = xT_hi[:, :, 0:P], xT_lo[:, :, 0:P]
    aT_hi = mT_hi[:, :, 0:P].rearrange("p (b f) n -> p b f n", b=2)
    aT_lo = mT_lo[:, :, 0:P].rearrange("p (b f) n -> p b f n", b=2)

    slot_in = [sem(f"slot_in{i}") for i in range(RING)]
    hi_done, lo_done, pe_piece = sem("hi_done"), sem("lo_done"), sem("pe_piece")
    small_in, p_in, band_in, scale_in = sem("small_in"), sem("p_in"), sem("band_in"), sem("scale_in")
    x_in = [sem(f"x_in{t}") for t in range(T)]
    eps_set = sem("eps_set")
    h_ready = sem("h_ready")
    warm = sem("warm")
    ss_done, std_done, rstd_done, tok_done = sem("ss_done"), sem("std_done"), sem("rstd_done"), sem("tok_done")
    tr_done, nhi_done, nlo_done = sem("tr_done"), sem("nhi_done"), sem("nlo_done")
    qkv_copied, qk_ss, qk_std, qk_rot = sem("qkv_copied"), sem("qk_ss"), sem("qk_std"), sem("qk_rot")
    qk_tr, qk_tr_copied = sem("qk_tr"), sem("qk_tr_copied")
    sig_done, glu_done, pads_set = sem("sig_done"), sem("glu_done"), sem("pads_set")
    conv_v, diag_a, diag_p, conv_mm_a, conv_mm_p, conv_out = sem("conv_v"), sem("diag_a"), sem("diag_p"), sem("conv_mm_a"), sem("conv_mm_p"), sem("conv_out")
    sc_done, neg_done, exp_done, nrm_done = sem("sc_done"), sem("neg_done"), sem("exp_done"), sem("nrm_done")
    pt_done, pt_copied, o_done, o_hi, o_lo = sem("pt_done"), sem("pt_copied"), sem("o_done"), sem("o_hi"), sem("o_lo")
    mean_mm, cent_done, sq_done, var_mm = sem("mean_mm"), sem("cent_done"), sem("sq_done"), sem("var_mm")
    lnstd_done, lnn_done, silu_c, c_hi, c_lo = sem("lnstd_done"), sem("lnn_done"), sem("silu_c"), sem("c_hi"), sem("c_lo")
    factor_d, factor_mm, factor_out, fscaled = sem("factor_d"), sem("factor_mm"), sem("factor_out"), sem("fscaled")
    fsilu, fmul, fhi, flo = sem("fsilu"), sem("fmul"), sem("fhi"), sem("flo")
    ptok_tr, p_hi, p_lo, sig_gate, gated = sem("ptok_tr"), sem("p_hi"), sem("p_lo"), sem("sig_gate"), sem("gated")
    scaled, pooled = sem("scaled"), sem("pooled")
    bank_done = sem("bank_done")
    rw_hi_done, rw_lo_done, logit_mm, route_v, gap_exp = sem("rw_hi_done"), sem("rw_lo_done"), sem("logit_mm"), sem("route_v"), sem("gap_exp")
    logit_out, logit_tr = sem("logit_out"), sem("logit_tr")
    mask_done, rank_mm, tabs_done = sem("mask_done"), sem("rank_mm"), sem("tabs_done")
    pick_done = sem("pick_done")
    gath_mm, xhi_done, xlo_done = sem("gath_mm"), sem("xhi_done"), sem("xlo_done")
    xsilu, xmul = sem("xsilu"), sem("xmul")
    at_mm, at_hi, at_lo = sem("at_mm"), sem("at_hi"), sem("at_lo")
    y_out, sp_mm, sp_out, scat_mm, scat_add = sem("y_out"), sem("sp_mm"), sem("sp_out"), sem("scat_mm"), sem("scat_add")
    last_mm, tail_in = sem("last_mm"), sem("tail_in")
    chain_v = sem("chain_v")
    stored = sem("stored")

    w_in = a["w_in"][0].rearrange("(k p) n -> p k n", p=P)

    def dense_source(name, kind, j, pieces):
        if name == "w_in":
            c0, n = {"col": (0, 512), "kv": (512, 256), "a": (768, 512), "b": (1280, 512)}[kind]
            return w_in[:, :, c0:c0 + n], KT, n
        if kind == "col":
            n = COLS * pieces // 4
            return a[name][0].rearrange("(k p) n -> p k n", p=P)[:, :, j * COLS:j * COLS + n], KT, n
        if kind == "pool":
            return a["pool_w"][0].rearrange("g (k p) n -> p (g k) n", p=P), 8, 256
        m = {"w_out": lambda: a["w_out"][0], "ffn_wd": lambda: a["ffn_wd"][0],
             "gate0": lambda: a["ple_gate_w"][0], "proj0": lambda: a["ple_proj"][0]}[name]()
        rows = m[j * ROWS * P:(j * ROWS + pieces) * P, :]
        return rows.rearrange("(r p) n -> p r n", p=P), pieces, D

    def moe_source(name, j, e):
        w = a[name][0]
        if name == "moe_wd":
            return w[bass.ds(e, 1), j * COLS:(j + 1) * COLS, :].rearrange("o (r p) n -> p (o r) n", p=P), ROWS, D
        return w[bass.ds(e, 1), :, j * COLS:(j + 1) * COLS].rearrange("o (k p) n -> p (o k) n", p=P), KT, COLS

    def piece_at(buf, n, width):
        return buf[:, n % AHEAD, :].rearrange("p (r n) -> p r n", n=width)

    block = nc.Block()
    block.__enter__()

    @block.sync
    def _(sp):
        def load(n_slot, src, rows, width):
            dst = ring[:, n_slot, 0:rows * width].rearrange("p (r n) -> p r n", r=rows)
            sp.dma_start(dst, src).then_inc(slot_in[n_slot], 16)

        for t in range(T):
            sp.dma_start(h[:, t, :], a["x"][0, t * P:(t + 1) * P, :]).then_inc(x_in[t], 16)
        for n, chunk in enumerate(DENSE):
            if last_piece_before(n) is not None:
                sp.wait_ge(lo_done, last_piece_before(n))
            if n == 2 * FREE_AFTER:
                sp.wait_ge(c_lo, 4)
                sp.wait_ge(o_lo, 4)
            load(slot_of(n), *dense_source(*chunk))

        def expert_loads(first, last, base):
            with sp.Fori(first, last) as it:
                for i, (name, j) in enumerate(EXPERT):
                    before = PB + 4 * (i - RING + 1) if i >= RING else FIRST[ND - RING + i + 1]
                    sp.wait_ge(lo_done, it * XP + before)
                    load(XSLOT[i], *moe_source(name, j, it - base))

        def tail_load(m):
            k0 = sum(TAIL_GATE[:m])
            off = 2 * PIECE if m == 0 else 0
            dst = ring[:, XSLOT[m], off:off + TAIL_GATE[m] * PIECE].rearrange("p (r n) -> p r n", n=D)
            ins = sp.dma_start(dst, a["ple_gate_w"][1, k0 * P:(k0 + TAIL_GATE[m]) * P, :].rearrange("(r p) n -> p r n", p=P))
            if m:
                ins.then_inc(slot_in[XSLOT[m]], 16)
                return
            ins.then_inc(tail_in, 16)
            sp.wait_ge(tail_in, 16)
            load(XSLOT[0], a["ple_proj"][1].rearrange("(r p) n -> p r n", p=P), 2, D)

        expert_loads(0, NE, 0)
        sp.wait_ge(tabs_done, 1)
        n_most = sp.value_load(most[0:1, 0:1])
        with sp.If(n_most > P):
            expert_loads(NE, ITERS, NE)
            for m in range(len(TAIL_GATE)):
                sp.wait_ge(lo_done, PT + 4 * (m + 1 - RING))
                tail_load(m)
        with sp.Else():
            for m in range(len(TAIL_GATE)):
                sp.wait_ge(lo_done, PB + NE * XP + 4 * (m + 1 - RING))
                tail_load(m)
            for s in range(RING):
                i0 = XSLOT.index(s)
                sp.wait_ge(slot_in[s], 16 * (XFILL[i0] - 1 + PER * NE + (s in XSLOT[:len(TAIL_GATE)])))
                sp.sem_inc(slot_in[s], 16 * PER * NE)
            sp.nop()
        out_rows = out[0].rearrange("(t p) d -> p t d", p=P)
        for t, c0, c1, n in ((0, 0, D, 2), (1, 0, 512, 3), (1, 512, D, 4)):
            sp.wait_ge(gated, n)
            sp.dma_start(out_rows[:, t, c0:c1], h[:, t, c0:c1]).then_inc(stored, 16)
        sp.wait_ge(stored, 16 * 3)

    @block.scalar
    def _(act):
        small = [(cst[:, :], a["consts"]), (vec[:, :], a["vectors"]),
                 (qk_gain, a["qk_gain"].broadcast_to([P, QK]))]
        for dst, src in small:
            act.dma_start(dst, src).then_inc(small_in, 16)
        n_small = 16 * 3

        def hi(n, chunk_sem=None, value=None, where=None):
            if chunk_sem is not None:
                act.wait_ge(chunk_sem, value)
            act.activation(hi_ring[:, n % AHEAD, :], where, ACT.Copy).then_inc(hi_done, 1)

        did = [0]

        def hi_upto(last):
            while did[0] <= min(last, PB - 1):
                n = did[0]
                c = max(m for m in range(ND) if FIRST[m] <= n)
                s = slot_of(c)
                if n >= AHEAD:
                    act.wait_ge(pe_piece, n - AHEAD + 1)
                off = (n - FIRST[c]) * PIECE
                hi(n, slot_in[s], 16 * fills_of(c), ring[:, s, off:off + PIECE])
                did[0] += 1
            for q in range(max(did[0] - PB, 0), last - PB + 1):
                act.wait_ge(pe_piece, PB + q - AHEAD + 1)
                hi(PB + q, slot_in[XSLOT[0]], 16 * XFILL[0], ring[:, XSLOT[0], q * PIECE:(q + 1) * PIECE])
                did[0] += 1

        def norm(i):
            act.activation(std[:, i, 0:1], eps[:, 0:1], ACT.Sqrt).then_inc(warm, 1)
            act.wait_ge(warm, i + 1)
            for t in range(T):
                act.wait_ge(h_ready, T * i + t + 1) if i else act.wait_ge(x_in[t], 16)
                act.activation(tok[:, t, :], h[:, t, :], ACT.Square, accum_out=ss[:, i, t:t + 1]).then_inc(ss_done, 1)
                act.wait_ge(ss_done, T * i + t + 1)
                act.activation(std[:, i, t:t + 1], ss[:, i, t:t + 1], ACT.Sqrt, bias=eps[:, 0:1], scale=1.0 / D).then_inc(std_done, 1)

        def norm_hi(i, bank=G8):
            for k in range(KT):
                act.wait_ge(tr_done, KT * i + (k | 1) + 1)
                act.activation(xT_hi[:, k, :], bank[:, k, :], ACT.Copy, scale=gains[:, i, k:k + 1]).then_inc(nhi_done, 1)

        act.wait_ge(eps_set, 1)
        norm(0)
        hi_upto(AHEAD - 1)
        act.wait_ge(small_in, n_small)
        norm_hi(0, Y8)
        hi_upto(7 + AHEAD)
        act.wait_ge(pe_piece, 8)
        act.activation(sig_b, G8[:, 4:8, :], ACT.Sigmoid).then_inc(sig_done, 1)

        def diagonals(first, last):
            for k in range(first, min(last, CONV_W)):
                if diag_used(k) > 0:
                    act.wait_ge(conv_mm_a, diag_used(k))
                act.activation(diag_of(3, k), ident, ACT.Copy, scale=conv_w[:, 3, k:k + 1]).then_inc(diag_a, 1)

        diagonals(0, DIAGS)
        hi_upto(11 + AHEAD)
        act.wait_ge(pe_piece, 12)
        act.activation(qk[:, :, 0:512], Y[:, 0:2, :], ACT.Copy).then_inc(qkv_copied, 1)
        hi_upto(13 + AHEAD)
        act.wait_ge(pe_piece, 14)
        act.activation(qk[:, :, 512:QK], Y[:, 2:4, 0:128], ACT.Copy).then_inc(qkv_copied, 1)
        act.activation(v_sb[:, :, :], Y[:, 2:4, 128:256], ACT.Copy).then_inc(qkv_copied, 1)
        diagonals(DIAGS, DIAGS + 4)
        act.wait_ge(qk_ss, 1)
        act.activation(s_small[:, 20:40], s_small[:, 0:20], ACT.Sqrt, bias=eps[:, 0:1], scale=1.0 / HEAD_DIM).then_inc(qk_std, 1)
        diagonals(DIAGS + 4, EARLY)
        act.wait_ge(qk_tr, 1)
        act.activation(qT[:, :, :], Y[:, 0:2, :].rearrange("p b (k n) -> p (b k) n", k=2), ACT.Copy).then_inc(qk_tr_copied, 1)
        act.activation(kT[:, :, :], Y[:, 2, :].rearrange("p (k n) -> p k n", k=2), ACT.Copy).then_inc(qk_tr_copied, 1)

        for i in range(HEADS + 2):
            diagonals(EARLY + 2 * i, EARLY + 2 * i + 2)
            if i < HEADS:
                act.wait_ge(neg_done, i + 1)
                for t in range(T):
                    act.activation(prob[:, i % 2, t, :], Y[:, i % 2, t * SEQ:(t + 1) * SEQ], ACT.Exp,
                                   bias=s_small[:, 44 + 2 * (i % 2) + t:45 + 2 * (i % 2) + t], scale=HEAD_DIM ** -0.5,
                                   accum_out=s_small[:, 48 + 2 * (i % 2) + t:49 + 2 * (i % 2) + t]).then_inc(exp_done, 1)
            if 1 <= i <= HEADS:
                act.wait_ge(pt_done, i)
                act.activation(probT[:, (i - 1) % 2, :, :],
                               Y[:, 2 + (i - 1) % 2, :].rearrange("p (k n) -> p k n", k=2), ACT.Copy).then_inc(pt_copied, 1)
            if i >= 3 and i % 2 == 1:
                c = (i - 3) // 2
                act.wait_ge(o_done, c + 1)
                act.activation(mT_hi[:, c, :], G[:, c % 2, 0:SEQ], ACT.Copy).then_inc(o_hi, 1)
        for c, done in ((2, conv_mm_p), (3, conv_mm_a)):
            act.wait_ge(done, CONV_W)
            act.activation(conv[:, c, :], G[:, c, 0:SEQ], ACT.Identity, bias=conv_b[:, c:c + 1]).then_inc(conv_out, 1)
        act.wait_ge(cent_done, 1)
        act.activation(ln_sq, conv, ACT.Square).then_inc(sq_done, 1)
        hi_upto(14 + AHEAD)
        act.wait_ge(var_mm, 1)
        act.activation(ln_std, G[:, 1, 0:SEQ], ACT.Sqrt, bias=eps[:, 0:1]).then_inc(lnstd_done, 1)
        act.wait_ge(lnn_done, 1)
        for c in range(CT + 1):
            if c < CT:
                act.activation(ln_out[:, c, :], conv[:, c, :], ACT.Silu, bias=ln_b[:, c:c + 1], scale=ln_g[:, c:c + 1]).then_inc(silu_c, 1)
            if c:
                act.wait_ge(silu_c, c)
                act.activation(mT_hi[:, 3 + c, :], ln_out[:, c - 1, :], ACT.Copy).then_inc(c_hi, 1)
                hi_upto(13 + c + AHEAD)
        hi_upto(21 + AHEAD)
        norm_hi(1, Y8)
        norm(1)
        hi_upto(FIRST[7] - 1 + AHEAD)
        act.wait_ge(factor_mm, 1)
        act.activation(factor_row, Y[:, 0, 0:SEQ], ACT.Copy).then_inc(factor_out, 1)

        def p_high(i):
            act.wait_ge(ptok_tr, i + 1)
            act.activation(pT_hi[i], p_bank[i].rearrange("p k (t n) -> p k t n", t=T), ACT.Copy).then_inc(p_hi, 1)

        last_group = max(c[2] for c in DENSE if c[0] == "ffn_wg")
        for i in range(2):
            for t in range(T):
                act.dma_start(p_tok[i][t], a["p"][i, 0, t * P:(t + 1) * P, :]).then_inc(p_in, 16)
        for n in range(6, ND):
            name, _, j, pieces = DENSE[n]
            if not name.startswith("ffn"):
                continue
            if (name, j) == ("ffn_wd", last_group):
                p_high(0)
                p_high(1)
            hi_upto(FIRST[n + 1] - 1 + AHEAD)
            f = pieces if name != "ffn_wd" else 0
            if name == "ffn_wg":
                act.wait_ge(fscaled, j + 1)
                act.activation(ffn_act[:, 0:f, :], ffn_act[:, 0:f, :], ACT.Silu).then_inc(fsilu, 1)
            if name == "ffn_wu":
                act.wait_ge(fmul, j + 1)
                b = 4 * (j % 2)
                act.activation(mT_hi[:, b:b + f, :], ffn_act[:, 0:f, :], ACT.Copy).then_inc(fhi, 1)

        def gate(i, norm_i, gate_end):
            act.activation(unused[:, i:i + 1], eps[:, 0:1], ACT.Sigmoid)
            act.wait_ge(rstd_done, T * (norm_i + 1))
            for b in range(2 * T):
                if b < 2 * T - 1:
                    act.wait_ge(bank_done, 3 * (2 + i) + b + 1)
                else:
                    act.wait_ge(pe_piece, gate_end)
                act.activation(tok[:, b // 2, (b % 2) * 512:(b % 2 + 1) * 512], Y[:, b, :], ACT.Sigmoid,
                               scale=rstd[:, norm_i, b // 2:b // 2 + 1]).then_inc(sig_gate, 1)

        g0 = [n for n in range(ND) if DENSE[n][0] == "proj0"][0]
        norm_hi(2, Y8)
        act.dma_start(bands, a["bands"].rearrange("p (t g n) -> p t g n", t=T, g=4)).then_inc(band_in, 16)
        hi_upto(FIRST[g0 + 1] - 1 + AHEAD)
        norm(2)
        hi_upto(FIRST[g0 + 3] - 3 + AHEAD)
        gate(0, 2, FIRST[g0 + 3])
        norm(3)
        hi_upto(FIRST[g0 + 3] - 1 + AHEAD)
        act.activation(rw_hi[:, :, :], rw, ACT.Copy).then_inc(rw_hi_done, 1)
        norm_hi(3)
        act.wait_ge(tr_done, 4 * KT)
        act.dma_start(scale_row, a["pool_scale"][0:1, :].broadcast_to([P, D])).then_inc(scale_in, 16)
        hi_upto(PB - 2 + AHEAD)
        norm_hi(4)
        norm(4)
        hi_upto(PB - 1 + AHEAD)
        act.wait_ge(route_v, 1)
        act.activation(rt[:, 48:50], rt[:, 46:48], ACT.Exp).then_inc(gap_exp, 1)

        def gathered_hi(value, first=0, last=KT):
            for k in range(first, last):
                act.wait_ge(gath_mm, value * 2 - 1 + k // 4)
                src = (G[:, 3, :], Y[:, 2, :])[k // 4][:, (k % 4) * P:(k % 4 + 1) * P]
                act.activation(xg_hi[:, k, :], src, ACT.Copy, scale=gains[:, 4, k:k + 1]).then_inc(xhi_done, 1)

        gathered_hi(1)

        def experts(first, last):
            with act.Fori(first, last) as it:
                for q in range(XP):
                    n = q + AHEAD
                    c, nxt = (n // 4) % NX, n // XP
                    act.wait_ge(pe_piece, it * XP + (PB + q + 1))
                    if n % 4 == 0:
                        act.wait_ge(slot_in[XSLOT[c]], it * (16 * PER) + 16 * (XFILL[c] + PER * nxt))
                    if q == XP - 1:
                        act.activation(y_sb, Y[:, 0:2, :].rearrange("p b n -> p (b n)"), ACT.Copy).then_inc(y_out, 1)
                    hi(PB + n, None, None, ring[:, XSLOT[c], (n % 4) * PIECE:(n % 4 + 1) * PIECE])
                    name, j = EXPERT[q // 4]
                    s = q % 4
                    if name == "moe_wg" and s == 3:
                        if j >= 1:
                            act.wait_ge(at_mm, it * GROUPS + j)
                            act.activation(aT_hi[:, (j - 1) % 2, :, :], G[:, 2, :].rearrange("p (f n) -> p f n", f=4),
                                           ACT.Copy).then_inc(at_hi, 1)
                        act.wait_ge(pe_piece, it * XP + (PB + q + 1))
                        act.activation(x_act, G[:, 0, :], ACT.Silu).then_inc(xsilu, 1)
                    if name == "moe_wu" and s == 3 and j == 3:
                        act.wait_ge(sp_mm, it + 1)
                        act.activation(spread, Y[:, 3, 0:SEQ], ACT.Copy).then_inc(sp_out, 1)
                    if name == "moe_wd" and s == 0 and j == GROUPS - 2:
                        act.wait_ge(at_mm, it * GROUPS + GROUPS)
                        act.activation(aT_hi[:, (GROUPS - 1) % 2, :, :], G[:, 2, :].rearrange("p (f n) -> p f n", f=4),
                                       ACT.Copy).then_inc(at_hi, 1)
                    if name == "moe_wd" and j == GROUPS - 2:
                        gathered_hi(it + 2, 2 * s, 2 * s + 2)

        experts(0, NE)
        act.wait_ge(tabs_done, 1)
        n_most = act.value_load(most[0:1, 0:1])
        with act.If(n_most > P):
            experts(NE, ITERS)
        with act.Else():
            for s, base, per in ((hi_done, PB + AHEAD, XP), (y_out, 1, 1), (sp_out, 1, 1)):
                act.wait_ge(s, base + NE * per)
                act.sem_inc(s, NE * per)
            act.nop()

        tdid = [AHEAD]

        def tail_upto(last):
            while tdid[0] <= last:
                q = tdid[0]
                c = q // 4
                act.wait_ge(pe_piece, PT + q - AHEAD + 1)
                if q % 4 == 0:
                    act.wait_ge(slot_in[XSLOT[c]], 16 * (XFILL[c] + PER * ITERS))
                hi(PT + q, None, None, ring[:, XSLOT[c], (q % 4) * PIECE:(q % 4 + 1) * PIECE])
                tdid[0] += 1

        tail_upto(4)
        norm_hi(5, Y8)
        tail_upto(5)
        norm(5)
        tail_upto(9)
        gate(1, 5, PT + 10)

    @block.vector
    def _(dve):
        chain = [0]

        def link(ins):
            chain[0] += 1
            ins.then_inc(chain_v, 1)
            dve.wait_ge(chain_v, chain[0])

        def lo(n, where):
            dve.tensor_tensor(lo_ring[:, n % AHEAD, :], where, hi_ring[:, n % AHEAD, :].bitcast(F32),
                              ALU.subtract).then_inc(lo_done, 1)

        did = [0]

        def lo_upto(last):
            while did[0] <= last:
                n = did[0]
                dve.wait_ge(hi_done, n + 1)
                if n < PB:
                    c = max(m for m in range(ND) if FIRST[m] <= n)
                    off = (n - FIRST[c]) * PIECE
                    lo(n, ring[:, slot_of(c), off:off + PIECE])
                else:
                    lo(n, ring[:, XSLOT[0], (n - PB) * PIECE:(n - PB + 1) * PIECE])
                did[0] += 1

        def factor(i, t):
            dve.wait_ge(std_done, T * i + t + 1)
            dve.reciprocal(rstd[:, i, t:t + 1], std[:, i, t:t + 1]).then_inc(rstd_done, 1)

        def norm(i):
            for t in range(T):
                factor(i, t)
                dve.wait_ge(rstd_done, T * i + t + 1)
                dve.tensor_scalar(tok[:, t, :], h[:, t, :], rstd[:, i, t:t + 1], None, ALU.mult).then_inc(tok_done, 1)

        def norm_lo(i, bank=G8):
            for k in range(KT):
                dve.wait_ge(nhi_done, KT * i + (k | 1) + 1)
                dve.scalar_tensor_tensor(out=xT_lo[:, k, :], in0=bank[:, k, :], scalar=gains[:, i, k:k + 1],
                                         in1=xT_hi[:, k, :].bitcast(F32), op0=ALU.mult, op1=ALU.subtract).then_inc(nlo_done, 1)

        def add_rows(i, use, end):
            for t in range(T):
                dve.wait_ge(bank_done, 3 * use + 2) if t == 0 else dve.wait_ge(pe_piece, end)
                dve.tensor_tensor(h[:, t, :], h[:, t, :], Y[:, 2 * t:2 * t + 2, :].rearrange("p b n -> p (b n)"),
                                  ALU.add).then_inc(h_ready, 1)
            dve.wait_ge(h_ready, T * (i + 1))

        dve.memset(eps[:, :], EPS).then_inc(eps_set, 1)
        norm(0)
        dve.sem_inc(h_ready, T)
        lo_upto(1)
        norm_lo(0, Y8)
        lo_upto(7 + AHEAD)
        dve.wait_ge(pads_set, 1)
        dve.wait_ge(sig_done, 1)
        dve.tensor_tensor(upad[:, :, PAD:PAD + SEQ], G8[:, 0:4, :], sig_b, ALU.mult).then_inc(glu_done, 1)
        dve.wait_ge(glu_done, 1)

        taps = [(k, c) for k in range(CONV_W) for c in range(2)]

        def tap(n):
            k, c = taps[n]
            if k == 0:
                dve.tensor_scalar(conv[:, c, :], upad[:, c, 0:SEQ], conv_w[:, c, 0:1], conv_b[:, c:c + 1],
                                  ALU.mult, ALU.add).then_inc(conv_v, 1)
            else:
                dve.wait_ge(conv_v, n - 1)
                dve.scalar_tensor_tensor(out=conv[:, c, :], in0=upad[:, c, k:k + SEQ], scalar=conv_w[:, c, k:k + 1],
                                         in1=conv[:, c, :], op0=ALU.mult, op1=ALU.add).then_inc(conv_v, 1)

        nt = 0
        for n in range(8, 14):
            for _ in range(5):
                tap(nt)
                nt += 1
            lo_upto(n + AHEAD)
        dve.wait_ge(qkv_copied, 2)
        qkh = qk.rearrange("p t (n f) -> p (t n) f", f=HEAD_DIM)
        link(dve.tensor_tensor(sq, qk, qk, ALU.mult))
        dve.tensor_reduce(s_small[:, 0:20], sq.rearrange("p t (n f) -> p (t n) f", f=HEAD_DIM), AX.X, ALU.add).then_inc(qk_ss, 1)
        dve.wait_ge(qk_std, 1)
        link(dve.reciprocal(s_small[:, 0:20], s_small[:, 20:40]))
        link(dve.tensor_tensor(qkh, qkh, s_small[:, 0:20].unsqueeze(2).broadcast_to([P, 20, HEAD_DIM]), ALU.mult))
        for t in range(T):
            ins = dve.tensor_tensor(qk[:, t, :], qk[:, t, :], qk_gain, ALU.mult)
        link(ins)
        for t in range(T):
            x = qk[:, t, :].rearrange("p (n c f) -> p n c f", c=2, f=HALF)
            cb = cos[:, t, :].unsqueeze(1).broadcast_to([P, 10, HALF])
            sn = sin[:, t, :].unsqueeze(1).broadcast_to([P, 10, HALF])
            r = rope[:, t]
            dve.tensor_tensor(r[:, 0], x[:, :, 0, :], cb, ALU.mult)
            dve.tensor_tensor(r[:, 1], x[:, :, 1, :], sn, ALU.mult)
            dve.tensor_tensor(r[:, 2], x[:, :, 1, :], cb, ALU.mult)
            ins = dve.tensor_tensor(r[:, 3], x[:, :, 0, :], sn, ALU.mult)
        link(ins)
        for t in range(T):
            r = rope[:, t]
            q_out = rot[:, t, 0:512].rearrange("p (n c f) -> p n c f", c=2, f=HALF)
            k_out = rot[:, t, 512:768].rearrange("p (n u c f) -> p n u c f", u=2, c=2, f=HALF)
            for c, (m, op) in enumerate(((0, ALU.subtract), (2, ALU.add))):
                ins = dve.tensor_tensor(q_out[:, :, c, :], r[:, m, 0:8, :], r[:, m + 1, 0:8, :], op)
                for u in range(2):
                    ins = dve.tensor_tensor(k_out[:, :, u, c, :], r[:, m, 8:10, :], r[:, m + 1, 8:10, :], op)
        ins.then_inc(qk_rot, 1)
        for i in range(HEADS + 2):
            if i < HEADS:
                b = i % 2
                dve.wait_ge(sc_done, i + 1)
                link(dve.tensor_reduce(s_small[:, 40 + 2 * b:42 + 2 * b], Y[:, b, :].rearrange("p (t n) -> p t n", t=T), AX.X, ALU.max))
                dve.tensor_scalar(s_small[:, 44 + 2 * b:46 + 2 * b], s_small[:, 40 + 2 * b:42 + 2 * b], -HEAD_DIM ** -0.5,
                                  None, ALU.mult).then_inc(neg_done, 1)
            for _ in range(4):
                if nt < len(taps):
                    tap(nt)
                    nt += 1
            if i < HEADS:
                dve.wait_ge(exp_done, T * (i + 1))
                link(dve.reciprocal(s_small[:, 52 + 2 * b:54 + 2 * b], s_small[:, 48 + 2 * b:50 + 2 * b]))
                for t in range(T):
                    ins = dve.tensor_scalar(prob[:, b, t, :], prob[:, b, t, :], s_small[:, 52 + 2 * b + t:53 + 2 * b + t], None, ALU.mult)
                ins.then_inc(nrm_done, 1)
            if i >= 3 and i % 2 == 1:
                c = (i - 3) // 2
                dve.wait_ge(o_hi, c + 1)
                dve.tensor_tensor(mT_lo[:, c, :], G[:, c % 2, 0:SEQ], mT_hi[:, c, :].bitcast(F32), ALU.subtract).then_inc(o_lo, 1)
        while nt < len(taps):
            tap(nt)
            nt += 1
        dve.wait_ge(mean_mm, 1)
        dve.tensor_tensor(conv, conv, G[:, 0, 0:SEQ].unsqueeze(1).broadcast_to([P, CT, SEQ]), ALU.subtract).then_inc(cent_done, 1)
        lo_upto(14 + AHEAD)
        dve.wait_ge(lnstd_done, 1)
        link(dve.reciprocal(ln_rstd, ln_std))
        dve.tensor_tensor(conv, conv, ln_rstd.unsqueeze(1).broadcast_to([P, CT, SEQ]), ALU.mult).then_inc(lnn_done, 1)
        for c in range(CT):
            dve.wait_ge(c_hi, c + 1)
            dve.tensor_tensor(mT_lo[:, 4 + c, :], ln_out[:, c, :], mT_hi[:, 4 + c, :].bitcast(F32), ALU.subtract).then_inc(c_lo, 1)
            lo_upto(14 + c + AHEAD)
        lo_upto(19 + AHEAD)
        add_rows(1, 0, 22)
        norm_lo(1, Y8)
        lo_upto(21 + AHEAD)
        for t in range(T):
            factor(1, t)
        dve.wait_ge(rstd_done, T * 2)
        for t in range(T):
            dve.tensor_scalar(factor_diag[:, t, :], ident, rstd[:, 1, t:t + 1], None, ALU.mult).then_inc(factor_d, 1)

        def p_low(i):
            dve.wait_ge(p_hi, i + 1)
            dve.tensor_tensor(pT_lo[i], p_bank[i].rearrange("p k (t n) -> p k t n", t=T), pT_hi[i].bitcast(F32),
                              ALU.subtract).then_inc(p_lo, 1)

        last_group = max(c[2] for c in DENSE if c[0] == "ffn_wg")
        for n in range(6, ND):
            name, _, j, pieces = DENSE[n]
            if not name.startswith("ffn"):
                continue
            if (name, j) == ("ffn_wd", last_group):
                p_low(0)
                p_low(1)
                lo_upto(FIRST[n + 1] - 3 + AHEAD)
                continue
            lo_upto(FIRST[n + 1] - 1 + AHEAD)
            if name == "ffn_wg":
                if j:
                    dve.wait_ge(flo, j)
                dve.wait_ge(factor_out, 1)
                dve.wait_ge(pe_piece, FIRST[n + 1])
                dve.tensor_tensor(ffn_act[:, 0:pieces, :], G8[:, 0:pieces, :],
                                  factor_row.unsqueeze(1).broadcast_to([P, pieces, SEQ]), ALU.mult).then_inc(fscaled, 1)
            if name == "ffn_wu":
                b = 4 * (j % 2)
                dve.wait_ge(pe_piece, FIRST[n + 1])
                dve.wait_ge(fsilu, j + 1)
                dve.tensor_tensor(ffn_act[:, 0:pieces, :], ffn_act[:, 0:pieces, :], G8[:, 4:4 + pieces, :], ALU.mult).then_inc(fmul, 1)
                dve.wait_ge(fhi, j + 1)
                dve.tensor_tensor(mT_lo[:, b:b + pieces, :], ffn_act[:, 0:pieces, :], mT_hi[:, b:b + pieces, :].bitcast(F32),
                                  ALU.subtract).then_inc(flo, 1)
        g0 = [n for n in range(ND) if DENSE[n][0] == "proj0"][0]
        for t in range(T):
            dve.wait_ge(bank_done, 3 * 1 + 2) if t == 0 else dve.wait_ge(pe_piece, FIRST[g0])
            dve.scalar_tensor_tensor(out=h[:, t, :], in0=Y[:, 2 * t:2 * t + 2, :].rearrange("p b n -> p (b n)"),
                                     scalar=rstd[:, 1, t:t + 1], in1=h[:, t, :], op0=ALU.mult, op1=ALU.add).then_inc(h_ready, 1)
        dve.wait_ge(h_ready, T * 3)

        def gate(i):
            for b in range(2 * T):
                t, c = b // 2, slice((b % 2) * 512, (b % 2 + 1) * 512)
                dve.wait_ge(sig_gate, 2 * T * i + b + 1)
                link(dve.tensor_tensor(tok[:, t, c], tok[:, t, c], G[:, b, :], ALU.mult))
                ins = dve.tensor_tensor(h[:, t, c], h[:, t, c], tok[:, t, c], ALU.add)
                if i:
                    ins.then_inc(gated, 1)
                elif b % 2:
                    ins.then_inc(h_ready, 1)

        lo_upto(FIRST[g0] - 1 + AHEAD)
        norm_lo(2, Y8)
        lo_upto(FIRST[g0 + 1] - 1 + AHEAD)
        for t in range(T):
            factor(2, t)
        lo_upto(FIRST[g0 + 3] - 3 + AHEAD)
        gate(0)
        dve.wait_ge(h_ready, T * 4)
        norm(3)
        lo_upto(FIRST[g0 + 3] - 1 + AHEAD)
        dve.wait_ge(rw_hi_done, 1)
        dve.tensor_tensor(rw_lo[:, :, :], rw, rw_hi[:, :, :].bitcast(F32), ALU.subtract).then_inc(rw_lo_done, 1)
        norm_lo(3)
        dve.wait_ge(scale_in, 16)
        for s in range(2):
            c = slice(s * 512, (s + 1) * 512)
            dve.wait_ge(pe_piece, PB - 1 + s)
            for t in range(T):
                dve.tensor_tensor(tok[:, t, c], Y[:, 2 * t + s, :], scale_row[:, c], ALU.mult).then_inc(scaled, 1)
            for t in range(T):
                dve.wait_ge(scaled, T * s + t + 1)
                dve.tensor_tensor(h[:, t, c], h[:, t, c], tok[:, t, c], ALU.add).then_inc(h_ready if s else pooled, 1)
        norm_lo(4)
        for t in range(T):
            factor(4, t)
        dve.wait_ge(rstd_done, T * 5)

        logit = rt[:, 0:16].rearrange("p (t e) -> p t e", t=T)
        best = rt[:, 16:32].rearrange("p (t e) -> p t e", t=T)
        idxf = rt[:, 32:36].rearrange("p (t e) -> p t e", t=T)
        gap, ex = rt[:, 46:48], rt[:, 48:50]
        p1, p2, one_more = rt[:, 50:52], rt[:, 52:54], rt[:, 54:56]
        hot1 = rt[:, 56:72].rearrange("p (t e) -> p t e", t=T)
        hot2 = rt[:, 72:88].rearrange("p (t e) -> p t e", t=T)
        mask = rt[:, 88:104].rearrange("p (t e) -> p t e", t=T)
        gate_a = rt[:, 104:120].rearrange("p (t e) -> p t e", t=T)
        rank1 = rt[:, 120:136].rearrange("p (t e) -> p t e", t=T)
        top_count = rt[:, 136:137]
        dve.wait_ge(logit_mm, 1)
        dve.tensor_copy(logit_row[0:NE, :], Y[0:NE, 0, 0:SEQ]).then_inc(logit_out, 1)
        dve.wait_ge(logit_tr, 1)
        for t in range(T):
            ins = dve.tensor_scalar(logit[:, t, :], Y[:, 1, t * NE:(t + 1) * NE], rstd[:, 4, t:t + 1], None, ALU.mult)
        link(ins)
        for t in range(T):
            ins = dve.max(best[:, t, :], logit[:, t, :])
        link(ins)
        for t in range(T):
            ins = dve.max_index(idx8[:, t, :], best[:, t, :], logit[:, t, :])
        link(ins)
        link(dve.tensor_copy(idxf, idx8[:, :, 0:2]))
        dve.tensor_tensor(gap, best[:, :, 1], best[:, :, 0], ALU.subtract).then_inc(route_v, 1)
        for t in range(T):
            dve.tensor_scalar(hot1[:, t, :], iota[:, 0:NE], idxf[:, t, 0:1], None, ALU.is_equal)
            ins = dve.tensor_scalar(hot2[:, t, :], iota[:, 0:NE], idxf[:, t, 1:2], None, ALU.is_equal)
        link(ins)
        dve.tensor_tensor(mask, hot1, hot2, ALU.add).then_inc(mask_done, 1)
        dve.wait_ge(gap_exp, 1)
        link(dve.tensor_scalar(one_more, ex, 1.0, None, ALU.add))
        link(dve.reciprocal(p1, one_more))
        link(dve.tensor_tensor(p2, p1, ex, ALU.mult))
        for t in range(T):
            ins = dve.tensor_scalar(gate_a[:, t, :], hot1[:, t, :], p1[:, t:t + 1], None, ALU.mult)
        link(ins)
        for t in range(T):
            ins = dve.scalar_tensor_tensor(out=gate_a[:, t, :], in0=hot2[:, t, :], scalar=p2[:, t:t + 1], in1=gate_a[:, t, :],
                                           op0=ALU.mult, op1=ALU.add)
        link(ins)
        for s in range(2):
            dve.tensor_copy(gate_tab[:, :, s * NE:(s + 1) * NE], gate_a)
        dve.memset(gate_tab[:, :, ITERS:], 0.0)
        dve.memset(slot_tab[:, :, ITERS:], NOWHERE)
        dve.wait_ge(mask_done, 1)
        dve.wait_ge(rank_mm, 1)
        ranks = Y[:, 2, 0:16].rearrange("p (t e) -> p t e", t=T)
        link(dve.scalar_tensor_tensor(out=rank1, in0=ranks, scalar=-NOWHERE, in1=mask, op0=ALU.add, op1=ALU.mult))
        for s in range(2):
            ins = dve.tensor_scalar(slot_tab[:, :, s * NE:(s + 1) * NE], rank1, NOWHERE - s * P, None, ALU.add)
        link(ins)

        def gathered_lo(value, first=0, last=KT):
            for k in range(first, last):
                dve.wait_ge(xhi_done, value + (k | 3) + 1)
                src = (G[:, 3, :], Y[:, 2, :])[k // 4][:, (k % 4) * P:(k % 4 + 1) * P]
                dve.scalar_tensor_tensor(out=xg_lo[:, k, :], in0=src, scalar=gains[:, 4, k:k + 1],
                                         in1=xg_hi[:, k, :].bitcast(F32), op0=ALU.mult, op1=ALU.subtract).then_inc(xlo_done, 1)

        def picks(it):
            for t in range(T):
                slot = slot_tab[:, t, bass.ds(it, 1)]
                dve.tensor_scalar(pick[:, t, :], iota, slot, rstd[:, 4, t:t + 1], ALU.is_equal, ALU.mult).then_inc(pick_done, 1)
            for t in range(T):
                slot = slot_tab[:, t, bass.ds(it, 1)]
                dve.tensor_scalar(pick_gated[:, t, :], iota, slot, gate_tab[:, t, bass.ds(it, 1)], ALU.is_equal, ALU.mult).then_inc(pick_done, 1)

        picks(0)
        dve.wait_ge(rank_mm, 2)
        link(dve.tensor_reduce(top_count, Y[:, 3, 0:8], AX.X, ALU.max))
        link(dve.tensor_copy(most[:, :], top_count))
        dve.sem_inc(tabs_done, 1)
        lo_upto(PB - 1 + AHEAD)
        gathered_lo(0)

        def experts(first, last):
            with dve.Fori(first, last) as it:
                for q in range(XP):
                    n = q + AHEAD
                    c = (n // 4) % NX
                    dve.wait_ge(hi_done, it * XP + (PB + n + 1))
                    lo(PB + n, ring[:, XSLOT[c], (n % 4) * PIECE:(n % 4 + 1) * PIECE])
                    name, j = EXPERT[q // 4]
                    s = q % 4

                    def at_low(j):
                        dve.wait_ge(at_hi, it * GROUPS + (j + 1))
                        dve.tensor_tensor(aT_lo[:, j % 2, :, :], G[:, 2, :].rearrange("p (f n) -> p f n", f=4),
                                          aT_hi[:, j % 2, :, :].bitcast(F32), ALU.subtract).then_inc(at_lo, 1)

                    if name == "moe_wg" and s == 3:
                        if j >= 1:
                            at_low(j - 1)
                        else:
                            dve.wait_ge(scat_mm, it + 1)
                            dve.wait_ge(scat_add, it * 4 + 1)
                    u = q - 3
                    if 0 <= u < 4:
                        acc = tok[:, u // 2, (u % 2) * 512:(u % 2 + 1) * 512]
                        dve.tensor_tensor(acc, acc, (G[:, 3, :], Y[:, 2, :], Y[:, 3, :], G[:, 2, :])[u], ALU.add).then_inc(scat_add, 1)
                    if name == "moe_wu" and s == 0 and j == 5:
                        dve.wait_ge(sp_mm, it + 1)
                        picks(it + 1)
                    if name == "moe_wu" and s == 3:
                        dve.wait_ge(pe_piece, it * XP + (PB + q + 1))
                        dve.wait_ge(xsilu, it * GROUPS + (j + 1))
                        dve.tensor_tensor(x_act, x_act, G[:, 1, :], ALU.mult).then_inc(xmul, 1)
                    if name == "moe_wd" and s == 0 and j == GROUPS - 2:
                        at_low(GROUPS - 1)
                    if name == "moe_wd" and j >= GROUPS - 2:
                        at = {GROUPS - 2: (0, 0, 2, 4, 6), GROUPS - 1: (6, 8, 8, 8, 8)}[j]
                        if at[s + 1] > at[s]:
                            gathered_lo(it * KT + KT, at[s], at[s + 1])

        experts(0, NE)
        dve.wait_ge(tabs_done, 1)
        n_most = dve.value_load(most[0:1, 0:1])
        with dve.If(n_most > P):
            experts(NE, ITERS)
        with dve.Else():
            for s, base, per in ((lo_done, PB + AHEAD, XP), (xlo_done, KT, KT), (scat_add, 1, 4)):
                dve.wait_ge(s, base + NE * per)
                dve.sem_inc(s, NE * per)
            dve.nop()
        dve.wait_ge(scat_add, 4 * ITERS + 1)
        for t in range(T):
            ins = dve.tensor_tensor(h[:, t, :], h[:, t, :], tok[:, t, :], ALU.add)
        link(ins)
        for t in range(T):
            dve.wait_ge(last_mm, t + 1)
            dve.tensor_tensor(h[:, t, :], h[:, t, :], Y[:, 2 * t:2 * t + 2, :].rearrange("p b n -> p (b n)"),
                              ALU.add).then_inc(h_ready, 1)

        tdid = [AHEAD]

        def tail_upto(last):
            while tdid[0] <= last:
                q = tdid[0]
                dve.wait_ge(hi_done, PT + q + 1)
                lo(PT + q, ring[:, XSLOT[q // 4], (q % 4) * PIECE:(q % 4 + 1) * PIECE])
                tdid[0] += 1

        tail_upto(4)
        norm_lo(5, Y8)
        tail_upto(5)
        for t in range(T):
            factor(5, t)
        tail_upto(9)
        gate(1)

    @block.gpsimd
    def _(pool):
        pool.memset(upad[:, :, 0:PAD], 0.0)
        pool.memset(upad[:, :, PAD + SEQ:], 0.0).then_inc(pads_set, 1)
        pool.wait_ge(small_in, 16 * 3)
        for k in range(CONV_W):
            if k == EARLY:
                pool.wait_ge(qk_tr, 1)
            if diag_used(k) > 0:
                pool.wait_ge(conv_mm_p, diag_used(k))
            pool.tensor_scalar(diag_of(2, k), ident, conv_w[:, 2, k:k + 1], None, ALU.mult).then_inc(diag_p, 1)

        pool.wait_ge(tabs_done, 1)
        pool.memset(y_sb, 0.0).then_inc(y_out, 1)
        pool.memset(spread, 0.0).then_inc(sp_out, 1)
        pool.memset(tok[:, :, :], 0.0).then_inc(scat_add, 1)

    @block.tensor
    def _(pe):
        def piece(n, last):
            last.then_inc(pe_piece, 1)

        def three(dst, s_hi, s_lo, m_hi, m_lo, start, stop):
            pe.matmul(dst, s_hi, m_hi, start=start, stop=False, skip_group_check=True)
            pe.matmul(dst, s_lo, m_hi, start=False, stop=False, skip_group_check=True)
            return pe.matmul(dst, s_hi, m_lo, start=False, stop=stop, skip_group_check=True)

        def norm(i, bank=G8):
            src = h if i in RAW else tok
            for half in range(2):
                for t in range(T):
                    if i == 4 and half == 0:
                        pe.wait_ge(pooled, t + 1)
                    elif i in RAW:
                        pe.wait_ge(h_ready, T * i + t + 1)
                    else:
                        pe.wait_ge(tok_done, T * SCALED.index(i) + t + 1)
                    for k in range(half * KT // 2, (half + 1) * KT // 2):
                        ins = pe.transpose(bank[:, k, t * P:(t + 1) * P], src[:, t, k * P:(k + 1) * P], ident)
                        if t == T - 1:
                            ins.then_inc(tr_done, 1)

        def cols_tokens(n0, pieces, dst, width):
            per = PIECE // width
            for s in range(pieces):
                pe.wait_ge(lo_done, n0 + s + 1)
                w_hi, w_lo = piece_at(hi_ring, n0 + s, width), piece_at(lo_ring, n0 + s, width)
                for r in range(per):
                    k = s * per + r
                    for t in range(T):
                        ins = three(dst(t), xT_hi[:, k, t * P:(t + 1) * P], xT_lo[:, k, t * P:(t + 1) * P],
                                    w_hi[:, r, :], w_lo[:, r, :], k == 0, k == KT - 1)
                piece(n0 + s, ins)
            return ins

        def cols_channels(n0, pieces, bank0, width, i):
            per = PIECE // width
            tiles = width // P
            for s in range(pieces):
                pe.wait_ge(lo_done, n0 + s + 1)
                w_hi, w_lo = piece_at(hi_ring, n0 + s, width), piece_at(lo_ring, n0 + s, width)
                for r in range(per):
                    k = s * per + r
                    if bank0 == 0:
                        pe.wait_ge(nlo_done, KT * i + k + 1)
                    for f in range(tiles):
                        ins = three(G8[:, 2 * bank0 + f, :], w_hi[:, r, f * P:(f + 1) * P], w_lo[:, r, f * P:(f + 1) * P],
                                    xT_hi[:, k, :], xT_lo[:, k, :], k == 0 and f % 2 == 0, k == KT - 1)
                piece(n0 + s, ins)
            return ins

        def rows(n, s_hi, s_lo, bank, first, last):
            pe.wait_ge(lo_done, n + 1)
            w_hi, w_lo = hi_ring[:, n % AHEAD, :], lo_ring[:, n % AHEAD, :]
            if len(s_hi.shape) == 2:
                s_hi, s_lo = (s.rearrange("p (t n) -> p t n", t=T) for s in (s_hi, s_lo))
            for t in range(T):
                for c in range(2):
                    ins = three(bank[:, 2 * t + c, :], s_hi[:, t, :], s_lo[:, t, :],
                                w_hi[:, c * 512:(c + 1) * 512], w_lo[:, c * 512:(c + 1) * 512], first, last)
            piece(n, ins)
            return ins

        def last_rows(n, tiles, bank):
            for u in range(2):
                pe.wait_ge(lo_done, n + u + 1)
            for t in range(T):
                for u, (s_hi, s_lo) in enumerate(tiles):
                    w_hi, w_lo = hi_ring[:, (n + u) % AHEAD, :], lo_ring[:, (n + u) % AHEAD, :]
                    for c in range(2):
                        ins = three(bank[:, 2 * t + c, :], s_hi[:, t * P:(t + 1) * P], s_lo[:, t * P:(t + 1) * P],
                                    w_hi[:, c * 512:(c + 1) * 512], w_lo[:, c * 512:(c + 1) * 512], False, u == 1)
                        if u and (t, c) != (T - 1, 1):
                            ins.then_inc(bank_done, 1)
                    if t == T - 1:
                        piece(n + u, ins)

        pe.wait_ge(small_in, 16 * 3)
        norm(0, Y8)
        cols_channels(0, 4, 0, 512, 0)
        cols_channels(4, 4, 2, 512, 0)
        cols_tokens(8, 4, lambda t: Y[:, t, :], 512)
        cols_tokens(12, 2, lambda t: Y[:, 2 + t, 0:256], 256)

        def conv_taps(first, last):
            for k in range(first, min(last, CONV_W)):
                for c, made, done in ((2, diag_p, conv_mm_p), (3, diag_a, conv_mm_a)):
                    pe.wait_ge(made, k + 1)
                    pe.matmul(G[:, c, 0:SEQ], diag_of(c, k), upad[:, c, k:k + SEQ],
                              start=(k == 0), stop=(k == CONV_W - 1)).then_inc(done, 1)

        pe.wait_ge(glu_done, 1)
        conv_taps(0, EARLY)
        pe.wait_ge(qk_rot, 1)
        pe.wait_ge(qkv_copied, 3)
        for c in range(6):
            for t in range(T):
                ins = pe.transpose(Y[:, c // 2, (c % 2) * SEQ + t * P:(c % 2) * SEQ + (t + 1) * P],
                                   rot[:, t, c * P:(c + 1) * P], ident)
        ins.then_inc(qk_tr, 1)
        pe.wait_ge(qk_tr_copied, 2)
        for i in range(HEADS + 2):
            if i < HEADS:
                if i >= 2:
                    pe.wait_ge(exp_done, T * (i - 1))
                lo_p = (i % 2) * HEAD_DIM
                for t in range(T):
                    ins = pe.matmul(Y[:, i % 2, t * SEQ:(t + 1) * SEQ], qT[lo_p:lo_p + HEAD_DIM, i // 2, t * P:(t + 1) * P],
                                    kT[lo_p:lo_p + HEAD_DIM, i // 4, :], start=True, stop=True)
                ins.then_inc(sc_done, 1)
            conv_taps(EARLY + 2 * i, EARLY + 2 * i + 2)
            if 1 <= i <= HEADS:
                hd = i - 1
                pe.wait_ge(nrm_done, hd + 1)
                if hd >= 2:
                    pe.wait_ge(pt_copied, hd - 1)
                for k in range(T):
                    for t in range(T):
                        ins = pe.transpose(Y[:, 2 + hd % 2, k * SEQ + t * P:k * SEQ + (t + 1) * P],
                                           prob[:, hd % 2, t, k * P:(k + 1) * P], ident)
                ins.then_inc(pt_done, 1)
            if i >= 2:
                hd = i - 2
                pe.wait_ge(pt_copied, hd + 1)
                if hd >= 4 and hd % 2 == 0:
                    pe.wait_ge(o_lo, hd // 2 - 1)
                lo_p = (hd % 2) * HEAD_DIM
                for k in range(T):
                    ins = pe.matmul(G[lo_p:lo_p + HEAD_DIM, (hd // 2) % 2, 0:SEQ],
                                    v_sb[:, k, (hd // 4) * HEAD_DIM:(hd // 4 + 1) * HEAD_DIM],
                                    probT[:, hd % 2, k, :], start=(k == 0), stop=(k == T - 1))
                if hd % 2:
                    ins.then_inc(o_done, 1)
        pe.wait_ge(o_lo, 4)
        pe.wait_ge(conv_v, CONV_W * 2)
        pe.wait_ge(conv_out, 2)
        for c in range(CT):
            ins = pe.matmul(G[:, 0, 0:SEQ], mean_mat, conv[:, c, :], start=(c == 0), stop=(c == CT - 1))
        ins.then_inc(mean_mm, 1)
        rows(14, mT_hi[:, 0, :], mT_lo[:, 0, :], Y, True, False)
        pe.wait_ge(sq_done, 1)
        for c in range(CT):
            ins = pe.matmul(G[:, 1, 0:SEQ], mean_mat, ln_sq[:, c, :], start=(c == 0), stop=(c == CT - 1))
        ins.then_inc(var_mm, 1)
        for e in range(1, 4):
            rows(14 + e, mT_hi[:, e, :], mT_lo[:, e, :], Y, False, False)
        for e in range(4, 6):
            pe.wait_ge(c_lo, e - 3)
            rows(14 + e, mT_hi[:, e, :], mT_lo[:, e, :], Y, False, False)
        pe.wait_ge(c_lo, 4)
        last_rows(20, [(mT_hi[:, e, :], mT_lo[:, e, :]) for e in (6, 7)], Y)

        def p_transposes(i):
            pe.wait_ge(p_in, 16 * 2 * T)
            for k in range(2):
                for t in range(T):
                    ins = pe.transpose(p_bank[i][:, k, t * P:(t + 1) * P], p_tok[i][t][:, k * P:(k + 1) * P], ident)
            ins.then_inc(ptok_tr, 1)

        last_group = max(c[2] for c in DENSE if c[0] == "ffn_wg")
        norm(1, Y8)
        for n in range(6, ND):
            name, _, j, pieces = DENSE[n]
            if name == "ffn_wg":
                if j >= 1:
                    pe.wait_ge(fscaled, j)
                cols_channels(FIRST[n], pieces, 0, COLS * pieces // 4, 1)
                if j == 0:
                    pe.wait_ge(factor_d, T)
                    for t in range(T):
                        ins = pe.matmul(Y[:, 0, t * P:(t + 1) * P], ones_mat, factor_diag[:, t, :], start=True, stop=True)
                    ins.then_inc(factor_mm, 1)
            if name == "ffn_wu":
                if j >= 1:
                    pe.wait_ge(fmul, j)
                cols_channels(FIRST[n], pieces, 2, COLS * pieces // 4, 1)
            if name == "ffn_wd":
                if j == last_group:
                    for i in range(2):
                        p_transposes(i)
                pe.wait_ge(factor_out, 1)
                pe.wait_ge(flo, j + 1)
                if j == last_group:
                    b = 4 * (j % 2)
                    last_rows(FIRST[n], [(mT_hi[:, b + f, :], mT_lo[:, b + f, :]) for f in range(2)], Y)
                    continue
                for f in range(pieces):
                    b = 4 * (j % 2) + f
                    rows(FIRST[n] + f, mT_hi[:, b, :], mT_lo[:, b, :], Y, j == 0 and f == 0, False)

        def ple(i, norm_i, first):
            pe.wait_ge(p_lo, 2)
            rows(first, pT_hi[i][:, 0], pT_lo[i][:, 0], G, True, False)
            norm(norm_i, Y8)
            rows(first + 1, pT_hi[i][:, 1], pT_lo[i][:, 1], G, False, True)
            pe.wait_ge(nlo_done, KT * (norm_i + 1))
            for k in range(KT - 2):
                rows(first + 2 + k, xT_hi[:, k, :], xT_lo[:, k, :], Y, k == 0, False)
            last_rows(first + KT, [(xT_hi[:, k, :], xT_lo[:, k, :]) for k in (KT - 2, KT - 1)], Y)

        ple(0, 2, FIRST[[n for n in range(ND) if DENSE[n][0] == "proj0"][0]])

        pe.wait_ge(band_in, 16)
        for t in range(T):
            pe.wait_ge(tok_done, T + t + 1)
            for k in range(KT):
                ins = pe.matmul(G8[:, k, :], tok[:, t, k * P:(k + 1) * P], bands[:, t, k // 2, :],
                                start=(t == 0 and k % 2 == 0), stop=(t == T - 1), skip_group_check=True)
                if t == T - 1:
                    ins.then_inc(tr_done, 1)
        for s in range(2):
            n = FIRST[ND - 1] + s
            pe.wait_ge(lo_done, n + 1)
            w_hi, w_lo = piece_at(hi_ring, n, 256), piece_at(lo_ring, n, 256)
            for r in range(4):
                g, k = 2 * s + r // 2, 4 * s + r
                pe.wait_ge(nlo_done, KT * 3 + k + 1)
                for t in range(T):
                    ins = three(Y[:, 2 * t + g // 2, (g % 2) * 256:(g % 2 + 1) * 256], xT_hi[:, k, t * P:(t + 1) * P],
                                xT_lo[:, k, t * P:(t + 1) * P], w_hi[:, r, :], w_lo[:, r, :], k % 4 == 0, k % 2 == 1)
            piece(n, ins)

        norm(4)
        pe.wait_ge(rw_lo_done, 1)
        pe.wait_ge(h_ready, T * 5)
        for k in range(KT):
            pe.wait_ge(nlo_done, KT * 4 + k + 1)
            ins = three(Y[0:NE, 0, 0:SEQ], rw_hi[:, k, :], rw_lo[:, k, :], xT_hi[:, k, :], xT_lo[:, k, :], k == 0, k == KT - 1)
        ins.then_inc(logit_mm, 1)
        pe.wait_ge(logit_out, 1)
        for t in range(T):
            ins = pe.transpose(Y[:, 1, t * NE:(t + 1) * NE], logit_row[0:NE, t * P:(t + 1) * P], ident[0:NE, 0:NE])
        ins.then_inc(logit_tr, 1)
        pe.wait_ge(mask_done, 1)
        mask = rt[:, 88:104].rearrange("p (t e) -> p t e", t=T)
        pe.matmul(Y[:, 2, 0:2 * NE], before_mat, rt[:, 88:104], start=True, stop=False, skip_group_check=True)
        pe.matmul(Y[:, 2, NE:2 * NE], ones_mat, mask[:, 0, :], start=False, stop=True, skip_group_check=True).then_inc(rank_mm, 1)
        for t in range(T):
            ins = pe.matmul(Y[:, 3, 0:NE], ones_mat, mask[:, t, :], start=(t == 0), stop=(t == T - 1))
        ins.then_inc(rank_mm, 1)

        def gather():
            for k in range(KT):
                dst = (G[:, 3, :], Y[:, 2, :])[k // 4][:, (k % 4) * P:(k % 4 + 1) * P]
                for t in range(T):
                    ins = pe.matmul(dst, h[:, t, k * P:(k + 1) * P], pick[:, t, :], start=(t == 0), stop=(t == T - 1))
                if k % 4 == 3:
                    ins.then_inc(gath_mm, 1)

        def last_expert(done):
            pe.wait_ge(xlo_done, done * KT + KT)
            pe.wait_ge(y_out, done + 1)
            pe.wait_ge(sp_out, done + 1)
            pe.wait_ge(scat_add, 4 * done + 1)

        def scatter(banks, t=0):
            for u, dst in enumerate(banks, 2 * t):
                ins = pe.matmul(dst, spread[:, (u // 2) * P:(u // 2 + 1) * P], y_sb[:, (u % 2) * 512:(u % 2 + 1) * 512],
                                start=True, stop=True)
            return ins

        pe.wait_ge(pick_done, 2)
        gather()

        def experts(first, last):
            with pe.Fori(first, last) as it:
                def transposes(j):
                    pe.wait_ge(xmul, it * GROUPS + (j + 1))
                    if j:
                        pe.wait_ge(at_lo, it * GROUPS + j)
                    else:
                        pe.wait_ge(scat_add, it * 4 + 5)
                    for f in range(4):
                        ins = pe.transpose(G[:, 2, f * P:(f + 1) * P], x_act[:, f * P:(f + 1) * P], ident)
                    ins.then_inc(at_mm, 1)

                for i, (name, j) in enumerate(EXPERT):
                    if name == "moe_wd":
                        for f in range(4):
                            if f == 0:
                                pe.wait_ge(at_lo, it * GROUPS + (j + 1))
                            n = PB + 4 * i + f
                            pe.wait_ge(lo_done, it * XP + (n + 1))
                            for c in range(2):
                                ins = three(Y[:, c, :], aT_hi[:, j % 2, f, :], aT_lo[:, j % 2, f, :],
                                            hi_ring[:, n % AHEAD, c * 512:(c + 1) * 512], lo_ring[:, n % AHEAD, c * 512:(c + 1) * 512],
                                            j == 0 and f == 0, j == GROUPS - 1 and f == 3)
                            piece(n, ins)
                            if j == GROUPS - 2 and f == 0:
                                transposes(GROUPS - 1)
                        continue
                    bank, free = (0, xsilu) if name == "moe_wg" else (1, xmul)
                    if j:
                        pe.wait_ge(free, it * GROUPS + j)
                    for s in range(4):
                        n = PB + 4 * i + s
                        pe.wait_ge(lo_done, it * XP + (n + 1))
                        if name == "moe_wg" and j == 0:
                            pe.wait_ge(xlo_done, it * KT + (2 * s + 2))
                        w_hi, w_lo = piece_at(hi_ring, n, 512), piece_at(lo_ring, n, 512)
                        for r in range(2):
                            k = 2 * s + r
                            ins = three(G[:, bank, :], xg_hi[:, k, :], xg_lo[:, k, :], w_hi[:, r, :], w_lo[:, r, :],
                                        k == 0, k == KT - 1)
                        piece(n, ins)
                    if name == "moe_wg":
                        if j == 0:
                            pe.wait_ge(y_out, it + 1)
                            pe.wait_ge(sp_out, it + 1)
                            scatter((G[:, 3, :], Y[:, 2, :], Y[:, 3, :], G[:, 2, :])).then_inc(scat_mm, 1)
                        else:
                            transposes(j - 1)
                    elif j == 3:
                        pe.wait_ge(pick_done, it * 4 + 4)
                        pe.wait_ge(scat_add, it * 4 + 5)
                        for t in range(T):
                            ins = pe.transpose(Y[:, 3, t * P:(t + 1) * P], pick_gated[:, t, :], ident)
                        ins.then_inc(sp_mm, 1)
                    elif j == GROUPS - 1:
                        pe.wait_ge(pick_done, it * 4 + 6)
                        gather()

        experts(0, NE)
        n_most = pe.value_load(most[0:1, 0:1])
        with pe.If(n_most > P):
            experts(NE, ITERS)
            last_expert(ITERS)
        with pe.Else():
            pe.wait_ge(pe_piece, PB + NE * XP)
            pe.sem_inc(pe_piece, NE * XP)
            last_expert(NE)
            pe.nop()
        for t in range(T):
            scatter([Y[:, 2 * t + c, :] for c in range(2)], t).then_inc(last_mm, 1)
        ple(1, 5, PT)

    block.__exit__(None, None, None)


def host_constants():
    c = np.zeros((P, C_END), np.float32)
    c[:, C_IDENT:C_IOTA] = np.eye(P)
    c[:, C_IOTA:C_MEAN] = np.arange(P)[None, :]
    c[:, C_MEAN:C_ONES] = 1.0 / CONV_CH
    c[:, C_ONES:C_BEFORE] = 1.0
    c[:, C_BEFORE:C_COS] = np.arange(P)[:, None] < np.arange(P)[None, :]
    pos = np.arange(SEQ)
    inv = (np.float32(10000.0) ** (-np.arange(0, HALF, 2, dtype=np.float32) / np.float32(HALF))).astype(np.float32)
    row, col = (pos // GRID_W).astype(np.float32), (pos % GRID_W).astype(np.float32)
    ang = np.concatenate([row[:, None] * inv, col[:, None] * inv], axis=-1).astype(np.float32)
    c[:, C_COS:C_SIN] = np.cos(ang).reshape(T, P, HALF).transpose(1, 0, 2).reshape(P, -1)
    c[:, C_SIN:C_END] = np.sin(ang).reshape(T, P, HALF).transpose(1, 0, 2).reshape(P, -1)
    bands = np.zeros((4, SEQ, SEQ), np.float32)
    for g, w in enumerate(POOL_WINDOWS):
        lo = np.clip(pos - w // 2, 0, SEQ - 1)
        hi = np.clip(pos + w - 1 - w // 2, 0, SEQ - 1)
        for t in range(SEQ):
            bands[g, lo[t]:hi[t] + 1, t] = 1.0 / (hi[t] - lo[t] + 1)
            bands[g, t, t] -= 1.0
    bands = bands.reshape(4, T, P, SEQ).transpose(2, 1, 0, 3).reshape(P, -1)
    return c, np.ascontiguousarray(bands)


def vectors(v):
    def along(x):
        return x.reshape(-1, P).T

    parts = [along(v[n][i]) for i in range(2) for n in ("norm_mix", "norm_ffn", "ple_norm")]
    parts.append(v["conv_w"][0].reshape(CONV_W, CT, P).transpose(2, 1, 0).reshape(P, -1))
    parts += [along(v[n][0]) for n in ("conv_b", "conv_ln_g", "conv_ln_b")]
    parts.append(v["router_w"][0].reshape(KT, P, NE).transpose(1, 0, 2).reshape(P, -1))
    return np.ascontiguousarray(np.concatenate(parts, axis=1))


_INS = ["x", "p", "w_in", "w_out", "ffn_wg", "ffn_wu", "ffn_wd", "pool_w", "pool_scale", "moe_wg", "moe_wu", "moe_wd",
        "ple_gate_w", "ple_proj"]


def kernel(**inputs):
    import concourse.bacc as _bacc
    from concourse.bass_utils import run_bass_kernel_spmd as _run

    nc = _bacc.Bacc("TRN2", target_bir_lowering=False, num_devices=1)
    consts, bands = host_constants()
    arrays = {f"in_{n}": np.ascontiguousarray(inputs[n]) for n in _INS}
    arrays["in_consts"], arrays["in_bands"] = consts, bands
    v = {n: np.asarray(inputs[n]) for n in inputs}
    arrays["in_vectors"] = vectors(v)
    arrays["in_qk_gain"] = np.concatenate([v["q_norm"][0]] * HEADS + [v["k_norm"][0]] * KV_HEADS)[None, :]
    a = {n[3:]: nc.dram_tensor(n, x.shape, mybir.dt.from_np(x.dtype), kind="ExternalInput").ap() for n, x in arrays.items()}
    out = nc.dram_tensor("out_0", (1, SEQ, D), F32, kind="ExternalOutput").ap()
    kernel_program(nc, a, out)
    r = _run(nc, [arrays], core_ids=[0])
    return r.results[0]["out_0"]
```
